# Optimizing a Trainium2 kernel written in Bass

```python
import jax, jax.numpy as jnp
from jax import lax
import numpy as np

D_MODEL = 1024
BATCH = 1
SEQ = 1024
DEPTH = 1

ATT_HEADS = 8
ATT_KV_HEADS = 2
ATT_GROUP = ATT_HEADS // ATT_KV_HEADS
ATT_HEAD_DIM = 64
WINDOW = 128
ATT_BLOCK = WINDOW
ROPE_THETA = 500000.0
ROPE_DIMS = ATT_HEAD_DIM // 4

RET_HEADS = 8
RET_QK_DIM = 64
RET_V_DIM = 128
RET_CHUNK = 128
RET_THETA = 10000.0

ATT_Q = ATT_HEADS * ATT_HEAD_DIM
ATT_KV = ATT_KV_HEADS * ATT_HEAD_DIM
RET_QK = RET_HEADS * RET_QK_DIM
RET_V = RET_HEADS * RET_V_DIM
IN_SIZES = (ATT_Q, ATT_KV, ATT_KV, RET_QK, RET_QK, RET_V, RET_V, D_MODEL, D_MODEL)
IN_WIDTH = 5888

PEER_HEADS = 8
N_KEYS = 128
N_EXPERTS = N_KEYS * N_KEYS
PEER_QUERY_DIM = 256
PEER_HALF = PEER_QUERY_DIM // 2
PEER_TOPK = 16
PEER_TOKEN_BLOCK = 128

EPS = 1e-6
F32 = jnp.float32

kernel_name = 'hybrid_swa_sink_retention_peer_block'

def rms_norm(x, gain):
    xf = x.astype(F32)
    y = xf * lax.rsqrt(jnp.mean(xf * xf, axis=-1, keepdims=True) + EPS)
    return (y * gain.astype(F32)).astype(x.dtype)

def split_columns(t, sizes):
    outs, start = [], 0
    for s in sizes:
        outs.append(t[..., start:start + s])
        start += s
    return outs

def apply_rotary(x, positions, rot_dims, theta):
    half = rot_dims // 2
    inv_freq = theta ** (-jnp.arange(half, dtype=F32) / half)
    ang = positions.astype(F32)[:, None] * inv_freq[None, :]
    cos = jnp.cos(ang)[:, None, :]
    sin = jnp.sin(ang)[:, None, :]
    xf = x.astype(F32)
    x1 = xf[..., :half]
    x2 = xf[..., half:rot_dims]
    out = jnp.concatenate([x1 * cos - x2 * sin, x2 * cos + x1 * sin, xf[..., rot_dims:]], axis=-1)
    return out.astype(x.dtype)

def sliding_window_attention(q, k, v, sinks):
    B, S = q.shape[0], q.shape[1]
    nb = S // ATT_BLOCK
    qb = q.reshape(B, nb, ATT_BLOCK, ATT_KV_HEADS, ATT_GROUP, ATT_HEAD_DIM)

    def with_previous_block(t):
        tb = t.reshape(B, nb, ATT_BLOCK, ATT_KV_HEADS, ATT_HEAD_DIM)
        prev = jnp.pad(tb[:, :-1], ((0, 0), (1, 0), (0, 0), (0, 0), (0, 0)))
        return jnp.concatenate([prev, tb], axis=2)

    kb = with_previous_block(k)
    vb = with_previous_block(v)
    s = jnp.einsum('bnqhgd,bnkhd->bnhgqk', qb, kb, preferred_element_type=F32)
    s = s * (ATT_HEAD_DIM ** -0.5)
    qi = jnp.arange(ATT_BLOCK)[:, None] + ATT_BLOCK
    kj = jnp.arange(2 * ATT_BLOCK)[None, :]
    diff = qi - kj
    band = (diff >= 0) & (diff < WINDOW)
    key_pos = jnp.arange(nb)[:, None] * ATT_BLOCK + kj - ATT_BLOCK
    mask = band[None] & (key_pos >= 0)[:, None, :]
    s = jnp.where(mask[None, :, None, None], s, -jnp.inf)
    sink = sinks.astype(F32).reshape(ATT_KV_HEADS, ATT_GROUP)[None, None, :, :, None, None]
    m = jnp.maximum(jnp.max(s, axis=-1, keepdims=True), sink)
    p = jnp.exp(s - m)
    p = p / (jnp.sum(p, axis=-1, keepdims=True) + jnp.exp(sink - m))
    o = jnp.einsum('bnhgqk,bnkhd->bnqhgd', p.astype(v.dtype), vb)
    return o.reshape(B, S, ATT_Q)

def chunkwise_retention(q, k, v):
    B, S = q.shape[0], q.shape[1]
    C = RET_CHUNK
    nc = S // C
    qc = q.astype(F32).reshape(B, nc, C, RET_HEADS, RET_QK_DIM)
    kc = k.astype(F32).reshape(B, nc, C, RET_HEADS, RET_QK_DIM)
    vc = v.astype(F32).reshape(B, nc, C, RET_HEADS, RET_V_DIM)
    log_gamma = jnp.log1p(-jnp.exp2(-5.0 - jnp.arange(RET_HEADS, dtype=F32)))
    idx = jnp.arange(C, dtype=F32)
    diff = idx[:, None] - idx[None, :]
    decay_inner = jnp.where(diff[None] >= 0,
                            jnp.exp(log_gamma[:, None, None] * jnp.maximum(diff, 0.0)[None]), 0.0)
    scores = jnp.einsum('bnihd,bnjhd->bnhij', qc, kc) * decay_inner[None, None]
    o_inner = jnp.einsum('bnhij,bnjhe->bnihe', scores, vc)
    w_key = jnp.exp(log_gamma[:, None] * (C - 1.0 - idx)[None, :])
    kv = jnp.einsum('bnjhd,hj,bnjhe->bnhde', kc, w_key, vc)
    chunk_decay = jnp.exp(log_gamma * C)[None, :, None, None]

    def step(state, kv_n):
        return state * chunk_decay + kv_n, state

    init = jnp.zeros((B, RET_HEADS, RET_QK_DIM, RET_V_DIM), F32)
    _, states = lax.scan(step, init, jnp.moveaxis(kv, 1, 0))
    states = jnp.moveaxis(states, 0, 1)
    w_query = jnp.exp(log_gamma[:, None] * (idx + 1.0)[None, :])
    o_cross = jnp.einsum('bnihd,hi,bnhde->bnihe', qc, w_query, states)
    return (o_inner + o_cross).reshape(B, S, RET_HEADS, RET_V_DIM)

def hybrid_mixer(hn, positions, w_in, att_sinks, w_att_branch, w_ret_branch, w_out):
    B, S = hn.shape[0], hn.shape[1]
    proj = hn @ w_in
    q_a, k_a, v_a, q_r, k_r, v_r, g_r, gate_a, gate_r = split_columns(proj, IN_SIZES)
    q_a = apply_rotary(q_a.reshape(B, S, ATT_HEADS, ATT_HEAD_DIM), positions, ROPE_DIMS, ROPE_THETA)
    k_a = apply_rotary(k_a.reshape(B, S, ATT_KV_HEADS, ATT_HEAD_DIM), positions, ROPE_DIMS, ROPE_THETA)
    v_a = v_a.reshape(B, S, ATT_KV_HEADS, ATT_HEAD_DIM)
    att = sliding_window_attention(q_a, k_a, v_a, att_sinks)
    q_r = apply_rotary(q_r.reshape(B, S, RET_HEADS, RET_QK_DIM), positions, RET_QK_DIM, RET_THETA)
    k_r = apply_rotary(k_r.reshape(B, S, RET_HEADS, RET_QK_DIM), positions, RET_QK_DIM, RET_THETA) * (RET_QK_DIM ** -0.5)
    ret = chunkwise_retention(q_r, k_r, v_r.reshape(B, S, RET_HEADS, RET_V_DIM))
    ret = ret * lax.rsqrt(jnp.mean(ret * ret, axis=-1, keepdims=True) + EPS)
    ret = jax.nn.silu(g_r) * ret.reshape(B, S, RET_V).astype(hn.dtype)
    merged = jax.nn.sigmoid(gate_a) * (att @ w_att_branch) + jax.nn.sigmoid(gate_r) * (ret @ w_ret_branch)
    return merged @ w_out

def peer_ffn(hn, w_query, sub_keys_1, sub_keys_2, expert_u, expert_v):
    B, S, D = hn.shape
    T = B * S
    hf = hn.reshape(T, D)
    q = (hf @ w_query).reshape(T, PEER_HEADS, 2, PEER_HALF)
    s1 = jnp.einsum('thc,kc->thk', q[:, :, 0], sub_keys_1, preferred_element_type=F32)
    s2 = jnp.einsum('thc,kc->thk', q[:, :, 1], sub_keys_2, preferred_element_type=F32)
    v1, i1 = lax.top_k(s1, PEER_TOPK)
    v2, i2 = lax.top_k(s2, PEER_TOPK)
    cand_score = (v1[..., :, None] + v2[..., None, :]).reshape(T, PEER_HEADS, PEER_TOPK * PEER_TOPK)
    cand_index = (i1[..., :, None] * N_KEYS + i2[..., None, :]).reshape(T, PEER_HEADS, PEER_TOPK * PEER_TOPK)
    top_score, pick = lax.top_k(cand_score, PEER_TOPK)
    expert_index = jnp.take_along_axis(cand_index, pick, axis=-1)
    gate = jax.nn.softmax(top_score, axis=-1)
    nblk = T // PEER_TOKEN_BLOCK

    def block_fn(args):
        xb, ib, gb = args
        u = expert_u[ib]
        a = jnp.einsum('td,thkd->thk', xb, u, preferred_element_type=F32)
        coef = gb * jax.nn.gelu(a, approximate=False)
        vv = expert_v[ib]
        return jnp.einsum('thk,thkd->td', coef.astype(vv.dtype), vv)

    out = lax.map(block_fn, (hf.reshape(nblk, PEER_TOKEN_BLOCK, D),
                             expert_index.reshape(nblk, PEER_TOKEN_BLOCK, PEER_HEADS, PEER_TOPK),
                             gate.reshape(nblk, PEER_TOKEN_BLOCK, PEER_HEADS, PEER_TOPK)))
    return out.reshape(B, S, D).astype(hn.dtype)

def setup_inputs(seed: int = 0) -> dict:
    key = jax.random.key(seed)
    ks = jax.random.split(key, 16)

    def normal(k, shape, scale):
        return jax.random.normal(k, shape, F32) * scale

    L = DEPTH
    return {
        'x': normal(ks[0], (BATCH, SEQ, D_MODEL), 1.0),
        'norm_mix': 1.0 + normal(ks[1], (L, D_MODEL), 0.01),
        'w_in': normal(ks[2], (L, D_MODEL, IN_WIDTH), D_MODEL ** -0.5),
        'att_sinks': normal(ks[3], (L, ATT_HEADS), 0.5),
        'w_att_branch': normal(ks[4], (L, ATT_Q, D_MODEL), ATT_Q ** -0.5),
        'w_ret_branch': normal(ks[5], (L, RET_V, D_MODEL), RET_V ** -0.5),
        'w_out': normal(ks[6], (L, D_MODEL, D_MODEL), D_MODEL ** -0.5),
        'norm_ffn': 1.0 + normal(ks[7], (L, D_MODEL), 0.01),
        'peer_w_query': normal(ks[8], (L, D_MODEL, PEER_HEADS * PEER_QUERY_DIM), D_MODEL ** -0.5),
        'peer_sub_keys_1': normal(ks[9], (L, N_KEYS, PEER_HALF), PEER_HALF ** -0.5),
        'peer_sub_keys_2': normal(ks[10], (L, N_KEYS, PEER_HALF), PEER_HALF ** -0.5),
        'peer_u': normal(ks[11], (L, N_EXPERTS, D_MODEL), D_MODEL ** -0.5),
        'peer_v': normal(ks[12], (L, N_EXPERTS, D_MODEL), 0.5),
        'norm_final': 1.0 + normal(ks[13], (D_MODEL,), 0.01),
    }

def reference(x, norm_mix, w_in, att_sinks, w_att_branch, w_ret_branch, w_out, norm_ffn,
              peer_w_query, peer_sub_keys_1, peer_sub_keys_2, peer_u, peer_v, norm_final):
    positions = jnp.arange(x.shape[1], dtype=jnp.int32)
    h = x
    for layer in range(DEPTH):
        h = h + hybrid_mixer(rms_norm(h, norm_mix[layer]), positions, w_in[layer], att_sinks[layer],
                             w_att_branch[layer], w_ret_branch[layer], w_out[layer])
        h = h + peer_ffn(rms_norm(h, norm_ffn[layer]), peer_w_query[layer], peer_sub_keys_1[layer],
                         peer_sub_keys_2[layer], peer_u[layer], peer_v[layer])
    return rms_norm(h, norm_final)


_drawn_inputs = setup_inputs


def setup_inputs(seed=0):
    import zlib

    import numpy as np

    out = dict(_drawn_inputs(seed))
    spreads = {}
    factors = {'att_sinks': 8.0, 'norm_final': 5.478}
    for name, (base, spread) in spreads.items():
        noise = np.random.default_rng([zlib.crc32(name.encode()), seed]).standard_normal(out[name].shape)
        drawn = base * np.exp(spread * noise) if base else spread * noise
        out[name] = __import__('jax').numpy.asarray(drawn.astype(out[name].dtype))
    for name, factor in factors.items():
        out[name] = (out[name] * factor).astype(out[name].dtype)
    return out
```

```python
from contextlib import ExitStack

import numpy as np

import concourse.bass as bass
from concourse import mybir

ALU = mybir.AluOpType
ACT = mybir.ActivationFunctionType
AX = mybir.AxisListType
F32 = mybir.dt.float32
U32 = mybir.dt.uint32

P = 128
SEQ, D = 1024, 1024
KD = D // P
GT = 2
GROUPS = SEQ // (P * GT)
HEADS, HD, KVH = 8, 64, 2
RH, RQ, RV = 8, 64, 128
PH, NKEY, TOPK = 8, 128, 16
SLOTS = PH * TOPK
EPS = 1e-6
CW = 512
NEG = -1.0e30
LOWEST = -3.0e38

CHUNKS = [("A0", "in", 0, 512), ("A1", "in", 512, 256), ("QR", "in", 768, 512), ("KR", "in", 1280, 512),
          ("V0", "in", 1792, 512), ("V1", "in", 2304, 512), ("G0", "in", 2816, 512), ("G1", "in", 3328, 512),
          ("WA", "att", 0, 1024), ("GA0", "in", 3840, 512), ("GA1", "in", 4352, 512),
          ("GR0", "in", 4864, 512), ("WR0", "ret", 0, 512), ("GR1", "in", 5376, 512), ("WR1", "ret", 512, 512),
          ("WO0", "out", 0, 512), ("WO1", "out", 512, 512),
          ("WQ0", "query", 0, 512), ("WQ1", "query", 512, 512), ("WQ2", "query", 1024, 512), ("WQ3", "query", 1536, 512)]
CHUNK = {c[0]: n for n, c in enumerate(CHUNKS)}
WBUFS = 2

STAGES = (
    [("norm", 0, 0), ("norm", 1, 0), ("A0", 0, 0), ("A0", 1, 0), ("A1", 0, 0), ("A1", 1, 0),
     ("QR", 0, 0), ("heads", 0, 0), ("QR", 1, 0), ("score", 0, 0), ("KR", 0, 0), ("turn", 0, 0), ("KR", 1, 0),
     ("mix", 0, 0), ("V", 0, 0), ("attT", 0, 0), ("V", 1, 0), ("heads", 1, 0), ("V", 0, 1), ("score", 1, 0),
     ("V", 1, 1), ("turn", 1, 0), ("G", 0, 0), ("mix", 1, 0), ("G", 1, 0), ("attT", 1, 0), ("G", 0, 1),
     ("rheads", 0, 0), ("G", 1, 1), ("rscore", 0, 0), ("WA", 0, 0), ("rmix", 0, 0), ("WA", 0, 1), ("retT", 0, 0),
     ("rheads", 1, 0), ("WA", 1, 0), ("rscore", 1, 0), ("WA", 1, 1), ("rmix", 1, 0), ("GA", 0, 0), ("retT", 1, 0),
     ("GA", 1, 0), ("GA", 0, 1), ("GA", 1, 1)]
    + [(k, t, n) for n in range(2) for k in ("GR", "WR") for t in range(GT)]
    + [("mT", 0, 0), ("mT", 1, 0)]
    + [("WO", t, n) for n in range(2) for t in range(GT)]
    + [("norm2", 0, 0), ("norm2", 1, 0)]
    + [(k, None, h) for h in range(PH) for k in ("query", "keys", "top")]
    + [(k, t, n) for t in range(GT) for k, m in (("cand", 2), ("gate", 1), ("decode", 2)) for n in range(m)]
)

BANKS_OF = dict(norm=2, A0=1, A1=1, QR=1, KR=1, V=1, G=1, heads=2, score=4, turn=4, mix=1, attT=1, rheads=2,
                rscore=2, rmix=4, retT=2, WA=1, GA=1, GR=1, WR=1, mT=2, WO=1, norm2=2, query=1, keys=1)
FILLS = [(s, i) for s in STAGES for i in range(BANKS_OF.get(s[0], 0))]
FILL = {f: n for n, f in enumerate(FILLS)}
NFILL = len(FILLS)
WORKBANKS = 6

ACT_OF = dict(norm=("rms", "xn"), V=("v",), G=("silu",), heads=("qT", "kT"), score=("probs",), turn=("pT",),
              attT=("attT",), rheads=("qT", "kT"), rmix=("rms",), retT=("retT",), WA=("m",), GA=("sig",), GR=("sig",),
              mT=("mT",), norm2=("rms", "hT"), query=("qT",), keys=("scores",), gate=("exp",))
DVE_OF = dict(norm=("rstd", "hT"), A0=("q",), A1=("kv",), QR=("q",), KR=("k",), score=("masked",), mix=("att",),
              rheads=("weighted",), rscore=("decayed",), rmix=("ret", "state"), retT=("gated",), GA=("m",), WR=("m",),
              WO=("h",), norm2=("rstd", "hn"), top=("top",), cand=("picks",), gate=("diff", "gate"), decode=("index",))


def places(made_in):
    order = [(s, r) for s in STAGES for r in made_in.get(s[0], ())]
    return {k: n for n, k in enumerate(order)}, len(order)


ACT_AT, NACT = places(ACT_OF)
DVE_AT, NDVE = places(DVE_OF)

RING = 8
QN = 4
NH2 = GT * PH
QUARTERS = [(h, q) for h in range(NH2 + 1) for q in range(TOPK // QN)]


def v_on_pe(slot):
    return slot % 2 == 0


def gathers():
    out = []
    for h, q in QUARTERS:
        for k in range(QN * q, QN * q + QN):
            if h < NH2:
                out.append(("u", h, k))
            if h:
                out.append(("v", h - 1, k))
    return out


GATHERS = gathers()
GATHER = {g: n for n, g in enumerate(GATHERS)}
NGATHER = len(GATHERS)
assert NGATHER % RING == 0


def used_counts():
    dve = pe = 0
    out = []
    for kind, _, k in GATHERS:
        if kind == "v" and v_on_pe(k):
            pe += 1
        else:
            dve += 1
        out.append((dve, pe))
    return out, dve, pe


USED, NUSED_DVE, NUSED_PE = used_counts()

SHARE = [STAGES[len(STAGES) * n // len(QUARTERS):len(STAGES) * (n + 1) // len(QUARTERS)] for n in range(len(QUARTERS))]

C_MASK, C_DECAY, C_WQ, C_WK, C_SD, C_ID, C_IOTA = 0, 256, 1280, 1792, 1800, 1804, 1932
C_ALL = 1948
ROT_R, ROT_A = 64, 16
T_ALL = 2 * (ROT_R + ROT_A)


def shape_constants():
    f = np.float32
    i = np.arange(P)
    c = np.zeros((P, C_ALL), f)
    diff = (i[:, None] + P) - np.arange(2 * P)[None, :]
    band = (diff >= 0) & (diff < P)
    c[:, C_MASK:C_MASK + 256] = np.where(band, 0.0, NEG)
    mask0 = np.where(band & (np.arange(2 * P)[None, :] >= P), 0.0, NEG).astype(f)
    lg = np.log1p(-np.exp2(-5.0 - np.arange(RH)))
    scale = RQ ** -0.5
    gap = i[None, :] - i[:, None]
    for half in range(2):
        for pair in range(4):
            h = 2 * pair + half
            block = np.where(gap >= 0, np.exp(lg[h] * np.maximum(gap, 0)), 0.0) * scale
            at = C_DECAY + (half * 4 + pair) * P
            c[:, at:at + P] = block
            c[half * 64:half * 64 + 64, C_WQ + pair * P:C_WQ + (pair + 1) * P] = np.exp(lg[h] * (i + 1.0))[None, :]
            c[half * 64:half * 64 + 64, C_SD + pair] = np.exp(lg[h] * P)
    for h in range(RH):
        c[:, C_WK + h] = np.exp(lg[h] * (P - 1.0 - i)) * scale
    c[:, C_ID:C_ID + P] = np.eye(P)
    c[:, C_IOTA:C_IOTA + 16] = np.arange(16)
    pos = np.arange(SEQ, dtype=f)
    rot = np.zeros((SEQ, T_ALL), f)
    at = 0
    for width, theta in ((ROT_R, 10000.0), (ROT_A, 500000.0)):
        half = width // 2
        freq = (f(theta) ** (-np.arange(half, dtype=f) / f(half))).astype(f)
        ang = (pos[:, None] * freq[None, :]).astype(np.float64)
        rot[:, at:at + width] = np.concatenate([np.cos(ang), np.cos(ang)], 1)
        rot[:, at + width:at + 2 * width] = np.concatenate([-np.sin(ang), np.sin(ang)], 1)
        at += 2 * width
    return c, rot, mask0


def is_first(g):
    return isinstance(g, int) and g == 0


def build_block(nc, x, norm_mix, w_in, att_sinks, w_att, w_ret, w_out, norm_ffn, w_query, keys1, keys2,
                peer_u, peer_v, norm_final, const_table, rot_table, mask_table, out):
    with ExitStack() as ctx:
        def sb(name, shape, dt=F32):
            return ctx.enter_context(nc.sbuf_tensor(name, shape, dt))

        def sem(name):
            return ctx.enter_context(nc.semaphore(name))

        work = [ctx.enter_context(nc.psum_tensor(f"work{i}", [P, CW], F32)) for i in range(WORKBANKS)]
        vsum = [ctx.enter_context(nc.psum_tensor(f"vsum{i}", [P, CW], F32)) for i in range(2)]

        const = sb("const", [P, C_ALL])
        gain_mix = sb("gain_mix", [P, KD])
        gain_ffn = sb("gain_ffn", [P, D])
        gain_fin = sb("gain_fin", [P, D])
        sinks = sb("sinks", [P, HEADS])
        keyT = sb("keyT", [P, 2, P])
        eps_t = sb("eps_t", [P, 1])
        rows = sb("rows", [P, RING, D])
        wbuf = sb("wbuf", [P, WBUFS, KD, CW])
        rot = sb("rot", [P, GT, T_ALL])
        xh = sb("xh", [P, GT, D])
        scratch = sb("scratch", [P, D])
        actT = sb("actT", [P, KD, GT * P])
        qa = sb("qa", [P, GT, 512])
        ka = sb("ka", [P, GT, P])
        va = sb("va", [P, GT + 1, P])
        kTa = sb("kTa", [P, (GT + 1) * P])
        hqT = sb("hqT", [P, 4, P])
        probs = sb("probs", [P, HEADS, 2 * P])
        probsT = sb("probsT", [P, HEADS, 2, P])
        att = sb("att", [P, 512])
        attT = sb("attT", [P, 4, GT * P])
        qk_m = sb("qk_m", [P, GT, D])
        vg = sb("vg", [P, 2, GT, D])
        state = sb("state", [P, 4, RV])
        retT_hn = sb("retT_hn", [P, 2 * D])
        pqT = sb("pqT", [P, 2, GT * P])
        h_cur = sb("h_cur", [P, GT, D])
        hn_cur = sb("hn_cur", [P, GT, D])
        vacc = sb("vacc", [P, D])
        diag = sb("diag", [P, 4, P])
        small = sb("small", [P, 128])
        top_v = sb("top_v", [P, GT, PH, 2, TOPK])
        top_i = sb("top_i", [P, GT, PH, 2, TOPK], U32)
        top_if = sb("top_if", [P, PH // 2, 2, TOPK])
        pick_v = sb("pick_v", [P, GT, SLOTS])
        pick_i = sb("pick_i", [P, GT, SLOTS], U32)
        part = sb("part", [P, 2, SLOTS // 2], U32)
        sel = sb("sel", [P, 2, SLOTS // 2])
        expg = sb("expg", [P, SLOTS])
        index_next = sb("index_next", [P, GT, SLOTS], U32)
        index_cur = sb("index_cur", [P, GT, SLOTS], U32)
        gate_next = sb("gate_next", [P, GT, SLOTS])
        gate_cur = sb("gate_cur", [P, GT, SLOTS])
        dots = sb("dots", [P, GT, SLOTS])
        coef = sb("coef", [P, GT, SLOTS])

        ident = const[:, C_ID:C_ID + P]
        decayed = probs[:, 0:4].rearrange("p a b -> p (a b)").rearrange("p (h i) -> p h i", h=RH)
        ret_parts = probsT[:, :].rearrange("p h b q -> p (h b q)").rearrange("p (n w) -> p n w", n=4)
        rkT = ret_parts[:, 0].rearrange("p (a b) -> p a b", a=4)
        rqwT = ret_parts[:, 1].rearrange("p (a b) -> p a b", a=4)
        kw = ret_parts[:, 2]
        mask_first = hn_cur[:, 0, 0:2 * P]
        key_raw = vacc[:, 0:2 * P].rearrange("p (s k) -> p s k", s=2)
        v_r, g_r = vg[:, 0], vg[:, 1]
        retT = retT_hn[:, :].rearrange("p (k t) -> p k t", k=KD)
        hn = retT_hn[:, :].rearrange("p (t d) -> p t d", t=GT)
        scores = vg[:, :, :, :].rearrange("p a b d -> p (a b d)").rearrange("p (t s k) -> p t s k", t=GT, s=2 * PH)
        cands = vg[:, :, :, :].rearrange("p a b d -> p (a b d)").rearrange("p (t h c) -> p t h c", t=GT, h=PH)

        def col(n, w=1):
            return small[:, n:n + w]
        SS, RMS, RSTD = 0, 2, 4
        MX, NM, RSUM, ESNK, DEN = 8, 16, 24, 32, 40
        SSR, RMSR, RINV, GSUM, GINV = 48, 56, 64, 72, 80
        FSS, FRMS, FRSTD = 96, 98, 100

        consts_landed = sem("consts_landed")
        set_up = sem("set_up")
        keys_turned = sem("keys_turned")
        keys_kept = sem("keys_kept")
        x_landed = [sem(f"x_landed{t}") for t in range(GT)]
        w_landed = [sem(f"w_landed{b}") for b in range(WBUFS)]
        filled = sem("filled")
        drained = [sem(f"drained{b}") for b in range(WORKBANKS)]
        act_made = sem("act_made")
        dve_made = sem("dve_made")
        act_step = sem("act_step")
        dve_step = sem("dve_step")
        row_landed = [sem(f"row_landed{b}") for b in range(RING)]
        used_dve = sem("used_dve")
        used_pe = sem("used_pe")
        gelu_made = sem("gelu_made")
        coef_made = sem("coef_made")
        diag_made = sem("diag_made")
        acc_made = sem("acc_made")
        fin_rms = sem("fin_rms")
        out_made = sem("out_made")
        out_stored = [sem(f"out_stored{t}") for t in range(GT)]
        handed_act = sem("handed_act")
        handed_dve = sem("handed_dve")
        passed = sem("passed")

        def at_least(eng, s, value):
            if isinstance(value, int) and value <= 0:
                return
            eng.wait_ge(s, value)

        def hold(eng, s, value):
            at_least(eng, s, value)
            eng.sem_inc(passed, 1)

        def wait_act(eng, g, stage, result):
            at_least(eng, act_made, g * NACT + ACT_AT[(stage, result)] + 1)

        def wait_dve(eng, g, stage, result):
            at_least(eng, dve_made, g * NDVE + DVE_AT[(stage, result)] + 1)

        def wait_filled(eng, g, stage, i=0):
            n = FILL[(stage, i)]
            at_least(eng, filled, g * NFILL + n + 1)
            return work[n % WORKBANKS], drained[n % WORKBANKS]

        def open_bank(pe, g, stage, i=0):
            n = FILL[(stage, i)]
            b = n % WORKBANKS
            per_group = len(range(b, NFILL, WORKBANKS))
            at_least(pe, drained[b], g * per_group + n // WORKBANKS)
            return work[b]

        def wait_weights(pe, g, name):
            n = CHUNK[name]
            b = n % WBUFS
            at_least(pe, w_landed[b], g * (16 * len(range(b, len(CHUNKS), WBUFS))) + 16 * (n // WBUFS + 1))
            return wbuf[:, b]

        W_DRAM = {"in": w_in, "att": w_att, "ret": w_ret, "out": w_out, "query": w_query}
        PER_TILE = 4
        NACC = GT * PER_TILE
        ACC_READ = [t * PER_TILE + 2 for t in range(GT)]

        LAST_USE = {}
        for s in STAGES:
            kind, t, n = s
            name = {"A0": "A0", "A1": "A1", "QR": "QR", "KR": "KR", "WA": "WA"}.get(kind)
            if kind in ("V", "G", "GA", "GR", "WR", "WO"):
                name = f"{kind}{n}"
            if kind == "query":
                name = f"WQ{n // 2}"
            if name:
                LAST_USE[name] = s

        block = ctx.enter_context(nc.Block())

        @block.sync
        def _(sp):
            sp.dma_start(const[:], const_table).then_inc(consts_landed, 16)
            sp.dma_start(mask_first, mask_table).then_inc(consts_landed, 16)
            sp.dma_start(gain_mix[:], norm_mix.rearrange("a (k p) -> p (a k)", p=P), allow_slow_non_contiguous=True).then_inc(consts_landed, 16)
            for t in range(2):
                sp.dma_start(key_raw[:, t], (keys1, keys2)[t]).then_inc(consts_landed, 16)
            sp.dma_start(sinks[:], att_sinks[0].partition_broadcast(P)).then_inc(consts_landed, 16)
            sp.dma_start(gain_ffn[:], norm_ffn[0].partition_broadcast(P)).then_inc(consts_landed, 16)
            sp.dma_start(gain_fin[:], norm_final.partition_broadcast(P)).then_inc(consts_landed, 16)

            def loads(g):
                for t in range(GT):
                    at_least(sp, handed_act, g * GT)
                    r0 = g * (GT * P) + t * P
                    sp.dma_start(xh[:, t], x[bass.ds(r0, P), :]).then_inc(x_landed[t], 16)
                    sp.dma_start(rot[:, t], rot_table[bass.ds(r0, P), :]).then_inc(x_landed[t], 16)
                for n, (name, which, c0, cw) in enumerate(CHUNKS):
                    b = n % WBUFS
                    m = n - WBUFS
                    if m < 0:
                        m = max(range(b, len(CHUNKS), WBUFS))
                        before = g - 1
                    else:
                        before = g
                    last = LAST_USE[CHUNKS[m][0]]
                    at_least(sp, filled, before * NFILL + FILL[(last, BANKS_OF[last[0]] - 1)] + 1)
                    src = W_DRAM[which].rearrange("(k p) n -> p k n", p=P)[:, :, c0:c0 + cw]
                    dst = wbuf[:, b].rearrange("p k n -> p (k n)")[:, 0:src.shape[1] * cw].rearrange(
                        "p (k n) -> p k n", n=cw)
                    sp.dma_start(dst, src).then_inc(w_landed[b], 16)

            loads(0)
            with sp.Fori(0, GROUPS - 1) as r:
                loads(r + 1)

        @block.gpsimd
        def _(pool):
            pool.memset(eps_t[:], EPS).then_inc(set_up, 1)
            pool.memset(va[:, 0], 0.0).then_inc(set_up, 1)
            pool.memset(kTa[:, 0:P], 0.0).then_inc(set_up, 1)
            pool.memset(state[:], 0.0).then_inc(set_up, 1)

            def retrieve(g):
                hold(pool, handed_dve, g + 1)
                for n, (kind, h, k) in enumerate(GATHERS):
                    m = n - RING
                    before, m = (g + 1, m) if m >= 0 else (g, m + NGATHER)
                    dve, pe = USED[m]
                    kind_m, _, k_m = GATHERS[m]
                    if kind_m == "v" and v_on_pe(k_m):
                        hold(pool, used_pe, before * NUSED_PE + pe)
                    else:
                        hold(pool, used_dve, before * NUSED_DVE + dve)
                    slot = (h % PH) * TOPK + k
                    pool.indirect_dma_start(
                        rows[:, n % RING], None, (peer_u if kind == "u" else peer_v),
                        bass.IndirectOffsetOnAxis(ap=index_cur[:, h // PH, slot:slot + 1], axis=0),
                    ).then_inc(row_landed[n % RING], 16)

            with pool.Fori(0, GROUPS) as r:
                retrieve(r)

        @block.tensor
        def _(pe):
            def turn(dst, src):
                return pe.transpose(dst, src, ident)

            def project(g, stage, weights, lhs, steps, c0=0, cw=CW):
                bank = open_bank(pe, g, stage)
                for k in range(steps):
                    last = pe.matmul(bank[:, 0:cw], lhs[:, k], weights[:, k, c0:c0 + cw],
                                     start=(k == 0), stop=(k == steps - 1))
                last.then_inc(filled, 1)

            def front(g, stage):
                kind, t, n = stage
                toks = slice(t * P, t * P + P) if t is not None else None
                if kind in ("norm", "norm2"):
                    src = scratch if kind == "norm" else hn[:, t]
                    if kind == "norm":
                        wait_act(pe, g, stage, "xn")
                    else:
                        wait_dve(pe, g, stage, "hn")
                    for i in range(2):
                        bank = open_bank(pe, g, stage, i)
                        for j in range(4):
                            k = 4 * i + j
                            last = turn(bank[:, j * P:(j + 1) * P], src[:, k * P:(k + 1) * P])
                        last.then_inc(filled, 1)
                elif kind in ("A0", "A1", "QR", "KR", "V", "G", "GA", "GR"):
                    name = kind + str(n) if kind in ("V", "G", "GA", "GR") else kind
                    wait_dve(pe, g, ("norm", t, 0), "hT")
                    w = wait_weights(pe, g, name)
                    cw = CHUNKS[CHUNK[name]][3]
                    if cw != CW:
                        w = w.rearrange("p k n -> p (k n)")[:, 0:KD * cw].rearrange("p (k n) -> p k n", n=cw)
                    project(g, stage, w, actT[:, :, toks], KD, 0, cw)
                elif kind == "heads":
                    wait_dve(pe, g, ("A0", t, 0), "q")
                    bank = open_bank(pe, g, stage, 0)
                    for p in range(4):
                        last = turn(bank[:, p * P:(p + 1) * P], qa[:, t, p * P:(p + 1) * P])
                    last.then_inc(filled, 1)
                    wait_dve(pe, g, ("A1", t, 0), "kv")
                    bank = open_bank(pe, g, stage, 1)
                    turn(bank[:, 0:P], ka[:, t]).then_inc(filled, 1)
                elif kind == "score":
                    wait_act(pe, g, ("heads", t, 0), "kT")
                    if is_first(g) and t == 0:
                        pe.wait_ge(set_up, 4)
                    for i in range(4):
                        c, p0 = i // 2, 2 * (i % 2)
                        bank = open_bank(pe, g, stage, i)
                        for j in range(2):
                            last = pe.matmul(bank[:, j * 256:(j + 1) * 256], hqT[c * 64:c * 64 + 64, p0 + j],
                                             kTa[c * 64:c * 64 + 64, t * P:(t + 2) * P], start=True, stop=True)
                        last.then_inc(filled, 1)
                elif kind == "turn":
                    wait_act(pe, g, ("score", t, 0), "probs")
                    for i in range(4):
                        bank = open_bank(pe, g, stage, i)
                        for j in range(2):
                            for b in range(2):
                                last = turn(bank[:, (2 * j + b) * P:(2 * j + b + 1) * P],
                                            probs[:, 2 * i + j, b * P:(b + 1) * P])
                        last.then_inc(filled, 1)
                elif kind == "mix":
                    wait_act(pe, g, ("turn", t, 0), "pT")
                    bank = open_bank(pe, g, stage)
                    for h in range(HEADS):
                        c = h // 4
                        for b in range(2):
                            last = pe.matmul(bank[:, h * 64:(h + 1) * 64], probsT[:, h, b],
                                             va[:, t + b, c * 64:(c + 1) * 64], start=(b == 0), stop=(b == 1))
                    last.then_inc(filled, 1)
                elif kind == "attT":
                    wait_dve(pe, g, ("mix", t, 0), "att")
                    bank = open_bank(pe, g, stage)
                    for k in range(4):
                        last = turn(bank[:, k * P:(k + 1) * P], att[:, k * P:(k + 1) * P])
                    last.then_inc(filled, 1)
                elif kind == "rheads":
                    for i, made in ((0, ("QR", "q")), (1, ("KR", "k"))):
                        wait_dve(pe, g, (made[0], t, 0), made[1])
                        bank = open_bank(pe, g, stage, i)
                        for p in range(4):
                            last = turn(bank[:, p * P:(p + 1) * P], qk_m[:, t, i * 512 + p * P:i * 512 + (p + 1) * P])
                        last.then_inc(filled, 1)
                elif kind == "rscore":
                    wait_act(pe, g, ("rheads", t, 0), "kT")
                    for c in range(2):
                        bank = open_bank(pe, g, stage, c)
                        for p in range(4):
                            last = pe.matmul(bank[:, p * P:(p + 1) * P], rkT[c * 64:c * 64 + 64, p],
                                             hqT[c * 64:c * 64 + 64, p], start=True, stop=True)
                        last.then_inc(filled, 1)
                elif kind == "rmix":
                    wait_dve(pe, g, ("rscore", t, 0), "decayed")
                    wait_act(pe, g, ("V", t, 1), "v")
                    if t:
                        wait_dve(pe, g, ("rmix", t - 1, 0), "state")
                    else:
                        at_least(pe, dve_made, (g - 1) * NDVE + DVE_AT[(("rmix", GT - 1, 0), "state")] + 1)
                    for c in range(2):
                        bank = open_bank(pe, g, stage, c)
                        for p in range(4):
                            h = 2 * p + c
                            pe.matmul(bank[:, p * P:(p + 1) * P], decayed[:, c * 4 + p],
                                      v_r[:, t, h * RV:(h + 1) * RV], start=True, stop=False)
                            last = pe.matmul(bank[:, p * P:(p + 1) * P], rqwT[c * 64:c * 64 + 64, p],
                                             state[c * 64:c * 64 + 64, p], start=False, stop=True)
                        last.then_inc(filled, 1)
                    for i in range(2):
                        bank = open_bank(pe, g, stage, 2 + i)
                        for j in range(2):
                            p = 2 * i + j
                            last = pe.matmul(bank[:, j * 256:(j + 1) * 256], kw[:, p * P:(p + 1) * P],
                                             v_r[:, t, p * 256:(p + 1) * 256], start=True, stop=True)
                        last.then_inc(filled, 1)
                elif kind in ("retT", "mT"):
                    if kind == "retT":
                        wait_dve(pe, g, stage, "gated")
                        src = g_r[:, t]
                    else:
                        wait_dve(pe, g, ("WR", t, 1), "m")
                        src = qk_m[:, t]
                    for i in range(2):
                        bank = open_bank(pe, g, stage, i)
                        for j in range(4):
                            k = 4 * i + j
                            last = turn(bank[:, j * P:(j + 1) * P], src[:, k * P:(k + 1) * P])
                        last.then_inc(filled, 1)
                elif kind == "WA":
                    wait_act(pe, g, ("attT", t, 0), "attT")
                    w = wait_weights(pe, g, "WA").rearrange("p k n -> p (k n)").rearrange("p (k n) -> p k n", n=1024)
                    project(g, stage, w, attT[:, :, toks], 4, n * CW)
                elif kind == "WR":
                    wait_act(pe, g, ("retT", t, 0), "retT")
                    project(g, stage, wait_weights(pe, g, f"WR{n}"), retT[:, :, toks], KD)
                elif kind == "WO":
                    wait_act(pe, g, ("mT", t, 0), "mT")
                    project(g, stage, wait_weights(pe, g, f"WO{n}"), actT[:, :, toks], KD)
                elif kind == "query":
                    wait_act(pe, g, ("norm2", GT - 1, 0), "hT")
                    w = wait_weights(pe, g, f"WQ{n // 2}")
                    bank = open_bank(pe, g, stage)
                    for half in range(2):
                        c0 = (n % 2) * 256 + half * P
                        for k in range(KD):
                            last = pe.matmul(bank[:, half * 256:(half + 1) * 256], w[:, k, c0:c0 + P], actT[:, k],
                                             start=(k == 0), stop=(k == KD - 1))
                    last.then_inc(filled, 1)
                elif kind == "keys":
                    wait_act(pe, g, ("query", None, n), "qT")
                    if is_first(g) and n == 0:
                        pe.wait_ge(keys_kept, 1)
                    bank = open_bank(pe, g, stage)
                    for tt in range(GT):
                        for half in range(2):
                            i = 2 * tt + half
                            last = pe.matmul(bank[:, i * P:(i + 1) * P], pqT[:, half, tt * P:(tt + 1) * P],
                                             keyT[:, half], start=True, stop=True)
                    last.then_inc(filled, 1)

            def retrieve(g, h, q):
                if not h:
                    return
                h -= 1
                t = h // PH
                for k in range(QN * q, QN * q + QN):
                    if not v_on_pe(k):
                        continue
                    n = GATHER[("v", h, k)]
                    pes = USED[n][1]
                    at_least(pe, diag_made, g * NUSED_PE + pes)
                    at_least(pe, row_landed[n % RING], g * (16 * (NGATHER // RING)) + 16 * (n // RING + 1))
                    first = h % PH == 0 and k == 0
                    if first:
                        at_least(pe, acc_made, (g + 1) * NACC + ACC_READ[0] if t else g * NACC + ACC_READ[GT - 1])
                    final = h % PH == PH - 1 and k == max(s for s in range(TOPK) if v_on_pe(s))
                    for j in range(2):
                        last = pe.matmul(vsum[j][:, :], diag[:, (pes - 1) % 4], rows[:, n % RING, j * CW:(j + 1) * CW],
                                         start=first, stop=final)
                    last.then_inc(used_pe, 1)

            pe.sem_inc(used_pe, NUSED_PE)
            pe.wait_ge(consts_landed, 16 * 8)
            for half in range(2):
                last = turn(vsum[0][:, half * P:(half + 1) * P], key_raw[:, half])
            last.then_inc(keys_turned, 1)
            for stage in STAGES:
                front(0, stage)
            with pe.Fori(0, GROUPS - 1) as r:
                for (h, q), stages in zip(QUARTERS, SHARE):
                    retrieve(r, h, q)
                    for stage in stages:
                        front(r + 1, stage)
            for h, q in QUARTERS:
                retrieve(GROUPS - 1, h, q)

        @block.scalar
        def _(act):
            steps = [0, 0]

            def own(g, ins):
                steps[0] += 1
                ins.then_inc(act_step, 1)
                act.wait_ge(act_step, g * steps[1] + steps[0])

            def rms_of(g, ss, rms, width):
                own(g, act.activation(rms, ss, ACT.Sqrt, bias=eps_t[:, 0:1], scale=1.0 / width))

            def drain_to(g, stage, i, dst, func=ACT.Copy, view=None):
                bank, free = wait_filled(act, g, stage, i)
                src = bank[:, :] if view is None else view(bank)
                own(g, act.activation(dst, src, func))
                act.sem_inc(free, 1)

            def front(g, stage):
                kind, t, n = stage
                toks = slice(t * P, t * P + P) if t is not None else None
                if kind == "norm":
                    if is_first(g) and t == 0:
                        act.wait_ge(set_up, 4)
                    at_least(act, x_landed[t], g * 32 + 32)
                    if t:
                        wait_filled(act, g, ("norm", t - 1, 0), 1)
                    else:
                        wait_dve(act, g - 1, ("retT", GT - 1, 0), "gated")
                        at_least(act, dve_made, (g - 1) * NDVE + DVE_AT[(("WR", GT - 1, 1), "m")] + 1)
                    own(g, act.activation(scratch[:], xh[:, t], ACT.Square, accum_out=col(SS + t)))
                    act.activation(col(RMS + t), col(SS + t), ACT.Sqrt, bias=eps_t[:, 0:1],
                                   scale=1.0 / D).then_inc(act_made, 1)
                    wait_dve(act, g, stage, "rstd")
                    act.activation(scratch[:], xh[:, t], ACT.Copy, scale=col(RSTD + t)).then_inc(act_made, 1)
                elif kind == "V":
                    at_least(act, dve_made, (g - 1) * NDVE + NDVE)
                    drain_to(g, stage, 0, v_r[:, t, n * CW:(n + 1) * CW])
                    act.sem_inc(act_made, 1)
                elif kind == "G":
                    drain_to(g, stage, 0, g_r[:, t, n * CW:(n + 1) * CW], ACT.Silu)
                    act.sem_inc(act_made, 1)
                elif kind == "heads":
                    drain_to(g, stage, 0, hqT[:, :, :].rearrange("p a b -> p (a b)"))
                    act.sem_inc(act_made, 1)
                    drain_to(g, stage, 1, kTa[:, (t + 1) * P:(t + 2) * P], view=lambda b: b[:, 0:P])
                    act.sem_inc(act_made, 1)
                elif kind == "score":
                    wait_dve(act, g, stage, "masked")
                    for h in range(HEADS):
                        ins = act.activation(probs[:, h], probs[:, h], ACT.Exp, bias=col(NM + h),
                                             accum_out=col(RSUM + h))
                    own(g, ins)
                    act.activation(col(ESNK, HEADS), col(ESNK, HEADS), ACT.Exp).then_inc(act_made, 1)
                elif kind == "turn":
                    for i in range(4):
                        drain_to(g, stage, i, probsT[:, 2 * i:2 * i + 2].rearrange("p h b q -> p (h b q)"))
                    act.sem_inc(act_made, 1)
                elif kind == "attT":
                    drain_to(g, stage, 0, attT[:, :, toks], view=lambda b: b[:, :].rearrange("p (k q) -> p k q", k=4))
                    if t == GT - 1:
                        own(g, act.activation(kTa[:, 0:P], kTa[:, GT * P:(GT + 1) * P], ACT.Copy))
                        own(g, act.activation(va[:, 0], va[:, GT], ACT.Copy))
                    act.sem_inc(act_made, 1)
                elif kind == "rheads":
                    if t:
                        pass
                    drain_to(g, stage, 0, hqT[:, :, :].rearrange("p a b -> p (a b)"))
                    act.sem_inc(act_made, 1)
                    drain_to(g, stage, 1, rkT[:, :, :].rearrange("p a b -> p (a b)"))
                    act.sem_inc(act_made, 1)
                elif kind == "rmix":
                    for c in range(2):
                        bank, _ = wait_filled(act, g, stage, c)
                        if c == 0:
                            if t:
                                wait_dve(act, g, ("retT", t - 1, 0), "gated")
                            else:
                                wait_filled(act, g, ("norm", GT - 1, 0), 1)
                        for p in range(4):
                            ins = act.activation(scratch[:, (c * 4 + p) * P:(c * 4 + p + 1) * P],
                                                 bank[:, p * P:(p + 1) * P], ACT.Square, accum_out=col(SSR + c * 4 + p))
                    own(g, ins)
                    act.activation(col(RMSR, RH), col(SSR, RH), ACT.Sqrt, bias=eps_t[:, 0:1],
                                   scale=1.0 / RV).then_inc(act_made, 1)
                elif kind in ("retT", "mT"):
                    dst = retT if kind == "retT" else actT
                    for i in range(2):
                        drain_to(g, stage, i, dst[:, 4 * i:4 * i + 4, toks],
                                 view=lambda b: b[:, :].rearrange("p (k q) -> p k q", k=4))
                    act.sem_inc(act_made, 1)
                elif kind == "WA":
                    wait_dve(act, g, ("rheads", t, 0), "weighted")
                    drain_to(g, stage, 0, qk_m[:, t, n * CW:(n + 1) * CW])
                    act.sem_inc(act_made, 1)
                elif kind in ("GA", "GR"):
                    if kind == "GR" or n:
                        wait_dve(act, g, ("GA", t, n - 1) if kind == "GA" else
                                 (("WR", t, n - 1) if n else ("GA", t, 1)), "m")
                    drain_to(g, stage, 0, qa[:, t], ACT.Sigmoid)
                    act.sem_inc(act_made, 1)
                elif kind == "norm2":
                    wait_dve(act, g, ("WO", t, 1), "h")
                    if t:
                        pass
                    own(g, act.activation(scratch[:], xh[:, t], ACT.Square, accum_out=col(SS + t)))
                    act.activation(col(RMS + t), col(SS + t), ACT.Sqrt, bias=eps_t[:, 0:1],
                                   scale=1.0 / D).then_inc(act_made, 1)
                    for i in range(2):
                        drain_to(g, stage, i, actT[:, 4 * i:4 * i + 4, toks],
                                 view=lambda b: b[:, :].rearrange("p (k q) -> p k q", k=4))
                    act.sem_inc(act_made, 1)
                elif kind == "query":
                    if n:
                        wait_filled(act, g, ("keys", None, n - 1))
                    drain_to(g, stage, 0, pqT[:, :, :].rearrange("p a b -> p (a b)"))
                    act.sem_inc(act_made, 1)
                elif kind == "keys":
                    drain_to(g, stage, 0, scores[:, :, 2 * n:2 * n + 2, :],
                             view=lambda b: b[:, :].rearrange("p (t s k) -> p t s k", t=GT, s=2))
                    act.sem_inc(act_made, 1)
                elif kind == "gate":
                    wait_dve(act, g, stage, "diff")
                    act.activation(expg[:], expg[:], ACT.Exp).then_inc(act_made, 1)

            def retrieve(g, h, q):
                if h < NH2 and q == 0 and h:
                    pass
                if h and q == 0:
                    hp = h - 1
                    t, s0 = hp // PH, (hp % PH) * TOPK
                    n = GATHER[("u", hp, TOPK - 1)]
                    at_least(act, used_dve, (g + 1) * NUSED_DVE + USED[n][0])
                    act.activation(dots[:, t, s0:s0 + TOPK], dots[:, t, s0:s0 + TOPK], ACT.Gelu).then_inc(gelu_made, 1)
                if h:
                    hp = h - 1
                    t, s0 = hp // PH, (hp % PH) * TOPK
                    for k in range(QN * q, QN * q + QN):
                        if not v_on_pe(k):
                            continue
                        n = GATHER[("v", hp, k)]
                        pes = USED[n][1]
                        at_least(act, coef_made, g * NH2 + hp + 1)
                        at_least(act, used_pe, (g + 1) * NUSED_PE + pes - 4)
                        act.activation(diag[:, (pes - 1) % 4], ident, ACT.Copy,
                                       scale=coef[:, t, s0 + k:s0 + k + 1]).then_inc(diag_made, 1)
                    if hp % PH == PH - 1 and q == TOPK // QN - 1:
                        at_least(act, acc_made, (g + 1) * NACC + t * PER_TILE + 3)
                        act.activation(vacc[:], h_cur[:, t], ACT.Square, accum_out=col(FSS)).then_inc(fin_rms, 1)
                        act.wait_ge(fin_rms, g * (2 * GT) + 2 * t + 1)
                        act.activation(col(FRMS), col(FSS), ACT.Sqrt, bias=eps_t[:, 0:1],
                                       scale=1.0 / D).then_inc(fin_rms, 1)
                        act.wait_ge(out_made, g * GT + t + 1)
                        act.dma_start(out[bass.ds(g * (GT * P) + t * P, P), :], h_cur[:, t]).then_inc(out_stored[t], 16)

            def hand_over(g):
                for t in range(GT):
                    at_least(act, out_stored[t], g * 16)
                    wait_dve(act, g, ("WO", t, 1), "h")
                    act.activation(h_cur[:, t], xh[:, t], ACT.Copy).then_inc(handed_act, 1)

            act.wait_ge(keys_turned, 1)
            act.activation(keyT[:, :, :].rearrange("p a b -> p (a b)"), vsum[0][:, 0:2 * P], ACT.Copy).then_inc(keys_kept, 1)
            for stage in STAGES:
                front(0, stage)
            steps[1] = steps[0]
            hand_over(0)
            with act.Fori(0, GROUPS - 1) as r:
                steps[0] = 0
                for (h, q), stages in zip(QUARTERS, SHARE):
                    retrieve(r, h, q)
                    for stage in stages:
                        front(r + 1, stage)
                assert steps[0] == steps[1]
                hand_over(r + 1)
            for h, q in QUARTERS:
                retrieve(GROUPS - 1, h, q)
            for t in range(GT):
                act.wait_ge(out_stored[t], 16 * GROUPS)

        @block.vector
        def _(dve):
            steps = [0, 0]

            def own(g, ins, apart=False):
                steps[0] += 1
                ins.then_inc(dve_step, 1)
                if apart:
                    hold(dve, dve_step, g * steps[1] + steps[0])
                else:
                    dve.wait_ge(dve_step, g * steps[1] + steps[0])

            def rotate(g, bank, free, dst, src, cos, sin, tmp, rest=None):
                w = src.shape[-1] // 2
                lo, hi = (slice(None),) * (len(src.shape) - 1) + (slice(0, w),), \
                    (slice(None),) * (len(src.shape) - 1) + (slice(w, 2 * w),)
                dve.tensor_tensor(tmp[lo], src[hi], sin[lo], ALU.mult)
                dve.tensor_tensor(tmp[hi], src[lo], sin[hi], ALU.mult)
                if rest is not None:
                    dve.tensor_copy(*rest)
                own(g, dve.tensor_tensor(dst, src, cos, ALU.mult))
                own(g, dve.tensor_tensor(dst, dst, tmp, ALU.add))
                dve.sem_inc(free, 1)

            def front(g, stage):
                kind, t, n = stage
                toks = slice(t * P, t * P + P) if t is not None else None
                if kind == "norm":
                    wait_act(dve, g, stage, "rms")
                    dve.reciprocal(col(RSTD + t), col(RMS + t)).then_inc(dve_made, 1)
                    if t == 0:
                        at_least(dve, filled, (g - 1) * NFILL + FILL[(("query", None, PH - 1), 0)] + 1)
                    for i in range(2):
                        bank, free = wait_filled(dve, g, stage, i)
                        gain = gain_mix[:, 4 * i:4 * i + 4].unsqueeze(2).to_broadcast([P, 4, P])
                        own(g, dve.tensor_tensor(actT[:, 4 * i:4 * i + 4, toks],
                                                 bank[:, :].rearrange("p (k q) -> p k q", k=4), gain, ALU.mult))
                        dve.sem_inc(free, 1)
                    dve.sem_inc(dve_made, 1)
                elif kind == "A0":
                    bank, free = wait_filled(dve, g, stage)
                    src = bank[:, :].rearrange("p (c h d) -> p c h d", c=2, h=4)
                    dst = qa[:, t].rearrange("p (h c d) -> p c h d", c=2, h=4)
                    cos = rot[:, t, 128:144]
                    sin = rot[:, t, 144:160]
                    for c in range(2):
                        tmp = att[:, c * 64:c * 64 + 64].rearrange("p (h d) -> p h d", h=4)
                        cs = cos.unsqueeze(1).to_broadcast([P, 4, ROT_A])
                        sn = sin.unsqueeze(1).to_broadcast([P, 4, ROT_A])
                        s = src[:, c]
                        o = dst[:, c]
                        dve.tensor_tensor(tmp[:, :, 0:8], s[:, :, 8:16], sn[:, :, 0:8], ALU.mult)
                        dve.tensor_tensor(tmp[:, :, 8:16], s[:, :, 0:8], sn[:, :, 8:16], ALU.mult)
                        dve.tensor_copy(o[:, :, 16:64], s[:, :, 16:64])
                        own(g, dve.tensor_tensor(o[:, :, 0:16], s[:, :, 0:16], cs, ALU.mult))
                        own(g, dve.tensor_tensor(o[:, :, 0:16], o[:, :, 0:16], tmp, ALU.add))
                    dve.sem_inc(free, 1)
                    dve.sem_inc(dve_made, 1)
                elif kind == "A1":
                    bank, free = wait_filled(dve, g, stage)
                    s = bank[:, 0:P].rearrange("p (h d) -> p h d", h=KVH)
                    o = ka[:, t].rearrange("p (h d) -> p h d", h=KVH)
                    tmp = att[:, 0:32].rearrange("p (h d) -> p h d", h=KVH)
                    cs = rot[:, t, 128:144].unsqueeze(1).to_broadcast([P, KVH, ROT_A])
                    sn = rot[:, t, 144:160].unsqueeze(1).to_broadcast([P, KVH, ROT_A])
                    dve.tensor_tensor(tmp[:, :, 0:8], s[:, :, 8:16], sn[:, :, 0:8], ALU.mult)
                    dve.tensor_tensor(tmp[:, :, 8:16], s[:, :, 0:8], sn[:, :, 8:16], ALU.mult)
                    dve.tensor_copy(o[:, :, 16:64], s[:, :, 16:64])
                    if t == 0:
                        at_least(dve, act_made, (g - 1) * NACT + ACT_AT[(("attT", GT - 1, 0), "attT")] + 1)
                    dve.tensor_copy(va[:, t + 1], bank[:, P:2 * P])
                    own(g, dve.tensor_tensor(o[:, :, 0:16], s[:, :, 0:16], cs, ALU.mult))
                    own(g, dve.tensor_tensor(o[:, :, 0:16], o[:, :, 0:16], tmp, ALU.add))
                    dve.sem_inc(free, 1)
                    dve.sem_inc(dve_made, 1)
                elif kind in ("QR", "KR"):
                    bank, free = wait_filled(dve, g, stage)
                    c0 = 0 if kind == "QR" else 512
                    s = bank[:, :].rearrange("p (h d) -> p h d", h=RH)
                    o = qk_m[:, t, c0:c0 + 512].rearrange("p (h d) -> p h d", h=RH)
                    tmp = att[:, :].rearrange("p (h d) -> p h d", h=RH)
                    if kind == "QR" and t == 0:
                        at_least(dve, filled, (g - 1) * NFILL + FILL[(("mT", GT - 1, 0), 1)] + 1)
                    cs = rot[:, t, 0:64].unsqueeze(1).to_broadcast([P, RH, ROT_R])
                    sn = rot[:, t, 64:128].unsqueeze(1).to_broadcast([P, RH, ROT_R])
                    dve.tensor_tensor(tmp[:, :, 0:32], s[:, :, 32:64], sn[:, :, 0:32], ALU.mult)
                    dve.tensor_tensor(tmp[:, :, 32:64], s[:, :, 0:32], sn[:, :, 32:64], ALU.mult)
                    own(g, dve.tensor_tensor(o, s, cs, ALU.mult))
                    own(g, dve.tensor_tensor(o, o, tmp, ALU.add))
                    dve.sem_inc(free, 1)
                    dve.sem_inc(dve_made, 1)
                elif kind == "score":
                    mask = mask_first if is_first(g) and t == 0 else const[:, C_MASK:C_MASK + 256]
                    for i in range(4):
                        bank, free = wait_filled(dve, g, stage, i)
                        own(g, dve.scalar_tensor_tensor(
                            out=probs[:, 2 * i:2 * i + 2], in0=bank[:, :].rearrange("p (h k) -> p h k", h=2),
                            scalar=HD ** -0.5, in1=mask.unsqueeze(1).to_broadcast([P, 2, 2 * P]),
                            op0=ALU.mult, op1=ALU.add))
                        dve.sem_inc(free, 1)
                    own(g, dve.tensor_reduce(col(MX, HEADS), probs[:], AX.X, ALU.max))
                    own(g, dve.tensor_tensor(col(MX, HEADS), col(MX, HEADS), sinks[:], ALU.max))
                    dve.tensor_tensor(col(ESNK, HEADS), sinks[:], col(MX, HEADS), ALU.subtract)
                    own(g, dve.tensor_scalar(col(NM, HEADS), col(MX, HEADS), -1.0, None, ALU.mult))
                    dve.sem_inc(dve_made, 1)
                elif kind == "mix":
                    wait_act(dve, g, ("score", t, 0), "probs")
                    own(g, dve.tensor_tensor(col(DEN, HEADS), col(RSUM, HEADS), col(ESNK, HEADS), ALU.add))
                    own(g, dve.reciprocal(col(DEN, HEADS), col(DEN, HEADS)))
                    bank, free = wait_filled(dve, g, stage)
                    own(g, dve.tensor_tensor(att[:, :].rearrange("p (h d) -> p h d", h=HEADS),
                                             bank[:, :].rearrange("p (h d) -> p h d", h=HEADS),
                                             col(DEN, HEADS).unsqueeze(2).to_broadcast([P, HEADS, HD]), ALU.mult))
                    dve.sem_inc(free, 1)
                    dve.sem_inc(dve_made, 1)
                elif kind == "rheads":
                    wait_act(dve, g, stage, "qT")
                    if t:
                        wait_filled(dve, g, ("rmix", t - 1, 0), 3)
                    dve.tensor_tensor(rqwT[:], hqT[:], const[:, C_WQ:C_WQ + 512].rearrange("p (a b) -> p a b", a=4),
                                      ALU.mult)
                    own(g, dve.tensor_tensor(kw[:, :].rearrange("p (h d) -> p h d", h=RH),
                                             qk_m[:, t, 512:1024].rearrange("p (h d) -> p h d", h=RH),
                                             const[:, C_WK:C_WK + RH].unsqueeze(2).to_broadcast([P, RH, RQ]), ALU.mult))
                    dve.sem_inc(dve_made, 1)
                elif kind == "rscore":
                    for c in range(2):
                        bank, free = wait_filled(dve, g, stage, c)
                        own(g, dve.tensor_tensor(decayed[:, 4 * c:4 * c + 4],
                                                 bank[:, :].rearrange("p (a b) -> p a b", a=4),
                                                 const[:, C_DECAY + c * 512:C_DECAY + (c + 1) * 512].rearrange(
                                                     "p (a b) -> p a b", a=4), ALU.mult))
                        dve.sem_inc(free, 1)
                    dve.sem_inc(dve_made, 1)
                elif kind == "rmix":
                    wait_act(dve, g, stage, "rms")
                    own(g, dve.reciprocal(col(RINV, RH), col(RMSR, RH)))
                    for c in range(2):
                        bank, free = wait_filled(dve, g, stage, c)
                        own(g, dve.tensor_tensor(
                            scratch[:, c * 512:(c + 1) * 512].rearrange("p (a b) -> p a b", a=4),
                            bank[:, :].rearrange("p (a b) -> p a b", a=4),
                            col(RINV + 4 * c, 4).unsqueeze(2).to_broadcast([P, 4, RV]), ALU.mult))
                        dve.sem_inc(free, 1)
                    dve.sem_inc(dve_made, 1)
                    own(g, dve.tensor_tensor(state[:], state[:],
                                             const[:, C_SD:C_SD + 4].unsqueeze(2).to_broadcast([P, 4, RV]), ALU.mult))
                    for i in range(2):
                        bank, free = wait_filled(dve, g, stage, 2 + i)
                        for c in range(2):
                            rows_c = slice(64 * c, 64 * c + 64)
                            src = bank[rows_c, :].rearrange("p (a b) -> p a b", a=2)[:, :, c * RV:(c + 1) * RV]
                            ins = dve.tensor_tensor(state[rows_c, 2 * i:2 * i + 2], state[rows_c, 2 * i:2 * i + 2],
                                                    src, ALU.add)
                        own(g, ins)
                        dve.sem_inc(free, 1)
                    dve.sem_inc(dve_made, 1)
                elif kind == "retT":
                    wait_act(dve, g, ("G", t, 1), "silu")
                    gv = g_r[:, t].rearrange("p (a c d) -> p c a d", a=4, c=2)
                    for c in range(2):
                        ins = dve.tensor_tensor(gv[:, c], scratch[:, c * 512:(c + 1) * 512].rearrange(
                            "p (a d) -> p a d", a=4), gv[:, c], ALU.mult)
                    ins.then_inc(dve_made, 1)
                elif kind == "GA":
                    wait_act(dve, g, stage, "sig")
                    wait_act(dve, g, ("WA", t, n), "m")
                    m = qk_m[:, t, n * CW:(n + 1) * CW]
                    dve.tensor_tensor(m, m, qa[:, t], ALU.mult).then_inc(dve_made, 1)
                elif kind == "WR":
                    wait_act(dve, g, ("GR", t, n), "sig")
                    bank, free = wait_filled(dve, g, stage)
                    own(g, dve.tensor_tensor(qa[:, t], bank[:, :], qa[:, t], ALU.mult))
                    dve.sem_inc(free, 1)
                    m = qk_m[:, t, n * CW:(n + 1) * CW]
                    dve.wait_ge(dve_made, g * NDVE + DVE_AT[(("GA", t, n), "m")] + 1)
                    dve.tensor_tensor(m, m, qa[:, t], ALU.add).then_inc(dve_made, 1)
                elif kind == "WO":
                    bank, free = wait_filled(dve, g, stage)
                    hcol = xh[:, t, n * CW:(n + 1) * CW]
                    own(g, dve.tensor_tensor(hcol, bank[:, :], hcol, ALU.add))
                    dve.sem_inc(free, 1)
                    dve.sem_inc(dve_made, 1)
                elif kind == "norm2":
                    wait_act(dve, g, stage, "rms")
                    own(g, dve.reciprocal(col(RSTD + t), col(RMS + t)))
                    dve.sem_inc(dve_made, 1)
                    if t == 0:
                        wait_filled(dve, g, ("WR", GT - 1, 1))
                    dve.scalar_tensor_tensor(out=hn[:, t], in0=xh[:, t], scalar=col(RSTD + t), in1=gain_ffn[:],
                                             op0=ALU.mult, op1=ALU.mult).then_inc(dve_made, 1)
                elif kind == "top":
                    wait_act_value = g * NACT + ACT_AT[(("keys", None, n), "scores")] + 1
                    hold(dve, act_made, wait_act_value)
                    pairs = [(tt, half) for tt in range(GT) for half in range(2)]
                    for step in range(5):
                        for tt, half in pairs:
                            s = scores[:, tt, 2 * n + half]
                            lo, hi = top_v[:, tt, n, half, 0:8], top_v[:, tt, n, half, 8:16]
                            ilo, ihi = top_i[:, tt, n, half, 0:8], top_i[:, tt, n, half, 8:16]
                            if step == 0:
                                ins = dve.max(lo, s)
                            elif step == 1:
                                ins = dve.max_index(ilo, lo, s)
                            elif step == 2:
                                ins = dve.match_replace(s, lo, s, LOWEST)
                            elif step == 3:
                                ins = dve.max(hi, s)
                            else:
                                ins = dve.max_index(ihi, hi, s)
                        own(g, ins, apart=True)
                    dve.sem_inc(dve_made, 1)
                elif kind == "cand":
                    hs = range(4 * n, 4 * n + 4)
                    c4 = cands[:, t, 4 * n:4 * n + 4].rearrange("p h (a b) -> p h a b", a=TOPK)
                    for h in hs:
                        ins = dve.tensor_tensor(cands[:, t, h].rearrange("p (a b) -> p a b", a=TOPK),
                                                top_v[:, t, h, 0].unsqueeze(2).to_broadcast([P, TOPK, TOPK]),
                                                top_v[:, t, h, 1].unsqueeze(1).to_broadcast([P, TOPK, TOPK]), ALU.add)
                    own(g, ins, apart=True)
                    for step in range(5):
                        for h in hs:
                            s = cands[:, t, h]
                            b = h * TOPK
                            lo, hi = pick_v[:, t, b:b + 8], pick_v[:, t, b + 8:b + 16]
                            ilo, ihi = pick_i[:, t, b:b + 8], pick_i[:, t, b + 8:b + 16]
                            if step == 0:
                                ins = dve.max(lo, s)
                            elif step == 1:
                                ins = dve.max_index(ilo, lo, s)
                            elif step == 2:
                                ins = dve.match_replace(s, lo, s, LOWEST)
                            elif step == 3:
                                ins = dve.max(hi, s)
                            else:
                                ins = dve.max_index(ihi, hi, s)
                        own(g, ins, apart=True)
                    dve.sem_inc(dve_made, 1)
                elif kind == "gate":
                    pv = pick_v[:, t].rearrange("p (h k) -> p h k", h=PH)
                    ev = expg[:, :].rearrange("p (h k) -> p h k", h=PH)
                    own(g, dve.tensor_tensor(ev, pv, pv[:, :, 0:1].to_broadcast([P, PH, TOPK]), ALU.subtract))
                    dve.sem_inc(dve_made, 1)
                    wait_act(dve, g, stage, "exp")
                    own(g, dve.tensor_reduce(col(GSUM, PH), ev, AX.X, ALU.add))
                    own(g, dve.reciprocal(col(GINV, PH), col(GSUM, PH)))
                    own(g, dve.tensor_tensor(gate_next[:, t].rearrange("p (h k) -> p h k", h=PH), ev,
                                             col(GINV, PH).unsqueeze(2).to_broadcast([P, PH, TOPK]), ALU.mult))
                    dve.sem_inc(dve_made, 1)
                elif kind == "decode":
                    half_slots = SLOTS // 2
                    picks = pick_i[:, t, n * half_slots:(n + 1) * half_slots]
                    dve.tensor_scalar(part[:, 0], picks, 4, None, ALU.logical_shift_right)
                    dve.tensor_scalar(part[:, 1], picks, 15, None, ALU.bitwise_and)
                    own(g, dve.tensor_copy(top_if[:], top_i[:, t, 4 * n:4 * n + 4]))
                    iota = const[:, C_IOTA:C_IOTA + 16].unsqueeze(1).to_broadcast([P, half_slots, TOPK])
                    big = [probs[:, 0:4].rearrange("p a b -> p (a b)").rearrange("p (s j) -> p s j", j=TOPK),
                           probs[:, 4:8].rearrange("p a b -> p (a b)").rearrange("p (s j) -> p s j", j=TOPK)]
                    for w in range(2):
                        ins = dve.tensor_tensor(big[w], part[:, w].unsqueeze(2).to_broadcast([P, half_slots, TOPK]),
                                                iota, ALU.is_equal)
                    own(g, ins)
                    for w in range(2):
                        for h in range(4):
                            b = big[w][:, h * TOPK:(h + 1) * TOPK]
                            ins = dve.tensor_tensor(b, b, top_if[:, h, w].unsqueeze(1).to_broadcast([P, TOPK, TOPK]),
                                                    ALU.mult)
                    own(g, ins)
                    for w in range(2):
                        ins = dve.tensor_reduce(sel[:, w], big[w], AX.X, ALU.add)
                    own(g, ins)
                    own(g, dve.scalar_tensor_tensor(out=index_next[:, t, n * half_slots:(n + 1) * half_slots],
                                                    in0=sel[:, 0], scalar=float(NKEY), in1=sel[:, 1],
                                                    op0=ALU.mult, op1=ALU.add))
                    dve.sem_inc(dve_made, 1)

            def retrieve(g, h, q):
                acc_base = 0
                for k in range(QN * q, QN * q + QN):
                    if h < NH2:
                        n = GATHER[("u", h, k)]
                        t, slot = h // PH, (h % PH) * TOPK + k
                        at_least(dve, row_landed[n % RING], g * (16 * (NGATHER // RING)) + 16 * (n // RING + 1))
                        dve.tensor_tensor_reduce(out=rows[:, n % RING], in0=rows[:, n % RING], in1=hn_cur[:, t],
                                                 scale=1.0, scalar=0.0, op0=ALU.mult, op1=ALU.add,
                                                 accum_out=dots[:, t, slot:slot + 1]).then_inc(used_dve, 1)
                    if not h:
                        continue
                    hp = h - 1
                    t, s0 = hp // PH, (hp % PH) * TOPK
                    if k == 0:
                        dve.wait_ge(gelu_made, g * NH2 + hp + 1)
                        dve.tensor_tensor(coef[:, t, s0:s0 + TOPK], dots[:, t, s0:s0 + TOPK],
                                          gate_cur[:, t, s0:s0 + TOPK], ALU.mult).then_inc(coef_made, 1)
                    if v_on_pe(k):
                        continue
                    n = GATHER[("v", hp, k)]
                    mine = [s for s in range(TOPK) if not v_on_pe(s)]
                    number = (hp % PH) * len(mine) + mine.index(k)
                    at_least(dve, row_landed[n % RING], g * (16 * (NGATHER // RING)) + 16 * (n // RING + 1))
                    c = coef[:, t, s0 + k:s0 + k + 1]
                    if number == 0:
                        dve.wait_ge(coef_made, g * NH2 + hp + 1)
                        ins = dve.tensor_scalar(vacc[:], rows[:, n % RING], c, None, ALU.mult)
                    else:
                        prev = GATHER[("v", hp - (mine.index(k) == 0), mine[mine.index(k) - 1])]
                        dve.wait_ge(used_dve, (g + 1) * NUSED_DVE + USED[prev][0])
                        if number % len(mine) == 0:
                            dve.wait_ge(coef_made, g * NH2 + hp + 1)
                        ins = dve.scalar_tensor_tensor(out=vacc[:], in0=rows[:, n % RING], scalar=c, in1=vacc[:],
                                                       op0=ALU.mult, op1=ALU.add)
                    ins.then_inc(used_dve, 1)
                if h and (h - 1) % PH == PH - 1 and q == TOPK // QN - 1:
                    t = (h - 1) // PH
                    base = (g + 1) * NACC + t * PER_TILE
                    dve.wait_ge(used_dve, (g + 1) * NUSED_DVE + USED[n][0])
                    pes = USED[GATHER[("v", h - 1, max(s for s in range(TOPK) if v_on_pe(s)))]][1]
                    dve.wait_ge(used_pe, (g + 1) * NUSED_PE + pes)
                    dve.tensor_tensor(vacc[:, 0:CW], vacc[:, 0:CW], vsum[0][:, :], ALU.add).then_inc(acc_made, 1)
                    dve.tensor_tensor(vacc[:, CW:D], vacc[:, CW:D], vsum[1][:, :], ALU.add).then_inc(acc_made, 1)
                    dve.wait_ge(acc_made, base + 2)
                    dve.wait_ge(handed_act, g * GT + GT)
                    dve.tensor_tensor(h_cur[:, t], h_cur[:, t], vacc[:], ALU.add).then_inc(acc_made, 1)
                    dve.wait_ge(fin_rms, g * (2 * GT) + 2 * t + 2)
                    dve.reciprocal(col(FRSTD), col(FRMS)).then_inc(acc_made, 1)
                    dve.wait_ge(acc_made, base + 4)
                    dve.scalar_tensor_tensor(out=h_cur[:, t], in0=h_cur[:, t], scalar=col(FRSTD), in1=gain_fin[:],
                                             op0=ALU.mult, op1=ALU.mult).then_inc(out_made, 1)

            def hand_over(g):
                dve.wait_ge(dve_made, g * NDVE + NDVE)
                at_least(dve, used_pe, (g + 1) * NUSED_PE)
                at_least(dve, used_dve, (g + 1) * NUSED_DVE)
                dve.tensor_copy(index_cur[:], index_next[:])
                dve.tensor_copy(gate_cur[:], gate_next[:])
                dve.tensor_copy(hn_cur[:], hn).then_inc(handed_dve, 1)
                dve.wait_ge(handed_dve, g + 1)

            dve.sem_inc(used_dve, NUSED_DVE)
            dve.sem_inc(acc_made, NACC)
            dve.wait_ge(consts_landed, 16 * 8)
            dve.wait_ge(set_up, 4)
            for stage in STAGES:
                front(0, stage)
            steps[1] = steps[0]
            hand_over(0)
            with dve.Fori(0, GROUPS - 1) as r:
                steps[0] = 0
                for (h, q), stages in zip(QUARTERS, SHARE):
                    retrieve(r, h, q)
                    for stage in stages:
                        front(r + 1, stage)
                assert steps[0] == steps[1]
                hand_over(r + 1)
            for h, q in QUARTERS:
                retrieve(GROUPS - 1, h, q)


_INS = ["x", "norm_mix", "w_in", "att_sinks", "w_att_branch", "w_ret_branch", "w_out", "norm_ffn", "peer_w_query",
        "peer_sub_keys_1", "peer_sub_keys_2", "peer_u", "peer_v", "norm_final"]


def kernel(**inputs):
    import numpy as _np
    import concourse.bacc as _bacc
    from concourse import mybir as _mybir
    from concourse.bass_utils import run_bass_kernel_spmd as _run

    nc = _bacc.Bacc("TRN2", target_bir_lowering=False, num_devices=1)
    arrays, aps = {}, {}
    for name in _INS:
        a = _np.ascontiguousarray(inputs[name])
        if a.ndim == 3:
            a = a[0]
        arrays[f"in_{name}"] = a
        aps[name] = nc.dram_tensor(f"in_{name}", a.shape, _mybir.dt.from_np(a.dtype), kind="ExternalInput").ap()
    const_table, rot_table, mask_table = shape_constants()
    for name, a in (("const_table", const_table), ("rot_table", rot_table), ("mask_table", mask_table)):
        arrays[f"in_{name}"] = a
        aps[name] = nc.dram_tensor(f"in_{name}", a.shape, _mybir.dt.from_np(a.dtype), kind="ExternalInput").ap()
    out = nc.dram_tensor("out_0", (SEQ, D), _mybir.dt.float32, kind="ExternalOutput").ap()
    build_block(nc, *[aps[n] for n in _INS], aps["const_table"], aps["rot_table"], aps["mask_table"], out)
    r = _run(nc, [arrays], core_ids=[0])
    return r.results[0]["out_0"].reshape(1, SEQ, D)
```

```python
from contextlib import ExitStack

import numpy as np

import concourse.bass as bass
from concourse import mybir

ALU = mybir.AluOpType
ACT = mybir.ActivationFunctionType
AX = mybir.AxisListType
F32 = mybir.dt.float32
U32 = mybir.dt.uint32

P = 128
SEQ, D = 1024, 1024
KD = D // P
GT = 2
GROUPS = SEQ // (P * GT)
HEADS, HD, KVH = 8, 64, 2
RH, RQ, RV = 8, 64, 128
PH, NKEY, TOPK = 8, 128, 16
SLOTS = PH * TOPK
EPS = 1e-6
CW = 512
NEG = -1.0e30
LOWEST = -3.0e38

CHUNKS = [("A0", "in", 0, 512), ("A1", "in", 512, 256), ("QR", "in", 768, 512), ("KR", "in", 1280, 512),
          ("V0", "in", 1792, 512), ("V1", "in", 2304, 512), ("G0", "in", 2816, 512), ("G1", "in", 3328, 512),
          ("WA", "att", 0, 1024), ("GA0", "in", 3840, 512), ("GA1", "in", 4352, 512),
          ("GR0", "in", 4864, 512), ("WR0", "ret", 0, 512), ("GR1", "in", 5376, 512), ("WR1", "ret", 512, 512),
          ("WO0", "out", 0, 512), ("WO1", "out", 512, 512),
          ("WQ0", "query", 0, 512), ("WQ1", "query", 512, 512), ("WQ2", "query", 1024, 512), ("WQ3", "query", 1536, 512)]
CHUNK = {c[0]: n for n, c in enumerate(CHUNKS)}
WBUFS = 2

EARLY_HEADS = 2
EARLY = (
    [("norm", 0, 0), ("norm", 1, 0), ("A0", 0, 0), ("A0", 1, 0), ("A1", 0, 0), ("A1", 1, 0),
     ("QR", 0, 0), ("heads", 0, 0), ("QR", 1, 0), ("score", 0, 0), ("KR", 0, 0), ("turn", 0, 0), ("KR", 1, 0),
     ("mix", 0, 0), ("V", 0, 0), ("attT", 0, 0), ("V", 1, 0), ("heads", 1, 0), ("V", 0, 1), ("score", 1, 0),
     ("V", 1, 1), ("turn", 1, 0), ("G", 0, 0), ("mix", 1, 0), ("G", 1, 0), ("attT", 1, 0), ("G", 0, 1),
     ("rheads", 0, 0), ("G", 1, 1), ("rscore", 0, 0), ("WA", 0, 0), ("rmix", 0, 0), ("WA", 0, 1), ("retT", 0, 0),
     ("rheads", 1, 0), ("WA", 1, 0), ("rscore", 1, 0), ("WA", 1, 1), ("rmix", 1, 0), ("GA", 0, 0), ("retT", 1, 0),
     ("GA", 1, 0), ("GA", 0, 1), ("GA", 1, 1)]
    + [(k, t, n) for n in range(2) for k in ("GR", "WR") for t in range(GT)]
    + [("mT", 0, 0), ("mT", 1, 0)]
    + [("WO", t, n) for n in range(2) for t in range(GT)]
    + [("norm2", 0, 0), ("norm2", 1, 0)]
    + [(k, None, h) for h in range(EARLY_HEADS) for k in ("query", "keys", "top", "pick", "index")]
)
LATE = [(k, None, h) for h in range(EARLY_HEADS, PH) for k in ("query", "keys", "top", "pick", "index")]
STAGES = EARLY + LATE

BANKS_OF = dict(norm=2, A0=1, A1=1, QR=1, KR=1, V=1, G=1, heads=2, score=4, turn=4, mix=1, attT=1, rheads=2,
                rscore=2, rmix=4, retT=2, WA=1, GA=1, GR=1, WR=1, mT=2, WO=1, norm2=2, query=1, keys=1)
FILLS = [(s, i) for s in STAGES for i in range(BANKS_OF.get(s[0], 0))]
FILL = {f: n for n, f in enumerate(FILLS)}
NFILL = len(FILLS)
WORKBANKS = 6

ACT_OF = dict(norm=("rms", "xn"), V=("v",), G=("silu",), heads=("qT", "kT"), score=("probs",), turn=("pT",),
              attT=("attT",), rheads=("qT", "kT"), rmix=("rms",), retT=("retT",), WA=("m",), GA=("sig",), GR=("sig",),
              mT=("mT",), norm2=("rms", "hT"), query=("qT",), keys=("scores",), pick=("exp",))
DVE_OF = dict(norm=("rstd", "hT"), A0=("q",), A1=("kv",), QR=("q",), KR=("k",), score=("masked",), mix=("att",),
              rheads=("weighted",), rscore=("decayed",), rmix=("ret", "state"), retT=("gated",), GA=("m",), WR=("m",),
              WO=("h",), norm2=("rstd", "hn"), top=("top",), pick=("picks",), index=("index",))


def places(made_in):
    order = [(s, r) for s in STAGES for r in made_in.get(s[0], ())]
    return {k: n for n, k in enumerate(order)}, len(order)


ACT_AT, NACT = places(ACT_OF)
DVE_AT, NDVE = places(DVE_OF)

RING = 10
QN = 4
NH2 = GT * PH
QUARTERS = [(h, q) for h in range(NH2 + 1) for q in range(TOPK // QN)]


def v_on_pe(slot):
    return slot % 2 == 0


def gathers():
    out = []
    for h, q in QUARTERS:
        for k in range(QN * q, QN * q + QN):
            if h < NH2:
                out.append(("u", h, k))
            if h:
                out.append(("v", h - 1, k))
    return out


GATHERS = gathers()
GATHER = {g: n for n, g in enumerate(GATHERS)}
NGATHER = len(GATHERS)


def landed_in(g, n):
    return g * (16 * len(range(n % RING, NGATHER, RING))) + 16 * (n // RING + 1)


def last_tenant(n):
    if n >= RING:
        return n - RING, False
    return max(range(n, NGATHER, RING)), True


def used_counts():
    dve = pe = 0
    out = []
    for kind, _, k in GATHERS:
        if kind == "v" and v_on_pe(k):
            pe += 1
        else:
            dve += 1
        out.append((dve, pe))
    return out, dve, pe


USED, NUSED_DVE, NUSED_PE = used_counts()

LATE_FROM, LATE_TO, HAND_0, HAND_1 = 2, 20, 63, 6


def share(stages, first, end):
    at = [len(stages) * (n - first) // (end - first) for n in range(first, end + 1)]
    return {n: stages[at[n - first]:at[n - first + 1]] for n in range(first, end)}


LATE_SHARE = share(LATE, LATE_FROM, LATE_TO)
EARLY_SHARE = share(EARLY, LATE_TO, HAND_0)

C_MASK, C_DECAY, C_WQ, C_WK, C_SD, C_ID, C_IOTA = 0, 256, 1280, 1792, 1800, 1804, 1932
C_ALL = 1948
ROT_R, ROT_A = 64, 16
T_ALL = 2 * (ROT_R + ROT_A)


def shape_constants():
    f = np.float32
    i = np.arange(P)
    c = np.zeros((P, C_ALL), f)
    diff = (i[:, None] + P) - np.arange(2 * P)[None, :]
    band = (diff >= 0) & (diff < P)
    c[:, C_MASK:C_MASK + 256] = np.where(band, 0.0, NEG)
    mask0 = np.where(band & (np.arange(2 * P)[None, :] >= P), 0.0, NEG).astype(f)
    lg = np.log1p(-np.exp2(-5.0 - np.arange(RH)))
    scale = RQ ** -0.5
    gap = i[None, :] - i[:, None]
    for half in range(2):
        for pair in range(4):
            h = 2 * pair + half
            block = np.where(gap >= 0, np.exp(lg[h] * np.maximum(gap, 0)), 0.0) * scale
            at = C_DECAY + (half * 4 + pair) * P
            c[:, at:at + P] = block
            c[half * 64:half * 64 + 64, C_WQ + pair * P:C_WQ + (pair + 1) * P] = np.exp(lg[h] * (i + 1.0))[None, :]
            c[half * 64:half * 64 + 64, C_SD + pair] = np.exp(lg[h] * P)
    for h in range(RH):
        c[:, C_WK + h] = np.exp(lg[h] * (P - 1.0 - i)) * scale
    c[:, C_ID:C_ID + P] = np.eye(P)
    c[:, C_IOTA:C_IOTA + 16] = np.arange(16)
    pos = np.arange(SEQ, dtype=f)
    rot = np.zeros((SEQ, T_ALL), f)
    at = 0
    for width, theta in ((ROT_R, 10000.0), (ROT_A, 500000.0)):
        half = width // 2
        freq = (f(theta) ** (-np.arange(half, dtype=f) / f(half))).astype(f)
        ang = (pos[:, None] * freq[None, :]).astype(np.float64)
        rot[:, at:at + width] = np.concatenate([np.cos(ang), np.cos(ang)], 1)
        rot[:, at + width:at + 2 * width] = np.concatenate([-np.sin(ang), np.sin(ang)], 1)
        at += 2 * width
    return c, rot, mask0


def is_first(g):
    return isinstance(g, int) and g == 0


def build_block(nc, x, norm_mix, w_in, att_sinks, w_att, w_ret, w_out, norm_ffn, w_query, keys1, keys2,
                peer_u, peer_v, norm_final, const_table, rot_table, mask_table, out):
    with ExitStack() as ctx:
        def sb(name, shape, dt=F32):
            return ctx.enter_context(nc.sbuf_tensor(name, shape, dt))

        def sem(name):
            return ctx.enter_context(nc.semaphore(name))

        work = [ctx.enter_context(nc.psum_tensor(f"work{i}", [P, CW], F32)) for i in range(WORKBANKS)]
        vsum = [ctx.enter_context(nc.psum_tensor(f"vsum{i}", [P, CW], F32)) for i in range(2)]

        const = sb("const", [P, C_ALL])
        gain_mix = sb("gain_mix", [P, KD])
        gain_ffn = sb("gain_ffn", [P, D])
        gain_fin = sb("gain_fin", [P, D])
        sinks = sb("sinks", [P, HEADS])
        keyT = sb("keyT", [P, 2, P])
        eps_t = sb("eps_t", [P, 1])
        rows = sb("rows", [P, RING, D])
        wbuf = sb("wbuf", [P, WBUFS, KD, CW])
        rot = sb("rot", [P, GT, T_ALL])
        xh = sb("xh", [P, GT, D])
        scratch = sb("scratch", [P, D])
        actT = sb("actT", [P, KD, GT * P])
        qa = sb("qa", [P, GT, 512])
        ka = sb("ka", [P, GT, P])
        va = sb("va", [P, GT + 1, P])
        kTa = sb("kTa", [P, (GT + 1) * P])
        probs = sb("probs", [P, HEADS, 2 * P])
        probsT = sb("probsT", [P, HEADS, 2, P])
        att = sb("att", [P, 512])
        attT = sb("attT", [P, 4, GT * P])
        qk_m = sb("qk_m", [P, GT, D])
        vg = sb("vg", [P, 2, GT, D])
        state = sb("state", [P, 4, RV])
        retT_hn = sb("retT_hn", [P, 2 * D])
        pqT = sb("pqT", [P, 2, GT * P])
        h_cur = sb("h_cur", [P, GT, D])
        hn_cur = sb("hn_cur", [P, GT, D])
        vacc = sb("vacc", [P, D])
        diag = sb("diag", [P, 4, P])
        small = sb("small", [P, 128])
        top_v = sb("top_v", [P, GT, 2, TOPK])
        top_i = sb("top_i", [P, GT, 2, TOPK], U32)
        top_if = sb("top_if", [P, 2, GT, TOPK])
        pick_v = sb("pick_v", [P, GT, TOPK])
        pick_i = sb("pick_i", [P, GT, TOPK], U32)
        part = sb("part", [P, 2, GT, TOPK], U32)
        sel = sb("sel", [P, 2, GT, TOPK])
        expg = sb("expg", [P, GT, TOPK])
        index_next = sb("index_next", [P, GT, EARLY_HEADS * TOPK], U32)
        index_cur = sb("index_cur", [P, GT, SLOTS], U32)
        gate_next = sb("gate_next", [P, GT, EARLY_HEADS * TOPK])
        gate_cur = sb("gate_cur", [P, GT, SLOTS])
        dots = sb("dots", [P, GT, SLOTS])
        coef = sb("coef", [P, GT, SLOTS])

        ident = const[:, C_ID:C_ID + P]
        decayed = probs[:, 0:4].rearrange("p a b -> p (a b)").rearrange("p (h i) -> p h i", h=RH)
        ret_parts = probsT[:, :].rearrange("p h b q -> p (h b q)").rearrange("p (n w) -> p n w", n=4)
        rkT = ret_parts[:, 0].rearrange("p (a b) -> p a b", a=4)
        rqwT = ret_parts[:, 1].rearrange("p (a b) -> p a b", a=4)
        kw = ret_parts[:, 2]
        hqT = ret_parts[:, 3].rearrange("p (a b) -> p a b", a=4)
        mask_first = hn_cur[:, 0, 0:2 * P]
        key_raw = vacc[:, 0:2 * P].rearrange("p (s k) -> p s k", s=2)
        v_r, g_r = vg[:, 0], vg[:, 1]
        retT = retT_hn[:, :].rearrange("p (k t) -> p k t", k=KD)
        hn = retT_hn[:, :].rearrange("p (t d) -> p t d", t=GT)
        scores = vg[:, :, :, :].rearrange("p a b d -> p (a b d)").rearrange("p (t s k) -> p t s k", t=GT, s=2 * PH)
        cands = vg[:, :, :, :].rearrange("p a b d -> p (a b d)").rearrange("p (t h c) -> p t h c", t=GT, h=PH)

        def col(n, w=1):
            return small[:, n:n + w]
        SS, RMS, RSTD = 0, 2, 4
        MX, NM, RSUM, ESNK, DEN = 8, 16, 24, 32, 40
        SSR, RMSR, RINV, GSUM, GINV = 48, 56, 64, 72, 80
        FSS, FRMS, FRSTD = 96, 98, 100

        consts_landed = sem("consts_landed")
        set_up = sem("set_up")
        keys_turned = sem("keys_turned")
        keys_kept = sem("keys_kept")
        x_landed = [sem(f"x_landed{t}") for t in range(GT)]
        w_landed = [sem(f"w_landed{b}") for b in range(WBUFS)]
        filled = sem("filled")
        drained = [sem(f"drained{b}") for b in range(WORKBANKS)]
        act_made = sem("act_made")
        dve_made = sem("dve_made")
        act_step = [sem("act_early_step"), sem("act_late_step")]
        dve_step = [sem("dve_early_step"), sem("dve_late_step")]
        row_landed = [sem(f"row_landed{b}") for b in range(RING)]
        used_dve = sem("used_dve")
        used_pe = sem("used_pe")
        gelu_made = sem("gelu_made")
        coef_made = sem("coef_made")
        diag_made = sem("diag_made")
        acc_made = sem("acc_made")
        fin_rms = sem("fin_rms")
        out_made = sem("out_made")
        out_stored = [sem(f"out_stored{t}") for t in range(GT)]
        handed_act = sem("handed_act")
        handed_dve = sem("handed_dve")
        passed = sem("passed")

        def act_count(g, stage, result):
            return g * NACT + ACT_AT[(stage, result)] + 1

        def dve_count(g, stage, result):
            return g * NDVE + DVE_AT[(stage, result)] + 1

        def fill_count(g, stage, i=0):
            return g * NFILL + FILL[(stage, i)] + 1

        def bank_of(stage, i=0):
            b = FILL[(stage, i)] % WORKBANKS
            return work[b], drained[b]

        def drain_count(g, stage, i=0):
            n = FILL[(stage, i)]
            return g * len(range(n % WORKBANKS, NFILL, WORKBANKS)) + n // WORKBANKS + 1

        def chunk(name):
            b = CHUNK[name] % WBUFS
            return wbuf[:, b], w_landed[b]

        def chunk_count(g, name):
            n = CHUNK[name]
            return g * (16 * len(range(n % WBUFS, len(CHUNKS), WBUFS))) + 16 * (n // WBUFS + 1)

        W_DRAM = {"in": w_in, "att": w_att, "ret": w_ret, "out": w_out, "query": w_query}
        PER_TILE = 4
        NACC = GT * PER_TILE
        ACC_READ = [t * PER_TILE + 2 for t in range(GT)]

        LAST_USE = {}
        for s in STAGES:
            kind, t, n = s
            name = {"A0": "A0", "A1": "A1", "QR": "QR", "KR": "KR", "WA": "WA"}.get(kind)
            if kind in ("V", "G", "GA", "GR", "WR", "WO"):
                name = f"{kind}{n}"
            if kind == "query":
                name = f"WQ{n // 2}"
            if name:
                LAST_USE[name] = s

        block = ctx.enter_context(nc.Block())

        @block.sync
        def _(sp):
            sp.dma_start(const[:], const_table).then_inc(consts_landed, 16)
            sp.dma_start(mask_first, mask_table).then_inc(consts_landed, 16)
            sp.dma_start(gain_mix[:], norm_mix.rearrange("a (k p) -> p (a k)", p=P), allow_slow_non_contiguous=True).then_inc(consts_landed, 16)
            for t in range(2):
                sp.dma_start(key_raw[:, t], (keys1, keys2)[t]).then_inc(consts_landed, 16)
            sp.dma_start(sinks[:], att_sinks[0].partition_broadcast(P)).then_inc(consts_landed, 16)
            sp.dma_start(gain_ffn[:], norm_ffn[0].partition_broadcast(P)).then_inc(consts_landed, 16)
            sp.dma_start(gain_fin[:], norm_final.partition_broadcast(P)).then_inc(consts_landed, 16)

            def loads(g):
                for t in range(GT):
                    if not is_first(g):
                        sp.wait_ge(handed_act, (g - 1) * GT + t + 1)
                    r0 = g * (GT * P) + t * P
                    sp.dma_start(xh[:, t], x[bass.ds(r0, P), :]).then_inc(x_landed[t], 16)
                    sp.dma_start(rot[:, t], rot_table[bass.ds(r0, P), :]).then_inc(x_landed[t], 16)
                for n, (name, which, c0, cw) in enumerate(CHUNKS):
                    buffer, landed = chunk(name)
                    if n >= WBUFS:
                        last = LAST_USE[CHUNKS[n - WBUFS][0]]
                        sp.wait_ge(filled, fill_count(g, last, BANKS_OF[last[0]] - 1))
                    elif not is_first(g):
                        last = LAST_USE[CHUNKS[max(range(n, len(CHUNKS), WBUFS))][0]]
                        sp.wait_ge(filled, fill_count(g - 1, last, BANKS_OF[last[0]] - 1))
                    src = W_DRAM[which].rearrange("(k p) n -> p k n", p=P)[:, :, c0:c0 + cw]
                    dst = buffer.rearrange("p k n -> p (k n)")[:, 0:src.shape[1] * cw].rearrange(
                        "p (k n) -> p k n", n=cw)
                    sp.dma_start(dst, src).then_inc(landed, 16)

            loads(0)
            with sp.Fori(0, GROUPS - 1) as r:
                loads(r + 1)

        @block.gpsimd
        def _(pool):
            pool.memset(eps_t[:], EPS).then_inc(set_up, 1)
            pool.memset(va[:, 0], 0.0).then_inc(set_up, 1)
            pool.memset(kTa[:, 0:P], 0.0).then_inc(set_up, 1)
            pool.memset(state[:], 0.0).then_inc(set_up, 1)

            def retrieve(g):
                for n, (kind, h, k) in enumerate(GATHERS):
                    t, head = h // PH, h % PH
                    if kind == "u" and k == 0:
                        if head < EARLY_HEADS:
                            pool.wait_ge(handed_dve, g * GT + t + 1)
                            pool.sem_inc(passed, 1)
                        else:
                            pool.wait_ge(dve_made, g * NDVE + DVE_AT[(("index", None, head), "index")] + 1)
                            pool.sem_inc(passed, 1)
                    m, of_last = last_tenant(n)
                    before = g if of_last else g + 1
                    dve, pe = USED[m]
                    kind_m, _, k_m = GATHERS[m]
                    if kind_m == "v" and v_on_pe(k_m):
                        pool.wait_ge(used_pe, before * NUSED_PE + pe)
                        pool.sem_inc(passed, 1)
                    else:
                        pool.wait_ge(used_dve, before * NUSED_DVE + dve)
                        pool.sem_inc(passed, 1)
                    slot = (h % PH) * TOPK + k
                    pool.indirect_dma_start(
                        rows[:, n % RING], None, (peer_u if kind == "u" else peer_v),
                        bass.IndirectOffsetOnAxis(ap=index_cur[:, h // PH, slot:slot + 1], axis=0),
                    ).then_inc(row_landed[n % RING], 16)

            with pool.Fori(0, GROUPS) as r:
                retrieve(r)

        @block.tensor
        def _(pe):
            def turn(dst, src):
                return pe.transpose(dst, src, ident)

            def project(g, stage, weights, lhs, steps, c0=0, cw=CW):
                bank, free = bank_of(stage)
                pe.wait_ge(free, drain_count(g, stage))
                for k in range(steps):
                    last = pe.matmul(bank[:, 0:cw], lhs[:, k], weights[:, k, c0:c0 + cw],
                                     start=(k == 0), stop=(k == steps - 1))
                last.then_inc(filled, 1)

            def front(g, stage):
                kind, t, n = stage
                toks = slice(t * P, t * P + P) if t is not None else None
                if kind in ("norm", "norm2"):
                    src = scratch if kind == "norm" else hn[:, t]
                    if kind == "norm":
                        pe.wait_ge(act_made, act_count(g, stage, "xn"))
                    else:
                        pe.wait_ge(dve_made, dve_count(g, stage, "hn"))
                    for i in range(2):
                        bank, free = bank_of(stage, i)
                        pe.wait_ge(free, drain_count(g, stage, i))
                        for j in range(4):
                            k = 4 * i + j
                            last = turn(bank[:, j * P:(j + 1) * P], src[:, k * P:(k + 1) * P])
                        last.then_inc(filled, 1)
                elif kind in ("A0", "A1", "QR", "KR", "V", "G", "GA", "GR"):
                    name = kind + str(n) if kind in ("V", "G", "GA", "GR") else kind
                    pe.wait_ge(dve_made, dve_count(g, ("norm", t, 0), "hT"))
                    w, landed = chunk(name)
                    pe.wait_ge(landed, chunk_count(g, name))
                    cw = CHUNKS[CHUNK[name]][3]
                    if cw != CW:
                        w = w.rearrange("p k n -> p (k n)")[:, 0:KD * cw].rearrange("p (k n) -> p k n", n=cw)
                    project(g, stage, w, actT[:, :, toks], KD, 0, cw)
                elif kind == "heads":
                    pe.wait_ge(dve_made, dve_count(g, ("A0", t, 0), "q"))
                    bank, free = bank_of(stage, 0)
                    pe.wait_ge(free, drain_count(g, stage, 0))
                    for p in range(4):
                        last = turn(bank[:, p * P:(p + 1) * P], qa[:, t, p * P:(p + 1) * P])
                    last.then_inc(filled, 1)
                    pe.wait_ge(dve_made, dve_count(g, ("A1", t, 0), "kv"))
                    bank, free = bank_of(stage, 1)
                    pe.wait_ge(free, drain_count(g, stage, 1))
                    turn(bank[:, 0:P], ka[:, t]).then_inc(filled, 1)
                elif kind == "score":
                    pe.wait_ge(act_made, act_count(g, ("heads", t, 0), "kT"))
                    if is_first(g) and t == 0:
                        pe.wait_ge(set_up, 4)
                    for i in range(4):
                        c, p0 = i // 2, 2 * (i % 2)
                        bank, free = bank_of(stage, i)
                        pe.wait_ge(free, drain_count(g, stage, i))
                        for j in range(2):
                            last = pe.matmul(bank[:, j * 256:(j + 1) * 256], hqT[c * 64:c * 64 + 64, p0 + j],
                                             kTa[c * 64:c * 64 + 64, t * P:(t + 2) * P], start=True, stop=True)
                        last.then_inc(filled, 1)
                elif kind == "turn":
                    pe.wait_ge(act_made, act_count(g, ("score", t, 0), "probs"))
                    for i in range(4):
                        bank, free = bank_of(stage, i)
                        pe.wait_ge(free, drain_count(g, stage, i))
                        for j in range(2):
                            for b in range(2):
                                last = turn(bank[:, (2 * j + b) * P:(2 * j + b + 1) * P],
                                            probs[:, 2 * i + j, b * P:(b + 1) * P])
                        last.then_inc(filled, 1)
                elif kind == "mix":
                    pe.wait_ge(act_made, act_count(g, ("turn", t, 0), "pT"))
                    bank, free = bank_of(stage)
                    pe.wait_ge(free, drain_count(g, stage))
                    for h in range(HEADS):
                        c = h // 4
                        for b in range(2):
                            last = pe.matmul(bank[:, h * 64:(h + 1) * 64], probsT[:, h, b],
                                             va[:, t + b, c * 64:(c + 1) * 64], start=(b == 0), stop=(b == 1))
                    last.then_inc(filled, 1)
                elif kind == "attT":
                    pe.wait_ge(dve_made, dve_count(g, ("mix", t, 0), "att"))
                    bank, free = bank_of(stage)
                    pe.wait_ge(free, drain_count(g, stage))
                    for k in range(4):
                        last = turn(bank[:, k * P:(k + 1) * P], att[:, k * P:(k + 1) * P])
                    last.then_inc(filled, 1)
                elif kind == "rheads":
                    for i, made in ((0, ("QR", "q")), (1, ("KR", "k"))):
                        pe.wait_ge(dve_made, dve_count(g, (made[0], t, 0), made[1]))
                        bank, free = bank_of(stage, i)
                        pe.wait_ge(free, drain_count(g, stage, i))
                        for p in range(4):
                            last = turn(bank[:, p * P:(p + 1) * P], qk_m[:, t, i * 512 + p * P:i * 512 + (p + 1) * P])
                        last.then_inc(filled, 1)
                elif kind == "rscore":
                    pe.wait_ge(act_made, act_count(g, ("rheads", t, 0), "kT"))
                    for c in range(2):
                        bank, free = bank_of(stage, c)
                        pe.wait_ge(free, drain_count(g, stage, c))
                        for p in range(4):
                            last = pe.matmul(bank[:, p * P:(p + 1) * P], rkT[c * 64:c * 64 + 64, p],
                                             hqT[c * 64:c * 64 + 64, p], start=True, stop=True)
                        last.then_inc(filled, 1)
                elif kind == "rmix":
                    pe.wait_ge(dve_made, dve_count(g, ("rscore", t, 0), "decayed"))
                    pe.wait_ge(act_made, act_count(g, ("V", t, 1), "v"))
                    if t:
                        pe.wait_ge(dve_made, dve_count(g, ("rmix", t - 1, 0), "state"))
                    else:
                        if not is_first(g):
                            pe.wait_ge(dve_made, (g - 1) * NDVE + DVE_AT[(("rmix", GT - 1, 0), "state")] + 1)
                    for c in range(2):
                        bank, free = bank_of(stage, c)
                        pe.wait_ge(free, drain_count(g, stage, c))
                        for p in range(4):
                            h = 2 * p + c
                            pe.matmul(bank[:, p * P:(p + 1) * P], decayed[:, c * 4 + p],
                                      v_r[:, t, h * RV:(h + 1) * RV], start=True, stop=False)
                            last = pe.matmul(bank[:, p * P:(p + 1) * P], rqwT[c * 64:c * 64 + 64, p],
                                             state[c * 64:c * 64 + 64, p], start=False, stop=True)
                        last.then_inc(filled, 1)
                    for i in range(2):
                        bank, free = bank_of(stage, 2 + i)
                        pe.wait_ge(free, drain_count(g, stage, 2 + i))
                        for j in range(2):
                            p = 2 * i + j
                            last = pe.matmul(bank[:, j * 256:(j + 1) * 256], kw[:, p * P:(p + 1) * P],
                                             v_r[:, t, p * 256:(p + 1) * 256], start=True, stop=True)
                        last.then_inc(filled, 1)
                elif kind in ("retT", "mT"):
                    if kind == "retT":
                        pe.wait_ge(dve_made, dve_count(g, stage, "gated"))
                        src = g_r[:, t]
                    else:
                        pe.wait_ge(dve_made, dve_count(g, ("WR", t, 1), "m"))
                        src = qk_m[:, t]
                    for i in range(2):
                        bank, free = bank_of(stage, i)
                        pe.wait_ge(free, drain_count(g, stage, i))
                        for j in range(4):
                            k = 4 * i + j
                            last = turn(bank[:, j * P:(j + 1) * P], src[:, k * P:(k + 1) * P])
                        last.then_inc(filled, 1)
                elif kind == "WA":
                    pe.wait_ge(act_made, act_count(g, ("attT", t, 0), "attT"))
                    w, landed = chunk("WA")
                    pe.wait_ge(landed, chunk_count(g, "WA"))
                    w = w.rearrange("p k n -> p (k n)").rearrange("p (k n) -> p k n", n=1024)
                    project(g, stage, w, attT[:, :, toks], 4, n * CW)
                elif kind == "WR":
                    pe.wait_ge(act_made, act_count(g, ("retT", t, 0), "retT"))
                    w, landed = chunk(f"WR{n}")
                    pe.wait_ge(landed, chunk_count(g, f"WR{n}"))
                    project(g, stage, w, retT[:, :, toks], KD)
                elif kind == "WO":
                    pe.wait_ge(act_made, act_count(g, ("mT", t, 0), "mT"))
                    w, landed = chunk(f"WO{n}")
                    pe.wait_ge(landed, chunk_count(g, f"WO{n}"))
                    project(g, stage, w, actT[:, :, toks], KD)
                elif kind == "query":
                    pe.wait_ge(act_made, act_count(g, ("norm2", GT - 1, 0), "hT"))
                    w, landed = chunk(f"WQ{n // 2}")
                    pe.wait_ge(landed, chunk_count(g, f"WQ{n // 2}"))
                    bank, free = bank_of(stage)
                    pe.wait_ge(free, drain_count(g, stage))
                    for half in range(2):
                        c0 = (n % 2) * 256 + half * P
                        for k in range(KD):
                            last = pe.matmul(bank[:, half * 256:(half + 1) * 256], w[:, k, c0:c0 + P], actT[:, k],
                                             start=(k == 0), stop=(k == KD - 1))
                    last.then_inc(filled, 1)
                elif kind == "keys":
                    pe.wait_ge(act_made, act_count(g, ("query", None, n), "qT"))
                    if is_first(g) and n == 0:
                        pe.wait_ge(keys_kept, 1)
                    bank, free = bank_of(stage)
                    pe.wait_ge(free, drain_count(g, stage))
                    for tt in range(GT):
                        for half in range(2):
                            i = 2 * tt + half
                            last = pe.matmul(bank[:, i * P:(i + 1) * P], pqT[:, half, tt * P:(tt + 1) * P],
                                             keyT[:, half], start=True, stop=True)
                    last.then_inc(filled, 1)

            def retrieve(g, h, q):
                if not h:
                    return
                h -= 1
                t = h // PH
                for k in range(QN * q, QN * q + QN):
                    if not v_on_pe(k):
                        continue
                    n = GATHER[("v", h, k)]
                    pes = USED[n][1]
                    pe.wait_ge(diag_made, g * NUSED_PE + pes)
                    pe.wait_ge(row_landed[n % RING], landed_in(g, n))
                    first = h % PH == 0 and k == 0
                    if first:
                        pe.wait_ge(acc_made, (g + 1) * NACC + ACC_READ[0] if t else g * NACC + ACC_READ[GT - 1])
                    final = h % PH == PH - 1 and k == max(s for s in range(TOPK) if v_on_pe(s))
                    for j in range(2):
                        last = pe.matmul(vsum[j][:, :], diag[:, (pes - 1) % 4], rows[:, n % RING, j * CW:(j + 1) * CW],
                                         start=first, stop=final)
                    last.then_inc(used_pe, 1)

            for free in drained:
                pe.sem_inc(free, 1)
            pe.sem_inc(used_pe, NUSED_PE)
            pe.wait_ge(consts_landed, 16 * 8)
            for half in range(2):
                last = turn(vsum[0][:, half * P:(half + 1) * P], key_raw[:, half])
            last.then_inc(keys_turned, 1)
            for stage in EARLY:
                front(0, stage)
            with pe.Fori(0, GROUPS - 1) as r:
                for n, (h, q) in enumerate(QUARTERS):
                    retrieve(r, h, q)
                    for stage in LATE_SHARE.get(n, ()):
                        front(r, stage)
                    for stage in EARLY_SHARE.get(n, ()):
                        front(r + 1, stage)
            for n, (h, q) in enumerate(QUARTERS):
                retrieve(GROUPS - 1, h, q)
                for stage in LATE_SHARE.get(n, ()):
                    front(GROUPS - 1, stage)

        @block.scalar
        def _(act):
            steps = [0]
            per_group = [None, 16]
            part_now = [0]

            def start_steps(which):
                steps[0], part_now[0] = 0, which

            def end_late():
                act.sem_inc(act_step[1], per_group[1] - steps[0])

            def step_sem():
                return act_step[part_now[0]]

            def next_step(g):
                steps[0] += 1
                return (0 if is_first(g) else g * per_group[part_now[0]]) + steps[0]

            def drain_to(g, stage, i, dst, func=ACT.Copy, view=None):
                act.wait_ge(filled, fill_count(g, stage, i))
                bank, free = bank_of(stage, i)
                src = bank[:, :] if view is None else view(bank)
                act.activation(dst, src, func).then_inc(step_sem(), 1)
                act.wait_ge(step_sem(), next_step(g))
                act.sem_inc(free, 1)

            def front(g, stage):
                kind, t, n = stage
                toks = slice(t * P, t * P + P) if t is not None else None
                if kind == "norm":
                    if is_first(g) and t == 0:
                        act.wait_ge(set_up, 4)
                    act.wait_ge(x_landed[t], g * 32 + 32)
                    if t:
                        act.wait_ge(filled, fill_count(g, ("norm", t - 1, 0), 1))
                    else:
                        if not is_first(g):
                            act.wait_ge(dve_made, (g - 1) * NDVE + DVE_AT[(("WR", GT - 1, 1), "m")] + 1)
                    act.activation(scratch[:], xh[:, t], ACT.Square, accum_out=col(SS + t)).then_inc(step_sem(), 1)
                    act.wait_ge(step_sem(), next_step(g))
                    act.activation(col(RMS + t), col(SS + t), ACT.Sqrt, bias=eps_t[:, 0:1],
                                   scale=1.0 / D).then_inc(act_made, 1)
                    act.wait_ge(dve_made, dve_count(g, stage, "rstd"))
                    act.activation(scratch[:], xh[:, t], ACT.Copy, scale=col(RSTD + t)).then_inc(act_made, 1)
                elif kind == "V":
                    if not is_first(g):
                        act.wait_ge(dve_made, (g - 1) * NDVE + NDVE)
                    drain_to(g, stage, 0, v_r[:, t, n * CW:(n + 1) * CW])
                    act.sem_inc(act_made, 1)
                elif kind == "G":
                    drain_to(g, stage, 0, g_r[:, t, n * CW:(n + 1) * CW], ACT.Silu)
                    act.sem_inc(act_made, 1)
                elif kind == "heads":
                    drain_to(g, stage, 0, ret_parts[:, 3])
                    act.sem_inc(act_made, 1)
                    drain_to(g, stage, 1, kTa[:, (t + 1) * P:(t + 2) * P], view=lambda b: b[:, 0:P])
                    act.sem_inc(act_made, 1)
                elif kind == "score":
                    act.wait_ge(dve_made, dve_count(g, stage, "masked"))
                    for h in range(HEADS):
                        ins = act.activation(probs[:, h], probs[:, h], ACT.Exp, bias=col(NM + h),
                                             accum_out=col(RSUM + h))
                    ins.then_inc(step_sem(), 1)
                    act.wait_ge(step_sem(), next_step(g))
                    act.activation(col(ESNK, HEADS), col(ESNK, HEADS), ACT.Exp).then_inc(act_made, 1)
                elif kind == "turn":
                    for i in range(4):
                        drain_to(g, stage, i, probsT[:, 2 * i:2 * i + 2].rearrange("p h b q -> p (h b q)"))
                    act.sem_inc(act_made, 1)
                elif kind == "attT":
                    drain_to(g, stage, 0, attT[:, :, toks], view=lambda b: b[:, :].rearrange("p (k q) -> p k q", k=4))
                    if t == GT - 1:
                        act.activation(kTa[:, 0:P], kTa[:, GT * P:(GT + 1) * P], ACT.Copy).then_inc(step_sem(), 1)
                        act.wait_ge(step_sem(), next_step(g))
                        act.activation(va[:, 0], va[:, GT], ACT.Copy).then_inc(step_sem(), 1)
                        act.wait_ge(step_sem(), next_step(g))
                    act.sem_inc(act_made, 1)
                elif kind == "rheads":
                    drain_to(g, stage, 0, ret_parts[:, 3])
                    act.sem_inc(act_made, 1)
                    drain_to(g, stage, 1, ret_parts[:, 0])
                    act.sem_inc(act_made, 1)
                elif kind == "rmix":
                    for c in range(2):
                        act.wait_ge(filled, fill_count(g, stage, c))
                        bank, _ = bank_of(stage, c)
                        if c == 0:
                            if t:
                                act.wait_ge(dve_made, dve_count(g, ("retT", t - 1, 0), "gated"))
                            else:
                                act.wait_ge(filled, fill_count(g, ("norm", GT - 1, 0), 1))
                        for p in range(4):
                            ins = act.activation(scratch[:, (c * 4 + p) * P:(c * 4 + p + 1) * P],
                                                 bank[:, p * P:(p + 1) * P], ACT.Square, accum_out=col(SSR + c * 4 + p))
                    ins.then_inc(step_sem(), 1)
                    act.wait_ge(step_sem(), next_step(g))
                    act.activation(col(RMSR, RH), col(SSR, RH), ACT.Sqrt, bias=eps_t[:, 0:1],
                                   scale=1.0 / RV).then_inc(act_made, 1)
                elif kind in ("retT", "mT"):
                    dst = retT if kind == "retT" else actT
                    for i in range(2):
                        drain_to(g, stage, i, dst[:, 4 * i:4 * i + 4, toks],
                                 view=lambda b: b[:, :].rearrange("p (k q) -> p k q", k=4))
                    act.sem_inc(act_made, 1)
                elif kind == "WA":
                    act.wait_ge(dve_made, dve_count(g, ("rheads", t, 0), "weighted"))
                    drain_to(g, stage, 0, qk_m[:, t, n * CW:(n + 1) * CW])
                    act.sem_inc(act_made, 1)
                elif kind in ("GA", "GR"):
                    if kind == "GR" or n:
                        act.wait_ge(dve_made, dve_count(g, ("GA", t, n - 1) if kind == "GA" else
                                 (("WR", t, n - 1) if n else ("GA", t, 1)), "m"))
                    drain_to(g, stage, 0, qa[:, t], ACT.Sigmoid)
                    act.sem_inc(act_made, 1)
                elif kind == "norm2":
                    act.wait_ge(dve_made, dve_count(g, ("WO", t, 1), "h"))
                    act.activation(scratch[:], xh[:, t], ACT.Square, accum_out=col(SS + t)).then_inc(step_sem(), 1)
                    act.wait_ge(step_sem(), next_step(g))
                    act.activation(col(RMS + t), col(SS + t), ACT.Sqrt, bias=eps_t[:, 0:1],
                                   scale=1.0 / D).then_inc(act_made, 1)
                    for i in range(2):
                        drain_to(g, stage, i, actT[:, 4 * i:4 * i + 4, toks],
                                 view=lambda b: b[:, :].rearrange("p (k q) -> p k q", k=4))
                    act.sem_inc(act_made, 1)
                elif kind == "query":
                    if n:
                        act.wait_ge(filled, fill_count(g, ("keys", None, n - 1)))
                    drain_to(g, stage, 0, pqT[:, :, :].rearrange("p a b -> p (a b)"))
                    act.sem_inc(act_made, 1)
                elif kind == "keys":
                    drain_to(g, stage, 0, scores[:, :, 2 * n:2 * n + 2, :],
                             view=lambda b: b[:, :].rearrange("p (t s k) -> p t s k", t=GT, s=2))
                    act.sem_inc(act_made, 1)
                elif kind == "pick":
                    act.wait_ge(dve_made, dve_count(g, stage, "picks"))
                    act.activation(expg[:], expg[:], ACT.Exp).then_inc(act_made, 1)

            def retrieve(g, h, q):
                if h and q == 0:
                    hp = h - 1
                    t, s0 = hp // PH, (hp % PH) * TOPK
                    n = GATHER[("u", hp, TOPK - 1)]
                    act.wait_ge(used_dve, (g + 1) * NUSED_DVE + USED[n][0])
                    act.activation(dots[:, t, s0:s0 + TOPK], dots[:, t, s0:s0 + TOPK], ACT.Gelu).then_inc(gelu_made, 1)
                if h:
                    hp = h - 1
                    t, s0 = hp // PH, (hp % PH) * TOPK
                    for k in range(QN * q, QN * q + QN):
                        if not v_on_pe(k):
                            continue
                        n = GATHER[("v", hp, k)]
                        pes = USED[n][1]
                        act.wait_ge(coef_made, g * NH2 + hp + 1)
                        act.wait_ge(used_pe, (g + 1) * NUSED_PE + pes - 4)
                        act.activation(diag[:, (pes - 1) % 4], ident, ACT.Copy,
                                       scale=coef[:, t, s0 + k:s0 + k + 1]).then_inc(diag_made, 1)
                    if hp % PH == PH - 1 and q == TOPK // QN - 1:
                        act.wait_ge(acc_made, (g + 1) * NACC + t * PER_TILE + 3)
                        act.activation(vacc[:], h_cur[:, t], ACT.Square, accum_out=col(FSS)).then_inc(fin_rms, 1)
                        act.wait_ge(fin_rms, g * (2 * GT) + 2 * t + 1)
                        act.activation(col(FRMS), col(FSS), ACT.Sqrt, bias=eps_t[:, 0:1],
                                       scale=1.0 / D).then_inc(fin_rms, 1)
                        act.wait_ge(out_made, g * GT + t + 1)
                        act.dma_start(out[bass.ds(g * (GT * P) + t * P, P), :], h_cur[:, t]).then_inc(out_stored[t], 16)

            def hand_over(g, t):
                if not is_first(g):
                    act.wait_ge(out_stored[t], g * 16)
                act.wait_ge(dve_made, dve_count(g, ("WO", t, 1), "h"))
                act.activation(h_cur[:, t], xh[:, t], ACT.Copy).then_inc(handed_act, 1)

            act.wait_ge(keys_turned, 1)
            act.activation(keyT[:, :, :].rearrange("p a b -> p (a b)"), vsum[0][:, 0:2 * P], ACT.Copy).then_inc(keys_kept, 1)
            start_steps(0)
            for stage in EARLY:
                front(0, stage)
            per_group[0] = steps[0]
            hand_over(0, 0)
            with act.Fori(0, GROUPS - 1) as r:
                start_steps(1)
                for n, (h, q) in enumerate(QUARTERS):
                    if n == HAND_0:
                        assert steps[0] == per_group[0]
                        hand_over(r + 1, 0)
                    retrieve(r, h, q)
                    if n == HAND_1:
                        hand_over(r, 1)
                    for stage in LATE_SHARE.get(n, ()):
                        front(r, stage)
                    if n == LATE_TO - 1:
                        end_late()
                        start_steps(0)
                    for stage in EARLY_SHARE.get(n, ()):
                        front(r + 1, stage)
            start_steps(1)
            for n, (h, q) in enumerate(QUARTERS):
                retrieve(GROUPS - 1, h, q)
                if n == HAND_1:
                    hand_over(GROUPS - 1, 1)
                for stage in LATE_SHARE.get(n, ()):
                    front(GROUPS - 1, stage)
            for t in range(GT):
                act.wait_ge(out_stored[t], 16 * GROUPS)

        @block.vector
        def _(dve):
            steps = [0]
            per_group = [None, 160]
            part_now = [0]

            def start_steps(which):
                steps[0], part_now[0] = 0, which

            def end_late():
                dve.sem_inc(dve_step[1], per_group[1] - steps[0])

            def step_sem():
                return dve_step[part_now[0]]

            def next_step(g):
                steps[0] += 1
                return (0 if is_first(g) else g * per_group[part_now[0]]) + steps[0]

            def sixteen_largest(g, jobs):
                for step in range(5):
                    for values, top, place in jobs:
                        if step == 0:
                            ins = dve.max(top[:, 0:8], values)
                        elif step == 1:
                            ins = dve.max_index(place[:, 0:8], top[:, 0:8], values)
                        elif step == 2:
                            ins = dve.match_replace(values, top[:, 0:8], values, LOWEST)
                        elif step == 3:
                            ins = dve.max(top[:, 8:16], values)
                        else:
                            ins = dve.max_index(place[:, 8:16], top[:, 8:16], values)
                    ins.then_inc(step_sem(), 1)
                    dve.wait_ge(step_sem(), next_step(g))
                    if step < 4:
                        dve.sem_inc(passed, 1)

            def rotate(g, bank, free, dst, src, cos, sin, tmp, rest=None):
                w = src.shape[-1] // 2
                lo, hi = (slice(None),) * (len(src.shape) - 1) + (slice(0, w),), \
                    (slice(None),) * (len(src.shape) - 1) + (slice(w, 2 * w),)
                dve.tensor_tensor(tmp[lo], src[hi], sin[lo], ALU.mult)
                dve.tensor_tensor(tmp[hi], src[lo], sin[hi], ALU.mult)
                if rest is not None:
                    dve.tensor_copy(*rest)
                dve.tensor_tensor(dst, src, cos, ALU.mult).then_inc(step_sem(), 1)
                dve.wait_ge(step_sem(), next_step(g))
                dve.tensor_tensor(dst, dst, tmp, ALU.add).then_inc(step_sem(), 1)
                dve.wait_ge(step_sem(), next_step(g))
                dve.sem_inc(free, 1)

            def front(g, stage):
                kind, t, n = stage
                toks = slice(t * P, t * P + P) if t is not None else None
                if kind == "norm":
                    dve.wait_ge(act_made, act_count(g, stage, "rms"))
                    dve.reciprocal(col(RSTD + t), col(RMS + t)).then_inc(dve_made, 1)
                    if t == 0:
                        if not is_first(g):
                            dve.wait_ge(filled, (g - 1) * NFILL + FILL[(("query", None, PH - 1), 0)] + 1)
                    for i in range(2):
                        dve.wait_ge(filled, fill_count(g, stage, i))
                        bank, free = bank_of(stage, i)
                        gain = gain_mix[:, 4 * i:4 * i + 4].unsqueeze(2).to_broadcast([P, 4, P])
                        dve.tensor_tensor(actT[:, 4 * i:4 * i + 4, toks],
                                                 bank[:, :].rearrange("p (k q) -> p k q", k=4), gain, ALU.mult).then_inc(step_sem(), 1)
                        dve.wait_ge(step_sem(), next_step(g))
                        dve.sem_inc(free, 1)
                    dve.sem_inc(dve_made, 1)
                elif kind == "A0":
                    dve.wait_ge(filled, fill_count(g, stage))
                    bank, free = bank_of(stage)
                    src = bank[:, :].rearrange("p (c h d) -> p c h d", c=2, h=4)
                    dst = qa[:, t].rearrange("p (h c d) -> p c h d", c=2, h=4)
                    cos = rot[:, t, 128:144]
                    sin = rot[:, t, 144:160]
                    for c in range(2):
                        tmp = att[:, c * 64:c * 64 + 64].rearrange("p (h d) -> p h d", h=4)
                        cs = cos.unsqueeze(1).to_broadcast([P, 4, ROT_A])
                        sn = sin.unsqueeze(1).to_broadcast([P, 4, ROT_A])
                        s = src[:, c]
                        o = dst[:, c]
                        dve.tensor_tensor(tmp[:, :, 0:8], s[:, :, 8:16], sn[:, :, 0:8], ALU.mult)
                        dve.tensor_tensor(tmp[:, :, 8:16], s[:, :, 0:8], sn[:, :, 8:16], ALU.mult)
                        dve.tensor_copy(o[:, :, 16:64], s[:, :, 16:64])
                        dve.tensor_tensor(o[:, :, 0:16], s[:, :, 0:16], cs, ALU.mult).then_inc(step_sem(), 1)
                        dve.wait_ge(step_sem(), next_step(g))
                        dve.tensor_tensor(o[:, :, 0:16], o[:, :, 0:16], tmp, ALU.add).then_inc(step_sem(), 1)
                        dve.wait_ge(step_sem(), next_step(g))
                    dve.sem_inc(free, 1)
                    dve.sem_inc(dve_made, 1)
                elif kind == "A1":
                    dve.wait_ge(filled, fill_count(g, stage))
                    bank, free = bank_of(stage)
                    s = bank[:, 0:P].rearrange("p (h d) -> p h d", h=KVH)
                    o = ka[:, t].rearrange("p (h d) -> p h d", h=KVH)
                    tmp = att[:, 0:32].rearrange("p (h d) -> p h d", h=KVH)
                    cs = rot[:, t, 128:144].unsqueeze(1).to_broadcast([P, KVH, ROT_A])
                    sn = rot[:, t, 144:160].unsqueeze(1).to_broadcast([P, KVH, ROT_A])
                    dve.tensor_tensor(tmp[:, :, 0:8], s[:, :, 8:16], sn[:, :, 0:8], ALU.mult)
                    dve.tensor_tensor(tmp[:, :, 8:16], s[:, :, 0:8], sn[:, :, 8:16], ALU.mult)
                    dve.tensor_copy(o[:, :, 16:64], s[:, :, 16:64])
                    if t == 0:
                        if not is_first(g):
                            dve.wait_ge(act_made, (g - 1) * NACT + ACT_AT[(("attT", GT - 1, 0), "attT")] + 1)
                    dve.tensor_copy(va[:, t + 1], bank[:, P:2 * P])
                    dve.tensor_tensor(o[:, :, 0:16], s[:, :, 0:16], cs, ALU.mult).then_inc(step_sem(), 1)
                    dve.wait_ge(step_sem(), next_step(g))
                    dve.tensor_tensor(o[:, :, 0:16], o[:, :, 0:16], tmp, ALU.add).then_inc(step_sem(), 1)
                    dve.wait_ge(step_sem(), next_step(g))
                    dve.sem_inc(free, 1)
                    dve.sem_inc(dve_made, 1)
                elif kind in ("QR", "KR"):
                    dve.wait_ge(filled, fill_count(g, stage))
                    bank, free = bank_of(stage)
                    c0 = 0 if kind == "QR" else 512
                    s = bank[:, :].rearrange("p (h d) -> p h d", h=RH)
                    o = qk_m[:, t, c0:c0 + 512].rearrange("p (h d) -> p h d", h=RH)
                    tmp = att[:, :].rearrange("p (h d) -> p h d", h=RH)
                    if kind == "QR" and t == 0:
                        if not is_first(g):
                            dve.wait_ge(filled, (g - 1) * NFILL + FILL[(("mT", GT - 1, 0), 1)] + 1)
                    cs = rot[:, t, 0:64].unsqueeze(1).to_broadcast([P, RH, ROT_R])
                    sn = rot[:, t, 64:128].unsqueeze(1).to_broadcast([P, RH, ROT_R])
                    dve.tensor_tensor(tmp[:, :, 0:32], s[:, :, 32:64], sn[:, :, 0:32], ALU.mult)
                    dve.tensor_tensor(tmp[:, :, 32:64], s[:, :, 0:32], sn[:, :, 32:64], ALU.mult)
                    dve.tensor_tensor(o, s, cs, ALU.mult).then_inc(step_sem(), 1)
                    dve.wait_ge(step_sem(), next_step(g))
                    dve.tensor_tensor(o, o, tmp, ALU.add).then_inc(step_sem(), 1)
                    dve.wait_ge(step_sem(), next_step(g))
                    dve.sem_inc(free, 1)
                    dve.sem_inc(dve_made, 1)
                elif kind == "score":
                    mask = mask_first if is_first(g) and t == 0 else const[:, C_MASK:C_MASK + 256]
                    for i in range(4):
                        dve.wait_ge(filled, fill_count(g, stage, i))
                        bank, free = bank_of(stage, i)
                        dve.scalar_tensor_tensor(
                            out=probs[:, 2 * i:2 * i + 2], in0=bank[:, :].rearrange("p (h k) -> p h k", h=2),
                            scalar=HD ** -0.5, in1=mask.unsqueeze(1).to_broadcast([P, 2, 2 * P]),
                            op0=ALU.mult, op1=ALU.add).then_inc(step_sem(), 1)
                        dve.wait_ge(step_sem(), next_step(g))
                        dve.sem_inc(free, 1)
                    dve.tensor_reduce(col(MX, HEADS), probs[:], AX.X, ALU.max).then_inc(step_sem(), 1)
                    dve.wait_ge(step_sem(), next_step(g))
                    dve.tensor_tensor(col(MX, HEADS), col(MX, HEADS), sinks[:], ALU.max).then_inc(step_sem(), 1)
                    dve.wait_ge(step_sem(), next_step(g))
                    dve.tensor_tensor(col(ESNK, HEADS), sinks[:], col(MX, HEADS), ALU.subtract)
                    dve.tensor_scalar(col(NM, HEADS), col(MX, HEADS), -1.0, None, ALU.mult).then_inc(step_sem(), 1)
                    dve.wait_ge(step_sem(), next_step(g))
                    dve.sem_inc(dve_made, 1)
                elif kind == "mix":
                    dve.wait_ge(act_made, act_count(g, ("score", t, 0), "probs"))
                    dve.tensor_tensor(col(DEN, HEADS), col(RSUM, HEADS), col(ESNK, HEADS), ALU.add).then_inc(step_sem(), 1)
                    dve.wait_ge(step_sem(), next_step(g))
                    dve.reciprocal(col(DEN, HEADS), col(DEN, HEADS)).then_inc(step_sem(), 1)
                    dve.wait_ge(step_sem(), next_step(g))
                    dve.wait_ge(filled, fill_count(g, stage))
                    bank, free = bank_of(stage)
                    dve.tensor_tensor(att[:, :].rearrange("p (h d) -> p h d", h=HEADS),
                                             bank[:, :].rearrange("p (h d) -> p h d", h=HEADS),
                                             col(DEN, HEADS).unsqueeze(2).to_broadcast([P, HEADS, HD]), ALU.mult).then_inc(step_sem(), 1)
                    dve.wait_ge(step_sem(), next_step(g))
                    dve.sem_inc(free, 1)
                    dve.sem_inc(dve_made, 1)
                elif kind == "rheads":
                    dve.wait_ge(act_made, act_count(g, stage, "qT"))
                    if t:
                        dve.wait_ge(filled, fill_count(g, ("rmix", t - 1, 0), 3))
                    dve.tensor_tensor(rqwT, hqT, const[:, C_WQ:C_WQ + 512].rearrange("p (a b) -> p a b", a=4),
                                      ALU.mult)
                    dve.tensor_tensor(kw.rearrange("p (h d) -> p h d", h=RH),
                                             qk_m[:, t, 512:1024].rearrange("p (h d) -> p h d", h=RH),
                                             const[:, C_WK:C_WK + RH].unsqueeze(2).to_broadcast([P, RH, RQ]), ALU.mult).then_inc(step_sem(), 1)
                    dve.wait_ge(step_sem(), next_step(g))
                    dve.sem_inc(dve_made, 1)
                elif kind == "rscore":
                    for c in range(2):
                        dve.wait_ge(filled, fill_count(g, stage, c))
                        bank, free = bank_of(stage, c)
                        dve.tensor_tensor(decayed[:, 4 * c:4 * c + 4],
                                                 bank[:, :].rearrange("p (a b) -> p a b", a=4),
                                                 const[:, C_DECAY + c * 512:C_DECAY + (c + 1) * 512].rearrange(
                                                     "p (a b) -> p a b", a=4), ALU.mult).then_inc(step_sem(), 1)
                        dve.wait_ge(step_sem(), next_step(g))
                        dve.sem_inc(free, 1)
                    dve.sem_inc(dve_made, 1)
                elif kind == "rmix":
                    dve.wait_ge(act_made, act_count(g, stage, "rms"))
                    dve.reciprocal(col(RINV, RH), col(RMSR, RH)).then_inc(step_sem(), 1)
                    dve.wait_ge(step_sem(), next_step(g))
                    for c in range(2):
                        dve.wait_ge(filled, fill_count(g, stage, c))
                        bank, free = bank_of(stage, c)
                        dve.tensor_tensor(
                            scratch[:, c * 512:(c + 1) * 512].rearrange("p (a b) -> p a b", a=4),
                            bank[:, :].rearrange("p (a b) -> p a b", a=4),
                            col(RINV + 4 * c, 4).unsqueeze(2).to_broadcast([P, 4, RV]), ALU.mult).then_inc(step_sem(), 1)
                        dve.wait_ge(step_sem(), next_step(g))
                        dve.sem_inc(free, 1)
                    dve.sem_inc(dve_made, 1)
                    dve.tensor_tensor(state[:], state[:],
                                             const[:, C_SD:C_SD + 4].unsqueeze(2).to_broadcast([P, 4, RV]), ALU.mult).then_inc(step_sem(), 1)
                    dve.wait_ge(step_sem(), next_step(g))
                    for i in range(2):
                        dve.wait_ge(filled, fill_count(g, stage, 2 + i))
                        bank, free = bank_of(stage, 2 + i)
                        for c in range(2):
                            rows_c = slice(64 * c, 64 * c + 64)
                            src = bank[rows_c, :].rearrange("p (a b) -> p a b", a=2)[:, :, c * RV:(c + 1) * RV]
                            ins = dve.tensor_tensor(state[rows_c, 2 * i:2 * i + 2], state[rows_c, 2 * i:2 * i + 2],
                                                    src, ALU.add)
                        ins.then_inc(step_sem(), 1)
                        dve.wait_ge(step_sem(), next_step(g))
                        dve.sem_inc(free, 1)
                    dve.sem_inc(dve_made, 1)
                elif kind == "retT":
                    dve.wait_ge(act_made, act_count(g, ("G", t, 1), "silu"))
                    gv = g_r[:, t].rearrange("p (a c d) -> p c a d", a=4, c=2)
                    for c in range(2):
                        ins = dve.tensor_tensor(gv[:, c], scratch[:, c * 512:(c + 1) * 512].rearrange(
                            "p (a d) -> p a d", a=4), gv[:, c], ALU.mult)
                    ins.then_inc(dve_made, 1)
                elif kind == "GA":
                    dve.wait_ge(act_made, act_count(g, stage, "sig"))
                    dve.wait_ge(act_made, act_count(g, ("WA", t, n), "m"))
                    m = qk_m[:, t, n * CW:(n + 1) * CW]
                    dve.tensor_tensor(m, m, qa[:, t], ALU.mult).then_inc(dve_made, 1)
                elif kind == "WR":
                    dve.wait_ge(act_made, act_count(g, ("GR", t, n), "sig"))
                    dve.wait_ge(filled, fill_count(g, stage))
                    bank, free = bank_of(stage)
                    dve.tensor_tensor(qa[:, t], bank[:, :], qa[:, t], ALU.mult).then_inc(step_sem(), 1)
                    dve.wait_ge(step_sem(), next_step(g))
                    dve.sem_inc(free, 1)
                    m = qk_m[:, t, n * CW:(n + 1) * CW]
                    dve.wait_ge(dve_made, g * NDVE + DVE_AT[(("GA", t, n), "m")] + 1)
                    dve.tensor_tensor(m, m, qa[:, t], ALU.add).then_inc(dve_made, 1)
                elif kind == "WO":
                    dve.wait_ge(filled, fill_count(g, stage))
                    bank, free = bank_of(stage)
                    hcol = xh[:, t, n * CW:(n + 1) * CW]
                    dve.tensor_tensor(hcol, bank[:, :], hcol, ALU.add).then_inc(step_sem(), 1)
                    dve.wait_ge(step_sem(), next_step(g))
                    dve.sem_inc(free, 1)
                    dve.sem_inc(dve_made, 1)
                elif kind == "norm2":
                    dve.wait_ge(act_made, act_count(g, stage, "rms"))
                    dve.reciprocal(col(RSTD + t), col(RMS + t)).then_inc(step_sem(), 1)
                    dve.wait_ge(step_sem(), next_step(g))
                    dve.sem_inc(dve_made, 1)
                    if t == 0:
                        dve.wait_ge(filled, fill_count(g, ("WR", GT - 1, 1)))
                    dve.scalar_tensor_tensor(out=hn[:, t], in0=xh[:, t], scalar=col(RSTD + t), in1=gain_ffn[:],
                                             op0=ALU.mult, op1=ALU.mult).then_inc(dve_made, 1)
                elif kind == "top":
                    dve.wait_ge(act_made, g * NACT + ACT_AT[(("keys", None, n), "scores")] + 1)
                    dve.sem_inc(passed, 1)
                    sixteen_largest(g, [(scores[:, tt, 2 * n + half], top_v[:, tt, half], top_i[:, tt, half])
                                        for tt in range(GT) for half in range(2)])
                    dve.sem_inc(dve_made, 1)
                elif kind == "pick":
                    for tt in range(GT):
                        ins = dve.tensor_tensor(cands[:, tt, n].rearrange("p (a b) -> p a b", a=TOPK),
                                                top_v[:, tt, 0].unsqueeze(2).to_broadcast([P, TOPK, TOPK]),
                                                top_v[:, tt, 1].unsqueeze(1).to_broadcast([P, TOPK, TOPK]), ALU.add)
                    ins.then_inc(step_sem(), 1)
                    dve.wait_ge(step_sem(), next_step(g))
                    dve.sem_inc(passed, 1)
                    sixteen_largest(g, [(cands[:, tt, n], pick_v[:, tt], pick_i[:, tt]) for tt in range(GT)])
                    dve.tensor_tensor(expg[:], pick_v[:], pick_v[:, :, 0:1].to_broadcast([P, GT, TOPK]),
                                             ALU.subtract).then_inc(step_sem(), 1)
                    dve.wait_ge(step_sem(), next_step(g))
                    dve.sem_inc(dve_made, 1)
                elif kind == "index":
                    both = GT * TOPK
                    slots = slice(n * TOPK, (n + 1) * TOPK)
                    if n < EARLY_HEADS:
                        index, gate = index_next, gate_next
                    else:
                        index, gate = index_cur, gate_cur
                        dve.wait_ge(used_pe, (g + 1) * NUSED_PE)
                    dve.tensor_scalar(part[:, 0], pick_i[:], 4, None, ALU.logical_shift_right)
                    dve.tensor_scalar(part[:, 1], pick_i[:], 15, None, ALU.bitwise_and)
                    dve.tensor_copy(top_if[:, :, :, :].rearrange("p w t j -> p t w j"), top_i[:]).then_inc(step_sem(), 1)
                    dve.wait_ge(step_sem(), next_step(g))
                    hot = probs[:, 0:4].rearrange("p a b -> p (a b)")
                    hot_s = hot.rearrange("p (s j) -> p s j", j=TOPK)
                    hot_wt = hot.rearrange("p (w s j) -> p w s j", w=2 * GT, j=TOPK)
                    dve.tensor_tensor(
                        hot_s, part[:, :, :, :].rearrange("p w t s -> p (w t s)").unsqueeze(2).to_broadcast(
                            [P, 2 * both, TOPK]),
                        const[:, C_IOTA:C_IOTA + 16].unsqueeze(1).to_broadcast([P, 2 * both, TOPK]), ALU.is_equal).then_inc(step_sem(), 1)
                    dve.wait_ge(step_sem(), next_step(g))
                    dve.tensor_tensor(
                        hot_wt, hot_wt, top_if[:, :, :, :].rearrange("p w t j -> p (w t) j").unsqueeze(2).to_broadcast(
                            [P, 2 * GT, TOPK, TOPK]), ALU.mult).then_inc(step_sem(), 1)
                    dve.wait_ge(step_sem(), next_step(g))
                    dve.tensor_reduce(sel[:, :, :, :].rearrange("p w t s -> p (w t s)"), hot_s, AX.X, ALU.add).then_inc(step_sem(), 1)
                    dve.wait_ge(step_sem(), next_step(g))
                    dve.scalar_tensor_tensor(out=index[:, :, slots], in0=sel[:, 0], scalar=float(NKEY), in1=sel[:, 1],
                                             op0=ALU.mult, op1=ALU.add)
                    dve.wait_ge(act_made, act_count(g, ("pick", None, n), "exp"))
                    dve.tensor_reduce(col(GSUM, GT), expg[:], AX.X, ALU.add).then_inc(step_sem(), 1)
                    dve.wait_ge(step_sem(), next_step(g))
                    dve.reciprocal(col(GINV, GT), col(GSUM, GT)).then_inc(step_sem(), 1)
                    dve.wait_ge(step_sem(), next_step(g))
                    dve.tensor_tensor(gate[:, :, slots], expg[:],
                                             col(GINV, GT).unsqueeze(2).to_broadcast([P, GT, TOPK]), ALU.mult).then_inc(step_sem(), 1)
                    dve.wait_ge(step_sem(), next_step(g))
                    dve.sem_inc(dve_made, 1)

            def retrieve(g, h, q):
                for k in range(QN * q, QN * q + QN):
                    if h < NH2:
                        n = GATHER[("u", h, k)]
                        t, slot = h // PH, (h % PH) * TOPK + k
                        dve.wait_ge(row_landed[n % RING], landed_in(g, n))
                        dve.tensor_tensor_reduce(out=rows[:, n % RING], in0=rows[:, n % RING], in1=hn_cur[:, t],
                                                 scale=1.0, scalar=0.0, op0=ALU.mult, op1=ALU.add,
                                                 accum_out=dots[:, t, slot:slot + 1]).then_inc(used_dve, 1)
                    if not h:
                        continue
                    hp = h - 1
                    t, s0 = hp // PH, (hp % PH) * TOPK
                    if k == 0:
                        dve.wait_ge(gelu_made, g * NH2 + hp + 1)
                        dve.tensor_tensor(coef[:, t, s0:s0 + TOPK], dots[:, t, s0:s0 + TOPK],
                                          gate_cur[:, t, s0:s0 + TOPK], ALU.mult).then_inc(coef_made, 1)
                    if v_on_pe(k):
                        continue
                    n = GATHER[("v", hp, k)]
                    mine = [s for s in range(TOPK) if not v_on_pe(s)]
                    number = (hp % PH) * len(mine) + mine.index(k)
                    dve.wait_ge(row_landed[n % RING], landed_in(g, n))
                    c = coef[:, t, s0 + k:s0 + k + 1]
                    if number == 0:
                        dve.wait_ge(coef_made, g * NH2 + hp + 1)
                        ins = dve.tensor_scalar(vacc[:], rows[:, n % RING], c, None, ALU.mult)
                    else:
                        prev = GATHER[("v", hp - (mine.index(k) == 0), mine[mine.index(k) - 1])]
                        dve.wait_ge(used_dve, (g + 1) * NUSED_DVE + USED[prev][0])
                        if number % len(mine) == 0:
                            dve.wait_ge(coef_made, g * NH2 + hp + 1)
                        ins = dve.scalar_tensor_tensor(out=vacc[:], in0=rows[:, n % RING], scalar=c, in1=vacc[:],
                                                       op0=ALU.mult, op1=ALU.add)
                    ins.then_inc(used_dve, 1)
                if h and (h - 1) % PH == PH - 1 and q == TOPK // QN - 1:
                    t = (h - 1) // PH
                    base = (g + 1) * NACC + t * PER_TILE
                    dve.wait_ge(used_dve, (g + 1) * NUSED_DVE + USED[n][0])
                    pes = USED[GATHER[("v", h - 1, max(s for s in range(TOPK) if v_on_pe(s)))]][1]
                    dve.wait_ge(used_pe, (g + 1) * NUSED_PE + pes)
                    dve.tensor_tensor(vacc[:, 0:CW], vacc[:, 0:CW], vsum[0][:, :], ALU.add).then_inc(acc_made, 1)
                    dve.tensor_tensor(vacc[:, CW:D], vacc[:, CW:D], vsum[1][:, :], ALU.add).then_inc(acc_made, 1)
                    dve.wait_ge(acc_made, base + 2)
                    dve.wait_ge(handed_act, g * GT + GT)
                    dve.tensor_tensor(h_cur[:, t], h_cur[:, t], vacc[:], ALU.add).then_inc(acc_made, 1)
                    dve.wait_ge(fin_rms, g * (2 * GT) + 2 * t + 2)
                    dve.reciprocal(col(FRSTD), col(FRMS)).then_inc(acc_made, 1)
                    dve.wait_ge(acc_made, base + 4)
                    dve.scalar_tensor_tensor(out=h_cur[:, t], in0=h_cur[:, t], scalar=col(FRSTD), in1=gain_fin[:],
                                             op0=ALU.mult, op1=ALU.mult).then_inc(out_made, 1)

            def hand_over(g, t):
                early = slice(0, EARLY_HEADS * TOPK)
                last = GATHER[("v", (t + 1) * PH - 1, TOPK - 1)]
                last_pe = GATHER[("v", (t + 1) * PH - 1, max(k for k in range(TOPK) if v_on_pe(k)))]
                if not is_first(g):
                    dve.wait_ge(used_pe, g * NUSED_PE + USED[last_pe][1])
                if not is_first(g):
                    dve.wait_ge(used_dve, g * NUSED_DVE + USED[last][0])
                dve.wait_ge(dve_made, g * NDVE + DVE_AT[(("index", None, EARLY_HEADS - 1), "index")] + 1)
                dve.tensor_copy(index_cur[:, t, early], index_next[:, t])
                dve.tensor_copy(gate_cur[:, t, early], gate_next[:, t])
                dve.tensor_copy(hn_cur[:, t], hn[:, t]).then_inc(handed_dve, 1)
                dve.wait_ge(handed_dve, g * GT + t + 1)

            dve.sem_inc(used_dve, NUSED_DVE)
            dve.sem_inc(acc_made, NACC)
            dve.wait_ge(consts_landed, 16 * 8)
            dve.wait_ge(set_up, 4)
            start_steps(0)
            for stage in EARLY:
                front(0, stage)
            per_group[0] = steps[0]
            hand_over(0, 0)
            with dve.Fori(0, GROUPS - 1) as r:
                start_steps(1)
                for n, (h, q) in enumerate(QUARTERS):
                    if n == HAND_0:
                        assert steps[0] == per_group[0]
                        hand_over(r + 1, 0)
                    retrieve(r, h, q)
                    if n == HAND_1:
                        hand_over(r, 1)
                    for stage in LATE_SHARE.get(n, ()):
                        front(r, stage)
                    if n == LATE_TO - 1:
                        end_late()
                        start_steps(0)
                    for stage in EARLY_SHARE.get(n, ()):
                        front(r + 1, stage)
            start_steps(1)
            for n, (h, q) in enumerate(QUARTERS):
                retrieve(GROUPS - 1, h, q)
                if n == HAND_1:
                    hand_over(GROUPS - 1, 1)
                for stage in LATE_SHARE.get(n, ()):
                    front(GROUPS - 1, stage)


_INS = ["x", "norm_mix", "w_in", "att_sinks", "w_att_branch", "w_ret_branch", "w_out", "norm_ffn", "peer_w_query",
        "peer_sub_keys_1", "peer_sub_keys_2", "peer_u", "peer_v", "norm_final"]


def kernel(**inputs):
    import numpy as _np
    import concourse.bacc as _bacc
    from concourse import mybir as _mybir
    from concourse.bass_utils import run_bass_kernel_spmd as _run

    nc = _bacc.Bacc("TRN2", target_bir_lowering=False, num_devices=1)
    arrays, aps = {}, {}
    for name in _INS:
        a = _np.ascontiguousarray(inputs[name])
        if a.ndim == 3:
            a = a[0]
        arrays[f"in_{name}"] = a
        aps[name] = nc.dram_tensor(f"in_{name}", a.shape, _mybir.dt.from_np(a.dtype), kind="ExternalInput").ap()
    const_table, rot_table, mask_table = shape_constants()
    for name, a in (("const_table", const_table), ("rot_table", rot_table), ("mask_table", mask_table)):
        arrays[f"in_{name}"] = a
        aps[name] = nc.dram_tensor(f"in_{name}", a.shape, _mybir.dt.from_np(a.dtype), kind="ExternalInput").ap()
    out = nc.dram_tensor("out_0", (SEQ, D), _mybir.dt.float32, kind="ExternalOutput").ap()
    build_block(nc, *[aps[n] for n in _INS], aps["const_table"], aps["rot_table"], aps["mask_table"], out)
    r = _run(nc, [arrays], core_ids=[0])
    return r.results[0]["out_0"].reshape(1, SEQ, D)
```

```python
from contextlib import ExitStack

import numpy as np

import concourse.bass as bass
from concourse import mybir

ALU = mybir.AluOpType
ACT = mybir.ActivationFunctionType
AX = mybir.AxisListType
F32 = mybir.dt.float32
U32 = mybir.dt.uint32

P = 128
SEQ, D = 1024, 1024
KD = D // P
GT = 2
GROUPS = SEQ // (P * GT)
HEADS, HD, KVH = 8, 64, 2
RH, RQ, RV = 8, 64, 128
PH, NKEY, TOPK = 8, 128, 16
SLOTS = PH * TOPK
EPS = 1e-6
CW = 512
NEG = -1.0e30
LOWEST = -3.0e38

CHUNKS = [("A0", "in", 0, 512), ("A1", "in", 512, 256), ("QR", "in", 768, 512), ("KR", "in", 1280, 512),
          ("V0", "in", 1792, 512), ("V1", "in", 2304, 512), ("G0", "in", 2816, 512), ("G1", "in", 3328, 512),
          ("WA", "att", 0, 1024), ("GA0", "in", 3840, 512), ("GA1", "in", 4352, 512),
          ("GR0", "in", 4864, 512), ("WR0", "ret", 0, 512), ("GR1", "in", 5376, 512), ("WR1", "ret", 512, 512),
          ("WO0", "out", 0, 512), ("WO1", "out", 512, 512),
          ("WQ0", "query", 0, 512), ("WQ1", "query", 512, 512), ("WQ2", "query", 1024, 512), ("WQ3", "query", 1536, 512)]
CHUNK = {c[0]: n for n, c in enumerate(CHUNKS)}
WBUFS = 2

EARLY_HEADS = 1
EARLY = (
    [("norm", 0, 0), ("norm", 1, 0), ("A0", 0, 0), ("A0", 1, 0), ("A1", 0, 0), ("A1", 1, 0),
     ("QR", 0, 0), ("heads", 0, 0), ("QR", 1, 0), ("score", 0, 0), ("KR", 0, 0), ("KR", 1, 0), ("turn", 0, 0),
     ("V", 0, 0), ("mix", 0, 0), ("V", 1, 0), ("heads", 1, 0), ("V", 0, 1), ("score", 1, 0),
     ("V", 1, 1), ("G", 0, 0), ("turn", 1, 0), ("G", 1, 0), ("mix", 1, 0), ("G", 0, 1),
     ("rheads", 0, 0), ("G", 1, 1), ("rscore", 0, 0), ("WA", 0, 0), ("rmix", 0, 0), ("WA", 0, 1), ("retT", 0, 0),
     ("rheads", 1, 0), ("WA", 1, 0), ("rscore", 1, 0), ("WA", 1, 1), ("rmix", 1, 0), ("GA", 0, 0), ("retT", 1, 0),
     ("GA", 1, 0), ("GA", 0, 1), ("GA", 1, 1)]
    + [(k, t, n) for n in range(2) for k in ("GR", "WR") for t in range(GT)]
    + [("mT", 0, 0), ("WO", 0, 0), ("mT", 1, 0), ("WO", 0, 1), ("norm2", 0, 0), ("WO", 1, 0),
       ("hT", 0, 0), ("WO", 1, 1), ("norm2", 1, 0), ("hT", 1, 0)]
    + [("query", None, 0), ("keys", None, 0), ("query", None, 1), ("keys", None, 1)]
    + [("top", None, 0), ("pick", None, 0), ("index", None, 0)]
)
HEAD_1 = [("top", None, 1), ("pick", None, 1), ("index", None, 1)]
LATE = [(k, None, h) for h in range(2, PH) for k in ("query", "keys", "top", "pick", "index")]
STAGES = EARLY + HEAD_1 + LATE

BANKS_OF = dict(norm=2, A0=1, A1=1, QR=1, KR=1, V=1, G=1, heads=2, score=4, turn=4, mix=1, rheads=2,
                rscore=2, rmix=4, retT=2, WA=1, GA=1, GR=1, WR=1, mT=2, WO=1, hT=2, query=1, keys=1)
FILLS = [(s, i) for s in STAGES for i in range(BANKS_OF.get(s[0], 0))]
FILL = {f: n for n, f in enumerate(FILLS)}
NFILL = len(FILLS)
WORKBANKS = 6

ACT_OF = dict(norm=("rms", "xn"), V=("v",), G=("silu",), heads=("qT", "kT"), score=("probs",), turn=("pT",),
              mix=("attT",), rheads=("kT",), rmix=("rms",), retT=("retT",), WA=("m",), GA=("sig",), GR=("sig",),
              mT=("mT",), norm2=("rms",), hT=("hT",), query=("qT",), keys=("scores",), pick=("exp",))
DVE_OF = dict(norm=("rstd", "hT"), A0=("q",), A1=("kv",), QR=("q",), KR=("k",), score=("masked",), turn=("normal",),
              rheads=("kw", "qwT"), rscore=("causal",), rmix=("gated", "state"), GA=("m",), WR=("m",),
              WO=("h",), norm2=("rstd", "hn"), top=("top",), pick=("picks",), index=("index",))


def places(made_in):
    order = [(s, r) for s in STAGES for r in made_in.get(s[0], ())]
    return {k: n for n, k in enumerate(order)}, len(order)


ACT_AT, NACT = places(ACT_OF)
DVE_AT, NDVE = places(DVE_OF)

RING = 12
QN = 2
NH2 = GT * PH
EIGHTHS = [(h, q) for h in range(NH2 + 1) for q in range(TOPK // QN)]


PE_SHARE = [12] * 6 + [5] * 8 + [8, 8]


def on_pe(h, k):
    n = PE_SHARE[h]
    return k * n // TOPK != (k + 1) * n // TOPK


def gathers():
    out = []
    for h, q in EIGHTHS:
        for k in range(QN * q, QN * q + QN):
            if h < NH2:
                out.append(("u", h, k))
            if h:
                out.append(("v", h - 1, k))
    return out


GATHERS = gathers()
GATHER = {g: n for n, g in enumerate(GATHERS)}
NGATHER = len(GATHERS)


def landed_in(g, n):
    return g * (16 * len(range(n % RING, NGATHER, RING))) + 16 * (n // RING + 1)


def last_tenant(n):
    if n >= RING:
        return n - RING, False
    return max(range(n, NGATHER, RING)), True


def used_counts():
    dve = pe = 0
    out = []
    for kind, h, k in GATHERS:
        if kind == "v" and on_pe(h, k):
            pe += 1
        else:
            dve += 1
        out.append((dve, pe))
    return out, dve, pe


USED, NUSED_DVE, NUSED_PE = used_counts()

V_ROWS = [[(h, k) for h in range(t * PH, (t + 1) * PH) for k in range(TOPK)] for t in range(GT)]
PE_ROWS = [[r for r in V_ROWS[t] if on_pe(*r)] for t in range(GT)]
DVE_ROWS = [[r for r in V_ROWS[t] if not on_pe(*r)] for t in range(GT)]

LATE_FROM, LATE_TO, HAND_0, HAND_1 = 4, 48, 128, 12


def share(stages, first, end):
    at = [len(stages) * (n - first) // (end - first) for n in range(first, end + 1)]
    return {n: stages[at[n - first]:at[n - first + 1]] for n in range(first, end)}


LATE_SHARE = share(LATE, LATE_FROM, LATE_TO)
HEAD_1_AT = [128, 130, 132]
EARLY_SHARE = share(EARLY, LATE_TO, HAND_0)
for n, s in zip(HEAD_1_AT, HEAD_1):
    EARLY_SHARE[n] = EARLY_SHARE.get(n, []) + [s]

C_MASK, C_CAUSAL, C_WQ, C_WK, C_SD, C_ID, C_IOTA = 0, 256, 384, 896, 904, 908, 1036
C_ALL = 1052
ROT_R, ROT_A = 64, 16
T_ALL = 2 * (ROT_R + ROT_A)


def shape_constants():
    f = np.float32
    i = np.arange(P)
    c = np.zeros((P, C_ALL), f)
    diff = (i[:, None] + P) - np.arange(2 * P)[None, :]
    band = (diff >= 0) & (diff < P)
    c[:, C_MASK:C_MASK + 256] = np.where(band, 0.0, NEG)
    mask0 = np.where(band & (np.arange(2 * P)[None, :] >= P), 0.0, NEG).astype(f)
    lg = np.log1p(-np.exp2(-5.0 - np.arange(RH)))
    scale = RQ ** -0.5
    c[:, C_CAUSAL:C_CAUSAL + P] = i[None, :] >= i[:, None]
    for half in range(2):
        for pair in range(4):
            h = 2 * pair + half
            c[half * 64:half * 64 + 64, C_WQ + pair * P:C_WQ + (pair + 1) * P] = np.exp(lg[h] * (i + 1.0))[None, :]
            c[half * 64:half * 64 + 64, C_SD + pair] = np.exp(lg[h] * P)
    for h in range(RH):
        c[:, C_WK + h] = np.exp(-lg[h] * (i + 1.0)) * scale
    c[:, C_ID:C_ID + P] = np.eye(P)
    c[:, C_IOTA:C_IOTA + 16] = np.arange(16)
    pos = np.arange(SEQ, dtype=f)
    rot = np.zeros((SEQ, T_ALL), f)
    at = 0
    for width, theta in ((ROT_R, 10000.0), (ROT_A, 500000.0)):
        half = width // 2
        freq = (f(theta) ** (-np.arange(half, dtype=f) / f(half))).astype(f)
        ang = (pos[:, None] * freq[None, :]).astype(np.float64)
        rot[:, at:at + width] = np.concatenate([np.cos(ang), np.cos(ang)], 1)
        rot[:, at + width:at + 2 * width] = np.concatenate([-np.sin(ang), np.sin(ang)], 1)
        at += 2 * width
    return c, rot, mask0


def is_first(g):
    return isinstance(g, int) and g == 0


def build_block(nc, x, norm_mix, w_in, att_sinks, w_att, w_ret, w_out, norm_ffn, w_query, keys1, keys2,
                peer_u, peer_v, norm_final, const_table, rot_table, mask_table, out):
    with ExitStack() as ctx:
        def sb(name, shape, dt=F32):
            return ctx.enter_context(nc.sbuf_tensor(name, shape, dt))

        def sem(name):
            return ctx.enter_context(nc.semaphore(name))

        work = [ctx.enter_context(nc.psum_tensor(f"work{i}", [P, CW], F32)) for i in range(WORKBANKS)]
        vsum = [ctx.enter_context(nc.psum_tensor(f"vsum{i}", [P, CW], F32)) for i in range(2)]

        const = sb("const", [P, C_ALL])
        gain_mix = sb("gain_mix", [P, KD])
        gain_ffn = sb("gain_ffn", [P, D])
        gain_fin = sb("gain_fin", [P, D])
        sinks = sb("sinks", [P, HEADS])
        keyT = sb("keyT", [P, 2, P])
        eps_t = sb("eps_t", [P, 1])
        rows = sb("rows", [P, RING, D])
        wbuf = sb("wbuf", [P, WBUFS, KD, CW])
        rot = sb("rot", [P, GT, T_ALL])
        xh = sb("xh", [P, GT, D])
        actT = sb("actT", [P, KD, GT * P])
        qa = sb("qa", [P, GT, 512])
        ka = sb("ka", [P, GT, P])
        va = sb("va", [P, GT + 1, P])
        kTa = sb("kTa", [P, (GT + 1) * P])
        probs = sb("probs", [P, HEADS, 2 * P])
        probsT = sb("probsT", [P, HEADS, 2, P])
        spare = sb("spare", [P, 512])
        attT = sb("attT", [P, 4, GT * P])
        qk_m = sb("qk_m", [P, GT, D])
        vg = sb("vg", [P, 2, GT, D])
        state = sb("state", [P, 4, RV])
        retT_hn = sb("retT_hn", [P, 2 * D])
        pqT = sb("pqT", [P, 2, GT * P])
        h_cur = sb("h_cur", [P, GT, D])
        hn_cur = sb("hn_cur", [P, GT, D])
        vacc = sb("vacc", [P, D])
        diag = sb("diag", [P, 4, P])
        small = sb("small", [P, 128])
        top_v = sb("top_v", [P, GT, 2, TOPK])
        top_i = sb("top_i", [P, GT, 2, TOPK], U32)
        top_if = sb("top_if", [P, 2, GT, TOPK])
        pick_v = sb("pick_v", [P, GT, TOPK])
        pick_i = sb("pick_i", [P, GT, TOPK], U32)
        part = sb("part", [P, 2, GT, TOPK], U32)
        sel = sb("sel", [P, 2, GT, TOPK])
        expg = sb("expg", [P, GT, TOPK])
        index_next = sb("index_next", [P, GT, EARLY_HEADS * TOPK], U32)
        index_cur = sb("index_cur", [P, GT, SLOTS], U32)
        gate_next = sb("gate_next", [P, GT, EARLY_HEADS * TOPK])
        gate_cur = sb("gate_cur", [P, GT, SLOTS])
        dots = sb("dots", [P, 2, TOPK])
        coef = sb("coef", [P, 2, TOPK])

        ident = const[:, C_ID:C_ID + P]
        causal = probs[:, 0:4].rearrange("p a b -> p (a b)").rearrange("p (h i) -> p h i", h=RH)
        ret_parts = probsT[:, :].rearrange("p h b q -> p (h b q)").rearrange("p (n w) -> p n w", n=4)
        rkT = ret_parts[:, 0].rearrange("p (a b) -> p a b", a=4)
        rqwT = ret_parts[:, 1].rearrange("p (a b) -> p a b", a=4)
        kw = ret_parts[:, 2]
        hqT = ret_parts[:, 3].rearrange("p (a b) -> p a b", a=4)
        mask_first = hn_cur[:, 0, 0:2 * P]
        key_raw = vacc[:, 0:2 * P].rearrange("p (s k) -> p s k", s=2)
        v_r, g_r = vg[:, 0], vg[:, 1]
        retT = retT_hn[:, :].rearrange("p (k t) -> p k t", k=KD)
        hn = retT_hn[:, :].rearrange("p (t d) -> p t d", t=GT)
        scores = vg[:, :, :, :].rearrange("p a b d -> p (a b d)").rearrange("p (t s k) -> p t s k", t=GT, s=2 * PH)
        cands = vg[:, :, :, :].rearrange("p a b d -> p (a b d)").rearrange("p (t h c) -> p t h c", t=GT, h=PH)

        def col(n, w=1):
            return small[:, n:n + w]
        SS, RMS, RSTD = 0, 2, 4
        MX, NM, RSUM, ESNK, DEN = 8, 16, 24, 32, 40
        SSR, RMSR, RINV, GSUM, GINV = 48, 56, 64, 72, 80
        FSS, FRMS, FRSTD = 96, 98, 100

        consts_landed = sem("consts_landed")
        gains_landed = sem("gains_landed")
        late_consts_landed = sem("late_consts_landed")
        set_up = sem("set_up")
        keys_turned = sem("keys_turned")
        keys_kept = sem("keys_kept")
        x_landed = [sem(f"x_landed{t}") for t in range(GT)]
        w_landed = [sem(f"w_landed{b}") for b in range(WBUFS)]
        filled = sem("filled")
        drained = [sem(f"drained{b}") for b in range(WORKBANKS)]
        act_made = sem("act_made")
        dve_made = sem("dve_made")
        act_step = [sem("act_early_step"), sem("act_late_step")]
        dve_step = [sem("dve_early_step"), sem("dve_late_step")]
        row_landed = [sem(f"row_landed{b}") for b in range(RING)]
        used_dve = sem("used_dve")
        used_pe = sem("used_pe")
        gelu_made = sem("gelu_made")
        coef_made = sem("coef_made")
        diag_made = sem("diag_made")
        acc_made = sem("acc_made")
        fin_rms = sem("fin_rms")
        out_made = sem("out_made")
        out_stored = [sem(f"out_stored{t}") for t in range(GT)]
        handed_act = sem("handed_act")
        handed_dve = sem("handed_dve")
        passed = sem("passed")

        def act_count(g, stage, result):
            return g * NACT + ACT_AT[(stage, result)] + 1

        def dve_count(g, stage, result):
            return g * NDVE + DVE_AT[(stage, result)] + 1

        def fill_count(g, stage, i=0):
            return g * NFILL + FILL[(stage, i)] + 1

        def bank_of(stage, i=0):
            b = FILL[(stage, i)] % WORKBANKS
            return work[b], drained[b]

        def drain_count(g, stage, i=0):
            n = FILL[(stage, i)]
            return g * len(range(n % WORKBANKS, NFILL, WORKBANKS)) + n // WORKBANKS + 1

        def chunk(name):
            b = CHUNK[name] % WBUFS
            return wbuf[:, b], w_landed[b]

        def chunk_count(g, name):
            n = CHUNK[name]
            return g * (16 * len(range(n % WBUFS, len(CHUNKS), WBUFS))) + 16 * (n // WBUFS + 1)

        W_DRAM = {"in": w_in, "att": w_att, "ret": w_ret, "out": w_out, "query": w_query}
        PER_TILE = 4
        NACC = GT * PER_TILE
        ACC_READ = [t * PER_TILE + 2 for t in range(GT)]

        LAST_USE = {}
        for s in STAGES:
            kind, t, n = s
            name = {"A0": "A0", "A1": "A1", "QR": "QR", "KR": "KR", "WA": "WA"}.get(kind)
            if kind in ("V", "G", "GA", "GR", "WR", "WO"):
                name = f"{kind}{n}"
            if kind == "query":
                name = f"WQ{n // 2}"
            if name:
                LAST_USE[name] = s

        block = ctx.enter_context(nc.Block())

        @block.sync
        def _(sp):
            def loads(g):
                for t in range(GT):
                    if not is_first(g):
                        sp.wait_ge(handed_act, (g - 1) * GT + t + 1)
                    r0 = g * (GT * P) + t * P
                    sp.dma_start(xh[:, t], x[bass.ds(r0, P), :]).then_inc(x_landed[t], 16)
                    sp.dma_start(rot[:, t], rot_table[bass.ds(r0, P), :]).then_inc(x_landed[t], 16)
                    if is_first(g) and t == 0:
                        sp.dma_start(const[:], const_table).then_inc(consts_landed, 16)
                for n, (name, which, c0, cw) in enumerate(CHUNKS):
                    buffer, landed = chunk(name)
                    if n >= WBUFS:
                        last = LAST_USE[CHUNKS[n - WBUFS][0]]
                        sp.wait_ge(filled, fill_count(g, last, BANKS_OF[last[0]] - 1))
                    elif not is_first(g):
                        last = LAST_USE[CHUNKS[max(range(n, len(CHUNKS), WBUFS))][0]]
                        sp.wait_ge(filled, fill_count(g - 1, last, BANKS_OF[last[0]] - 1))
                    src = W_DRAM[which].rearrange("(k p) n -> p k n", p=P)[:, :, c0:c0 + cw]
                    dst = buffer.rearrange("p k n -> p (k n)")[:, 0:src.shape[1] * cw].rearrange(
                        "p (k n) -> p k n", n=cw)
                    sp.dma_start(dst, src).then_inc(landed, 16)

            loads(0)
            with sp.Fori(0, GROUPS - 1) as r:
                loads(r + 1)

        @block.gpsimd
        def _(pool):
            pool.dma_start(gain_mix[:], norm_mix.rearrange("a (k p) -> p (a k)", p=P),
                           allow_slow_non_contiguous=True).then_inc(gains_landed, 16)
            pool.memset(eps_t[:], EPS).then_inc(set_up, 1)
            pool.memset(va[:, 0], 0.0).then_inc(set_up, 1)
            pool.memset(kTa[:, 0:P], 0.0).then_inc(set_up, 1)
            pool.memset(state[:], 0.0).then_inc(set_up, 1)
            pool.dma_start(mask_first, mask_table).then_inc(late_consts_landed, 16)
            pool.dma_start(sinks[:], att_sinks[0].partition_broadcast(P)).then_inc(late_consts_landed, 16)
            for half, keys in enumerate((keys1, keys2)):
                pool.dma_start(key_raw[:, half], keys).then_inc(late_consts_landed, 16)
            pool.dma_start(gain_ffn[:], norm_ffn[0].partition_broadcast(P)).then_inc(late_consts_landed, 16)
            pool.dma_start(gain_fin[:], norm_final.partition_broadcast(P)).then_inc(late_consts_landed, 16)

            def retrieve(g):
                for n, (kind, h, k) in enumerate(GATHERS):
                    t, head = h // PH, h % PH
                    if kind == "u" and k == 0:
                        if head < EARLY_HEADS:
                            pool.wait_ge(handed_dve, g * GT + t + 1)
                            pool.sem_inc(passed, 1)
                        else:
                            pool.wait_ge(dve_made, g * NDVE + DVE_AT[(("index", None, head), "index")] + 1)
                            pool.sem_inc(passed, 1)
                    m, of_last = last_tenant(n)
                    before = g if of_last else g + 1
                    dve, pe = USED[m]
                    kind_m, h_m, k_m = GATHERS[m]
                    if kind_m == "v" and on_pe(h_m, k_m):
                        pool.wait_ge(used_pe, before * NUSED_PE + pe)
                        pool.sem_inc(passed, 1)
                    else:
                        pool.wait_ge(used_dve, before * NUSED_DVE + dve)
                        pool.sem_inc(passed, 1)
                    slot = (h % PH) * TOPK + k
                    pool.indirect_dma_start(
                        rows[:, n % RING], None, (peer_u if kind == "u" else peer_v),
                        bass.IndirectOffsetOnAxis(ap=index_cur[:, h // PH, slot:slot + 1], axis=0),
                    ).then_inc(row_landed[n % RING], 16)

            with pool.Fori(0, GROUPS) as r:
                retrieve(r)

        @block.tensor
        def _(pe):
            def turn(dst, src):
                return pe.transpose(dst, src, ident)

            def project(g, stage, weights, lhs, steps, c0=0, cw=CW):
                bank, free = bank_of(stage)
                pe.wait_ge(free, drain_count(g, stage))
                for k in range(steps):
                    last = pe.matmul(bank[:, 0:cw], lhs[:, k], weights[:, k, c0:c0 + cw],
                                     start=(k == 0), stop=(k == steps - 1))
                last.then_inc(filled, 1)

            def front(g, stage):
                kind, t, n = stage
                toks = slice(t * P, t * P + P) if t is not None else None
                if kind in ("norm", "hT"):
                    src = hn[:, t]
                    if kind == "norm":
                        pe.wait_ge(act_made, act_count(g, stage, "xn"))
                    else:
                        pe.wait_ge(dve_made, dve_count(g, ("norm2", t, 0), "hn"))
                    for i in range(2):
                        bank, free = bank_of(stage, i)
                        pe.wait_ge(free, drain_count(g, stage, i))
                        for j in range(4):
                            k = 4 * i + j
                            last = turn(bank[:, j * P:(j + 1) * P], src[:, k * P:(k + 1) * P])
                        last.then_inc(filled, 1)
                elif kind in ("A0", "A1", "QR", "KR", "V", "G", "GA", "GR"):
                    name = kind + str(n) if kind in ("V", "G", "GA", "GR") else kind
                    pe.wait_ge(dve_made, dve_count(g, ("norm", t, 0), "hT"))
                    w, landed = chunk(name)
                    pe.wait_ge(landed, chunk_count(g, name))
                    cw = CHUNKS[CHUNK[name]][3]
                    if cw != CW:
                        w = w.rearrange("p k n -> p (k n)")[:, 0:KD * cw].rearrange("p (k n) -> p k n", n=cw)
                    project(g, stage, w, actT[:, :, toks], KD, 0, cw)
                elif kind == "heads":
                    pe.wait_ge(dve_made, dve_count(g, ("A0", t, 0), "q"))
                    bank, free = bank_of(stage, 0)
                    pe.wait_ge(free, drain_count(g, stage, 0))
                    for p in range(4):
                        last = turn(bank[:, p * P:(p + 1) * P], qa[:, t, p * P:(p + 1) * P])
                    last.then_inc(filled, 1)
                    pe.wait_ge(dve_made, dve_count(g, ("A1", t, 0), "kv"))
                    bank, free = bank_of(stage, 1)
                    pe.wait_ge(free, drain_count(g, stage, 1))
                    turn(bank[:, 0:P], ka[:, t]).then_inc(filled, 1)
                elif kind == "score":
                    pe.wait_ge(act_made, act_count(g, ("heads", t, 0), "kT"))
                    if is_first(g) and t == 0:
                        pe.wait_ge(set_up, 4)
                    for i in range(4):
                        c, p0 = i // 2, 2 * (i % 2)
                        bank, free = bank_of(stage, i)
                        pe.wait_ge(free, drain_count(g, stage, i))
                        for j in range(2):
                            last = pe.matmul(bank[:, j * 256:(j + 1) * 256], hqT[c * 64:c * 64 + 64, p0 + j],
                                             kTa[c * 64:c * 64 + 64, t * P:(t + 2) * P], start=True, stop=True)
                        last.then_inc(filled, 1)
                elif kind == "turn":
                    pe.wait_ge(dve_made, dve_count(g, stage, "normal"))
                    for i in range(4):
                        bank, free = bank_of(stage, i)
                        pe.wait_ge(free, drain_count(g, stage, i))
                        for j in range(2):
                            for b in range(2):
                                last = turn(bank[:, (2 * j + b) * P:(2 * j + b + 1) * P],
                                            probs[:, 2 * i + j, b * P:(b + 1) * P])
                        last.then_inc(filled, 1)
                elif kind == "mix":
                    pe.wait_ge(act_made, act_count(g, ("turn", t, 0), "pT"))
                    bank, free = bank_of(stage)
                    pe.wait_ge(free, drain_count(g, stage))
                    for c in range(KVH):
                        for odd in range(2):
                            h = 4 * c + odd
                            for b in range(2):
                                last = pe.matmul(bank[odd * 64:odd * 64 + 64, c * 256:(c + 1) * 256],
                                                 va[:, t + b, c * 64:(c + 1) * 64], probsT[:, h:h + 3:2, b],
                                                 start=(b == 0), stop=(b == 1))
                    last.then_inc(filled, 1)
                elif kind == "rheads":
                    for i, src in enumerate((qk_m[:, t, 0:512], kw)):
                        if i:
                            pe.wait_ge(dve_made, dve_count(g, stage, "kw"))
                        else:
                            pe.wait_ge(dve_made, dve_count(g, ("QR", t, 0), "q"))
                        bank, free = bank_of(stage, i)
                        pe.wait_ge(free, drain_count(g, stage, i))
                        for p in range(4):
                            last = turn(bank[:, p * P:(p + 1) * P], src[:, p * P:(p + 1) * P])
                        last.then_inc(filled, 1)
                elif kind == "rscore":
                    pe.wait_ge(act_made, act_count(g, ("rheads", t, 0), "kT"))
                    pe.wait_ge(dve_made, dve_count(g, ("rheads", t, 0), "qwT"))
                    for c in range(2):
                        bank, free = bank_of(stage, c)
                        pe.wait_ge(free, drain_count(g, stage, c))
                        for p in range(4):
                            last = pe.matmul(bank[:, p * P:(p + 1) * P], rkT[c * 64:c * 64 + 64, p],
                                             rqwT[c * 64:c * 64 + 64, p], start=True, stop=True)
                        last.then_inc(filled, 1)
                elif kind == "rmix":
                    pe.wait_ge(dve_made, dve_count(g, ("rscore", t, 0), "causal"))
                    pe.wait_ge(act_made, act_count(g, ("V", t, 1), "v"))
                    if t:
                        pe.wait_ge(dve_made, dve_count(g, ("rmix", t - 1, 0), "state"))
                    else:
                        if not is_first(g):
                            pe.wait_ge(dve_made, (g - 1) * NDVE + DVE_AT[(("rmix", GT - 1, 0), "state")] + 1)
                    for c in range(2):
                        bank, free = bank_of(stage, c)
                        pe.wait_ge(free, drain_count(g, stage, c))
                        for p in range(4):
                            h = 2 * p + c
                            pe.matmul(bank[:, p * P:(p + 1) * P], causal[:, c * 4 + p],
                                      v_r[:, t, h * RV:(h + 1) * RV], start=True, stop=False)
                            last = pe.matmul(bank[:, p * P:(p + 1) * P], rqwT[c * 64:c * 64 + 64, p],
                                             state[c * 64:c * 64 + 64, p], start=False, stop=True)
                        last.then_inc(filled, 1)
                    for i in range(2):
                        bank, free = bank_of(stage, 2 + i)
                        pe.wait_ge(free, drain_count(g, stage, 2 + i))
                        for j in range(2):
                            p = 2 * i + j
                            last = pe.matmul(bank[:, j * 256:(j + 1) * 256], kw[:, p * P:(p + 1) * P],
                                             v_r[:, t, p * 256:(p + 1) * 256], start=True, stop=True)
                        last.then_inc(filled, 1)
                elif kind in ("retT", "mT"):
                    if kind == "retT":
                        pe.wait_ge(dve_made, dve_count(g, ("rmix", t, 0), "gated"))
                        src = g_r[:, t]
                    else:
                        pe.wait_ge(dve_made, dve_count(g, ("WR", t, 1), "m"))
                        src = qk_m[:, t]
                    for i in range(2):
                        bank, free = bank_of(stage, i)
                        pe.wait_ge(free, drain_count(g, stage, i))
                        for j in range(4):
                            k = 4 * i + j
                            last = turn(bank[:, j * P:(j + 1) * P], src[:, k * P:(k + 1) * P])
                        last.then_inc(filled, 1)
                elif kind == "WA":
                    pe.wait_ge(act_made, act_count(g, ("mix", t, 0), "attT"))
                    w, landed = chunk("WA")
                    pe.wait_ge(landed, chunk_count(g, "WA"))
                    w = w.rearrange("p k n -> p (k n)").rearrange("p (k n) -> p k n", n=1024)
                    project(g, stage, w, attT[:, :, toks], 4, n * CW)
                elif kind == "WR":
                    pe.wait_ge(act_made, act_count(g, ("retT", t, 0), "retT"))
                    w, landed = chunk(f"WR{n}")
                    pe.wait_ge(landed, chunk_count(g, f"WR{n}"))
                    project(g, stage, w, retT[:, :, toks], KD)
                elif kind == "WO":
                    pe.wait_ge(act_made, act_count(g, ("mT", t, 0), "mT"))
                    w, landed = chunk(f"WO{n}")
                    pe.wait_ge(landed, chunk_count(g, f"WO{n}"))
                    project(g, stage, w, actT[:, :, toks], KD)
                elif kind == "query":
                    pe.wait_ge(act_made, act_count(g, ("hT", GT - 1, 0), "hT"))
                    w, landed = chunk(f"WQ{n // 2}")
                    pe.wait_ge(landed, chunk_count(g, f"WQ{n // 2}"))
                    bank, free = bank_of(stage)
                    pe.wait_ge(free, drain_count(g, stage))
                    for half in range(2):
                        c0 = (n % 2) * 256 + half * P
                        for k in range(KD):
                            last = pe.matmul(bank[:, half * 256:(half + 1) * 256], w[:, k, c0:c0 + P], actT[:, k],
                                             start=(k == 0), stop=(k == KD - 1))
                    last.then_inc(filled, 1)
                elif kind == "keys":
                    pe.wait_ge(act_made, act_count(g, ("query", None, n), "qT"))
                    if is_first(g) and n == 0:
                        pe.wait_ge(keys_kept, 1)
                    bank, free = bank_of(stage)
                    pe.wait_ge(free, drain_count(g, stage))
                    for tt in range(GT):
                        for half in range(2):
                            i = 2 * tt + half
                            last = pe.matmul(bank[:, i * P:(i + 1) * P], pqT[:, half, tt * P:(tt + 1) * P],
                                             keyT[:, half], start=True, stop=True)
                    last.then_inc(filled, 1)

            def retrieve(g, h, q):
                if not h:
                    return
                h -= 1
                t = h // PH
                for k in range(QN * q, QN * q + QN):
                    if not on_pe(h, k):
                        continue
                    n = GATHER[("v", h, k)]
                    pes = USED[n][1]
                    pe.wait_ge(diag_made, g * NUSED_PE + pes)
                    pe.wait_ge(row_landed[n % RING], landed_in(g, n))
                    first, final = (h, k) == PE_ROWS[t][0], (h, k) == PE_ROWS[t][-1]
                    if first:
                        pe.wait_ge(acc_made, (g + 1) * NACC + ACC_READ[0] if t else g * NACC + ACC_READ[GT - 1])
                    for j in range(2):
                        last = pe.matmul(vsum[j][:, :], diag[:, (pes - 1) % 4], rows[:, n % RING, j * CW:(j + 1) * CW],
                                         start=first, stop=final)
                    last.then_inc(used_pe, 1)

            for free in drained:
                pe.sem_inc(free, 1)
            pe.sem_inc(used_pe, NUSED_PE)
            pe.wait_ge(consts_landed, 16)
            for stage in EARLY:
                if stage == ("A0", 0, 0):
                    pe.wait_ge(late_consts_landed, 16 * 6)
                    for half in range(2):
                        last = turn(vsum[0][:, half * P:(half + 1) * P], key_raw[:, half])
                    last.then_inc(keys_turned, 1)
                front(0, stage)
            with pe.Fori(0, GROUPS - 1) as r:
                for n, (h, q) in enumerate(EIGHTHS):
                    retrieve(r, h, q)
                    for stage in LATE_SHARE.get(n, ()):
                        front(r, stage)
                    for stage in EARLY_SHARE.get(n, ()):
                        front(r + 1, stage)
            for n, (h, q) in enumerate(EIGHTHS):
                retrieve(GROUPS - 1, h, q)
                for stage in LATE_SHARE.get(n, ()):
                    front(GROUPS - 1, stage)

        @block.scalar
        def _(act):
            steps = [0]
            per_group = [None, 16]
            part_now = [0]

            def start_steps(which):
                steps[0], part_now[0] = 0, which

            def end_late():
                act.sem_inc(act_step[1], per_group[1] - steps[0])

            def step_sem():
                return act_step[part_now[0]]

            def next_step(g):
                steps[0] += 1
                return (0 if is_first(g) else g * per_group[part_now[0]]) + steps[0]

            def drain_to(g, stage, i, dst, func=ACT.Copy, view=None):
                act.wait_ge(filled, fill_count(g, stage, i))
                bank, free = bank_of(stage, i)
                src = bank[:, :] if view is None else view(bank)
                act.activation(dst, src, func).then_inc(step_sem(), 1)
                act.wait_ge(step_sem(), next_step(g))
                act.sem_inc(free, 1)

            def front(g, stage):
                kind, t, n = stage
                toks = slice(t * P, t * P + P) if t is not None else None
                if kind == "norm":
                    if is_first(g) and t == 0:
                        act.wait_ge(set_up, 4)
                    act.wait_ge(x_landed[t], g * 32 + 32)
                    if not is_first(g):
                        act.wait_ge(handed_dve, (g - 1) * GT + t + 1)
                    act.activation(hn[:, t], xh[:, t], ACT.Square, accum_out=col(SS + t)).then_inc(step_sem(), 1)
                    act.wait_ge(step_sem(), next_step(g))
                    act.activation(col(RMS + t), col(SS + t), ACT.Sqrt, bias=eps_t[:, 0:1],
                                   scale=1.0 / D).then_inc(act_made, 1)
                    act.wait_ge(dve_made, dve_count(g, stage, "rstd"))
                    act.activation(hn[:, t], xh[:, t], ACT.Copy, scale=col(RSTD + t)).then_inc(act_made, 1)
                elif kind == "V":
                    if not is_first(g):
                        act.wait_ge(dve_made, (g - 1) * NDVE + NDVE)
                    drain_to(g, stage, 0, v_r[:, t, n * CW:(n + 1) * CW])
                    act.sem_inc(act_made, 1)
                elif kind == "G":
                    drain_to(g, stage, 0, g_r[:, t, n * CW:(n + 1) * CW], ACT.Silu)
                    act.sem_inc(act_made, 1)
                elif kind == "heads":
                    drain_to(g, stage, 0, ret_parts[:, 3])
                    act.sem_inc(act_made, 1)
                    drain_to(g, stage, 1, kTa[:, (t + 1) * P:(t + 2) * P], view=lambda b: b[:, 0:P])
                    act.sem_inc(act_made, 1)
                elif kind == "score":
                    act.wait_ge(dve_made, dve_count(g, stage, "masked"))
                    for h in range(HEADS):
                        ins = act.activation(probs[:, h], probs[:, h], ACT.Exp, bias=col(NM + h),
                                             accum_out=col(RSUM + h))
                    ins.then_inc(step_sem(), 1)
                    act.wait_ge(step_sem(), next_step(g))
                    act.activation(col(ESNK, HEADS), col(ESNK, HEADS), ACT.Exp).then_inc(act_made, 1)
                elif kind == "turn":
                    for i in range(4):
                        drain_to(g, stage, i, probsT[:, 2 * i:2 * i + 2].rearrange("p h b q -> p (h b q)"))
                    act.sem_inc(act_made, 1)
                elif kind == "mix":
                    drain_to(g, stage, 0, attT[:, :, toks], view=lambda b: b[:, :].rearrange("p (k q) -> p k q", k=4))
                    if t == GT - 1:
                        act.activation(kTa[:, 0:P], kTa[:, GT * P:(GT + 1) * P], ACT.Copy).then_inc(step_sem(), 1)
                        act.wait_ge(step_sem(), next_step(g))
                        act.activation(va[:, 0], va[:, GT], ACT.Copy).then_inc(step_sem(), 1)
                        act.wait_ge(step_sem(), next_step(g))
                    act.sem_inc(act_made, 1)
                elif kind == "rheads":
                    drain_to(g, stage, 1, ret_parts[:, 0])
                    act.sem_inc(act_made, 1)
                elif kind == "rmix":
                    for c in range(2):
                        act.wait_ge(filled, fill_count(g, stage, c))
                        bank, _ = bank_of(stage, c)
                        for p in range(4):
                            ins = act.activation(spare[:, p * P:(p + 1) * P],
                                                 bank[:, p * P:(p + 1) * P], ACT.Square, accum_out=col(SSR + c * 4 + p))
                        ins.then_inc(step_sem(), 1)
                        act.wait_ge(step_sem(), next_step(g))
                    act.activation(col(RMSR, RH), col(SSR, RH), ACT.Sqrt, bias=eps_t[:, 0:1],
                                   scale=1.0 / RV).then_inc(act_made, 1)
                elif kind in ("retT", "mT"):
                    dst = retT if kind == "retT" else actT
                    for i in range(2):
                        drain_to(g, stage, i, dst[:, 4 * i:4 * i + 4, toks],
                                 view=lambda b: b[:, :].rearrange("p (k q) -> p k q", k=4))
                    act.sem_inc(act_made, 1)
                elif kind == "WA":
                    act.wait_ge(dve_made, dve_count(g, ("rheads", t, 0), "kw"))
                    drain_to(g, stage, 0, qk_m[:, t, n * CW:(n + 1) * CW])
                    act.sem_inc(act_made, 1)
                elif kind in ("GA", "GR"):
                    if kind == "GR" or n:
                        act.wait_ge(dve_made, dve_count(g, ("GA", t, n - 1) if kind == "GA" else
                                 (("WR", t, n - 1) if n else ("GA", t, 1)), "m"))
                    drain_to(g, stage, 0, qa[:, t], ACT.Sigmoid)
                    act.sem_inc(act_made, 1)
                elif kind == "norm2":
                    act.wait_ge(dve_made, dve_count(g, ("WO", t, 1), "h"))
                    act.activation(hn[:, t], xh[:, t], ACT.Square, accum_out=col(SS + t)).then_inc(step_sem(), 1)
                    act.wait_ge(step_sem(), next_step(g))
                    act.activation(col(RMS + t), col(SS + t), ACT.Sqrt, bias=eps_t[:, 0:1],
                                   scale=1.0 / D).then_inc(act_made, 1)
                elif kind == "hT":
                    for i in range(2):
                        drain_to(g, stage, i, actT[:, 4 * i:4 * i + 4, toks],
                                 view=lambda b: b[:, :].rearrange("p (k q) -> p k q", k=4))
                    act.sem_inc(act_made, 1)
                elif kind == "query":
                    if n:
                        act.wait_ge(filled, fill_count(g, ("keys", None, n - 1)))
                    drain_to(g, stage, 0, pqT[:, :, :].rearrange("p a b -> p (a b)"))
                    act.sem_inc(act_made, 1)
                elif kind == "keys":
                    drain_to(g, stage, 0, scores[:, :, 2 * n:2 * n + 2, :],
                             view=lambda b: b[:, :].rearrange("p (t s k) -> p t s k", t=GT, s=2))
                    act.sem_inc(act_made, 1)
                elif kind == "pick":
                    act.wait_ge(dve_made, dve_count(g, stage, "picks"))
                    act.activation(expg[:], expg[:], ACT.Exp).then_inc(act_made, 1)

            def retrieve(g, h, q):
                if h and q == 0:
                    hp = h - 1
                    n = GATHER[("u", hp, TOPK - 1)]
                    act.wait_ge(used_dve, (g + 1) * NUSED_DVE + USED[n][0])
                    act.activation(dots[:, hp % 2], dots[:, hp % 2], ACT.Gelu).then_inc(gelu_made, 1)
                if h:
                    hp = h - 1
                    t = hp // PH
                    for k in range(QN * q, QN * q + QN):
                        if not on_pe(hp, k):
                            continue
                        n = GATHER[("v", hp, k)]
                        pes = USED[n][1]
                        act.wait_ge(coef_made, g * NH2 + hp + 1)
                        act.wait_ge(used_pe, (g + 1) * NUSED_PE + pes - 4)
                        act.activation(diag[:, (pes - 1) % 4], ident, ACT.Copy,
                                       scale=coef[:, hp % 2, k:k + 1]).then_inc(diag_made, 1)
                    if hp % PH == PH - 1 and q == TOPK // QN - 1:
                        act.wait_ge(acc_made, (g + 1) * NACC + t * PER_TILE + 3)
                        act.activation(vacc[:], h_cur[:, t], ACT.Square, accum_out=col(FSS)).then_inc(fin_rms, 1)
                        act.wait_ge(fin_rms, g * (2 * GT) + 2 * t + 1)
                        act.activation(col(FRMS), col(FSS), ACT.Sqrt, bias=eps_t[:, 0:1],
                                       scale=1.0 / D).then_inc(fin_rms, 1)
                        act.wait_ge(out_made, g * GT + t + 1)
                        act.dma_start(out[bass.ds(g * (GT * P) + t * P, P), :], h_cur[:, t]).then_inc(out_stored[t], 16)

            def hand_over(g, t):
                if not is_first(g):
                    act.wait_ge(out_stored[t], g * 16)
                act.wait_ge(dve_made, dve_count(g, ("WO", t, 1), "h"))
                act.activation(h_cur[:, t], xh[:, t], ACT.Copy).then_inc(handed_act, 1)

            start_steps(0)
            for stage in EARLY:
                if stage == ("V", 0, 0):
                    act.wait_ge(keys_turned, 1)
                    act.activation(keyT[:, :, :].rearrange("p a b -> p (a b)"), vsum[0][:, 0:2 * P],
                                   ACT.Copy).then_inc(keys_kept, 1)
                front(0, stage)
            hand_over(0, 0)
            for stage in HEAD_1:
                front(0, stage)
            per_group[0] = steps[0]
            with act.Fori(0, GROUPS - 1) as r:
                start_steps(1)
                for n, (h, q) in enumerate(EIGHTHS):
                    if n == HAND_0:
                        hand_over(r + 1, 0)
                    retrieve(r, h, q)
                    if n == HAND_1:
                        hand_over(r, 1)
                    for stage in LATE_SHARE.get(n, ()):
                        front(r, stage)
                    if n == LATE_TO - 1:
                        end_late()
                        start_steps(0)
                    for stage in EARLY_SHARE.get(n, ()):
                        front(r + 1, stage)
                assert steps[0] == per_group[0]
            start_steps(1)
            for n, (h, q) in enumerate(EIGHTHS):
                retrieve(GROUPS - 1, h, q)
                if n == HAND_1:
                    hand_over(GROUPS - 1, 1)
                for stage in LATE_SHARE.get(n, ()):
                    front(GROUPS - 1, stage)
            for t in range(GT):
                act.wait_ge(out_stored[t], 16 * GROUPS)

        @block.vector
        def _(dve):
            steps = [0]
            per_group = [None, 160]
            part_now = [0]

            def start_steps(which):
                steps[0], part_now[0] = 0, which

            def end_late():
                dve.sem_inc(dve_step[1], per_group[1] - steps[0])

            def step_sem():
                return dve_step[part_now[0]]

            def next_step(g):
                steps[0] += 1
                return (0 if is_first(g) else g * per_group[part_now[0]]) + steps[0]

            def sixteen_largest(g, jobs):
                for step in range(5):
                    for values, top, place in jobs:
                        if step == 0:
                            ins = dve.max(top[:, 0:8], values)
                        elif step == 1:
                            ins = dve.max_index(place[:, 0:8], top[:, 0:8], values)
                        elif step == 2:
                            ins = dve.match_replace(values, top[:, 0:8], values, LOWEST)
                        elif step == 3:
                            ins = dve.max(top[:, 8:16], values)
                        else:
                            ins = dve.max_index(place[:, 8:16], top[:, 8:16], values)
                    ins.then_inc(step_sem(), 1)
                    dve.wait_ge(step_sem(), next_step(g))
                    if step < 4:
                        dve.sem_inc(passed, 1)

            def rotate(g, bank, free, dst, src, cos, sin, tmp, rest=None):
                w = src.shape[-1] // 2
                lo, hi = (slice(None),) * (len(src.shape) - 1) + (slice(0, w),), \
                    (slice(None),) * (len(src.shape) - 1) + (slice(w, 2 * w),)
                dve.tensor_tensor(tmp[lo], src[hi], sin[lo], ALU.mult)
                dve.tensor_tensor(tmp[hi], src[lo], sin[hi], ALU.mult)
                if rest is not None:
                    dve.tensor_copy(*rest)
                dve.tensor_tensor(dst, src, cos, ALU.mult).then_inc(step_sem(), 1)
                dve.wait_ge(step_sem(), next_step(g))
                dve.tensor_tensor(dst, dst, tmp, ALU.add).then_inc(step_sem(), 1)
                dve.wait_ge(step_sem(), next_step(g))
                dve.sem_inc(free, 1)

            def front(g, stage):
                kind, t, n = stage
                toks = slice(t * P, t * P + P) if t is not None else None
                if kind == "norm":
                    dve.wait_ge(act_made, act_count(g, stage, "rms"))
                    dve.reciprocal(col(RSTD + t), col(RMS + t)).then_inc(dve_made, 1)
                    if t == 0:
                        if not is_first(g):
                            dve.wait_ge(filled, (g - 1) * NFILL + FILL[(("query", None, PH - 1), 0)] + 1)
                    for i in range(2):
                        dve.wait_ge(filled, fill_count(g, stage, i))
                        bank, free = bank_of(stage, i)
                        gain = gain_mix[:, 4 * i:4 * i + 4].unsqueeze(2).to_broadcast([P, 4, P])
                        dve.tensor_tensor(actT[:, 4 * i:4 * i + 4, toks],
                                                 bank[:, :].rearrange("p (k q) -> p k q", k=4), gain, ALU.mult).then_inc(step_sem(), 1)
                        dve.wait_ge(step_sem(), next_step(g))
                        dve.sem_inc(free, 1)
                    dve.sem_inc(dve_made, 1)
                elif kind == "A0":
                    dve.wait_ge(filled, fill_count(g, stage))
                    bank, free = bank_of(stage)
                    src = bank[:, :].rearrange("p (c h d) -> p c h d", c=2, h=4)
                    dst = qa[:, t].rearrange("p (h c d) -> p c h d", c=2, h=4)
                    cos = rot[:, t, 128:144]
                    sin = rot[:, t, 144:160]
                    for c in range(2):
                        tmp = spare[:, c * 64:c * 64 + 64].rearrange("p (h d) -> p h d", h=4)
                        cs = cos.unsqueeze(1).to_broadcast([P, 4, ROT_A])
                        sn = sin.unsqueeze(1).to_broadcast([P, 4, ROT_A])
                        s = src[:, c]
                        o = dst[:, c]
                        dve.tensor_tensor(tmp[:, :, 0:8], s[:, :, 8:16], sn[:, :, 0:8], ALU.mult)
                        dve.tensor_tensor(tmp[:, :, 8:16], s[:, :, 0:8], sn[:, :, 8:16], ALU.mult)
                        dve.tensor_copy(o[:, :, 16:64], s[:, :, 16:64])
                        dve.tensor_tensor(o[:, :, 0:16], s[:, :, 0:16], cs, ALU.mult).then_inc(step_sem(), 1)
                        dve.wait_ge(step_sem(), next_step(g))
                        dve.tensor_tensor(o[:, :, 0:16], o[:, :, 0:16], tmp, ALU.add).then_inc(step_sem(), 1)
                        dve.wait_ge(step_sem(), next_step(g))
                    dve.sem_inc(free, 1)
                    dve.sem_inc(dve_made, 1)
                elif kind == "A1":
                    dve.wait_ge(filled, fill_count(g, stage))
                    bank, free = bank_of(stage)
                    s = bank[:, 0:P].rearrange("p (h d) -> p h d", h=KVH)
                    o = ka[:, t].rearrange("p (h d) -> p h d", h=KVH)
                    tmp = spare[:, 0:32].rearrange("p (h d) -> p h d", h=KVH)
                    cs = rot[:, t, 128:144].unsqueeze(1).to_broadcast([P, KVH, ROT_A])
                    sn = rot[:, t, 144:160].unsqueeze(1).to_broadcast([P, KVH, ROT_A])
                    dve.tensor_tensor(tmp[:, :, 0:8], s[:, :, 8:16], sn[:, :, 0:8], ALU.mult)
                    dve.tensor_tensor(tmp[:, :, 8:16], s[:, :, 0:8], sn[:, :, 8:16], ALU.mult)
                    dve.tensor_copy(o[:, :, 16:64], s[:, :, 16:64])
                    if t == 0:
                        if not is_first(g):
                            dve.wait_ge(act_made, (g - 1) * NACT + ACT_AT[(("mix", GT - 1, 0), "attT")] + 1)
                    dve.tensor_copy(va[:, t + 1], bank[:, P:2 * P])
                    dve.tensor_tensor(o[:, :, 0:16], s[:, :, 0:16], cs, ALU.mult).then_inc(step_sem(), 1)
                    dve.wait_ge(step_sem(), next_step(g))
                    dve.tensor_tensor(o[:, :, 0:16], o[:, :, 0:16], tmp, ALU.add).then_inc(step_sem(), 1)
                    dve.wait_ge(step_sem(), next_step(g))
                    dve.sem_inc(free, 1)
                    dve.sem_inc(dve_made, 1)
                elif kind in ("QR", "KR"):
                    dve.wait_ge(filled, fill_count(g, stage))
                    bank, free = bank_of(stage)
                    c0 = 0 if kind == "QR" else 512
                    s = bank[:, :].rearrange("p (h d) -> p h d", h=RH)
                    o = qk_m[:, t, c0:c0 + 512].rearrange("p (h d) -> p h d", h=RH)
                    tmp = spare[:, :].rearrange("p (h d) -> p h d", h=RH)
                    if kind == "QR" and t == 0:
                        if not is_first(g):
                            dve.wait_ge(filled, (g - 1) * NFILL + FILL[(("mT", GT - 1, 0), 1)] + 1)
                    cs = rot[:, t, 0:64].unsqueeze(1).to_broadcast([P, RH, ROT_R])
                    sn = rot[:, t, 64:128].unsqueeze(1).to_broadcast([P, RH, ROT_R])
                    dve.tensor_tensor(tmp[:, :, 0:32], s[:, :, 32:64], sn[:, :, 0:32], ALU.mult)
                    dve.tensor_tensor(tmp[:, :, 32:64], s[:, :, 0:32], sn[:, :, 32:64], ALU.mult)
                    dve.tensor_tensor(o, s, cs, ALU.mult).then_inc(step_sem(), 1)
                    dve.wait_ge(step_sem(), next_step(g))
                    dve.tensor_tensor(o, o, tmp, ALU.add).then_inc(step_sem(), 1)
                    dve.wait_ge(step_sem(), next_step(g))
                    dve.sem_inc(free, 1)
                    dve.sem_inc(dve_made, 1)
                elif kind == "score":
                    mask = mask_first if is_first(g) and t == 0 else const[:, C_MASK:C_MASK + 256]
                    if is_first(g) and t == 0:
                        dve.wait_ge(late_consts_landed, 16 * 6)
                    for i in range(4):
                        dve.wait_ge(filled, fill_count(g, stage, i))
                        bank, free = bank_of(stage, i)
                        dve.scalar_tensor_tensor(
                            out=probs[:, 2 * i:2 * i + 2], in0=bank[:, :].rearrange("p (h k) -> p h k", h=2),
                            scalar=HD ** -0.5, in1=mask.unsqueeze(1).to_broadcast([P, 2, 2 * P]),
                            op0=ALU.mult, op1=ALU.add).then_inc(step_sem(), 1)
                        dve.wait_ge(step_sem(), next_step(g))
                        dve.sem_inc(free, 1)
                    dve.tensor_reduce(col(MX, HEADS), probs[:], AX.X, ALU.max).then_inc(step_sem(), 1)
                    dve.wait_ge(step_sem(), next_step(g))
                    dve.tensor_tensor(col(MX, HEADS), col(MX, HEADS), sinks[:], ALU.max).then_inc(step_sem(), 1)
                    dve.wait_ge(step_sem(), next_step(g))
                    dve.tensor_tensor(col(ESNK, HEADS), sinks[:], col(MX, HEADS), ALU.subtract)
                    dve.tensor_scalar(col(NM, HEADS), col(MX, HEADS), -1.0, None, ALU.mult).then_inc(step_sem(), 1)
                    dve.wait_ge(step_sem(), next_step(g))
                    dve.sem_inc(dve_made, 1)
                elif kind == "turn":
                    dve.wait_ge(act_made, act_count(g, ("score", t, 0), "probs"))
                    dve.tensor_tensor(col(DEN, HEADS), col(RSUM, HEADS), col(ESNK, HEADS), ALU.add).then_inc(step_sem(), 1)
                    dve.wait_ge(step_sem(), next_step(g))
                    dve.reciprocal(col(DEN, HEADS), col(DEN, HEADS)).then_inc(step_sem(), 1)
                    dve.wait_ge(step_sem(), next_step(g))
                    dve.tensor_tensor(probs[:], probs[:], col(DEN, HEADS).unsqueeze(2).to_broadcast([P, HEADS, 2 * P]),
                                      ALU.mult).then_inc(dve_made, 1)
                elif kind == "rheads":
                    if t:
                        dve.wait_ge(filled, fill_count(g, ("rmix", t - 1, 0), 3))
                    else:
                        dve.wait_ge(filled, fill_count(g, ("mix", GT - 1, 0)))
                    dve.tensor_tensor(kw.rearrange("p (h d) -> p h d", h=RH),
                                      qk_m[:, t, 512:1024].rearrange("p (h d) -> p h d", h=RH),
                                      const[:, C_WK:C_WK + RH].unsqueeze(2).to_broadcast([P, RH, RQ]),
                                      ALU.mult).then_inc(dve_made, 1)
                    dve.wait_ge(filled, fill_count(g, stage, 0))
                    bank, free = bank_of(stage, 0)
                    dve.tensor_tensor(rqwT, bank[:, :].rearrange("p (a b) -> p a b", a=4),
                                      const[:, C_WQ:C_WQ + 512].rearrange("p (a b) -> p a b", a=4),
                                      ALU.mult).then_inc(step_sem(), 1)
                    dve.wait_ge(step_sem(), next_step(g))
                    dve.sem_inc(free, 1)
                    dve.sem_inc(dve_made, 1)
                elif kind == "rscore":
                    for c in range(2):
                        dve.wait_ge(filled, fill_count(g, stage, c))
                        bank, free = bank_of(stage, c)
                        dve.tensor_tensor(causal[:, 4 * c:4 * c + 4],
                                                 bank[:, :].rearrange("p (a b) -> p a b", a=4),
                                                 const[:, C_CAUSAL:C_CAUSAL + P].unsqueeze(1).to_broadcast([P, 4, P]), ALU.mult).then_inc(step_sem(), 1)
                        dve.wait_ge(step_sem(), next_step(g))
                        dve.sem_inc(free, 1)
                    dve.sem_inc(dve_made, 1)
                elif kind == "rmix":
                    dve.wait_ge(act_made, act_count(g, stage, "rms"))
                    dve.reciprocal(col(RINV, RH), col(RMSR, RH)).then_inc(step_sem(), 1)
                    dve.wait_ge(step_sem(), next_step(g))
                    dve.wait_ge(act_made, act_count(g, ("G", t, 1), "silu"))
                    gv = g_r[:, t].rearrange("p (a c d) -> p c a d", a=4, c=2)
                    for c in range(2):
                        ins = dve.tensor_tensor(gv[:, c], gv[:, c],
                                                col(RINV + 4 * c, 4).unsqueeze(2).to_broadcast([P, 4, RV]), ALU.mult)
                    ins.then_inc(step_sem(), 1)
                    dve.wait_ge(step_sem(), next_step(g))
                    for c in range(2):
                        dve.wait_ge(filled, fill_count(g, stage, c))
                        bank, free = bank_of(stage, c)
                        dve.tensor_tensor(gv[:, c], bank[:, :].rearrange("p (a b) -> p a b", a=4), gv[:, c],
                                          ALU.mult).then_inc(step_sem(), 1)
                        dve.wait_ge(step_sem(), next_step(g))
                        dve.sem_inc(free, 1)
                    dve.sem_inc(dve_made, 1)
                    for i in range(2):
                        dve.wait_ge(filled, fill_count(g, stage, 2 + i))
                        bank, free = bank_of(stage, 2 + i)
                        for c in range(2):
                            rows_c = slice(64 * c, 64 * c + 64)
                            src = bank[rows_c, :].rearrange("p (a b) -> p a b", a=2)[:, :, c * RV:(c + 1) * RV]
                            ins = dve.tensor_tensor(state[rows_c, 2 * i:2 * i + 2], state[rows_c, 2 * i:2 * i + 2],
                                                    src, ALU.add)
                        ins.then_inc(step_sem(), 1)
                        dve.wait_ge(step_sem(), next_step(g))
                        dve.sem_inc(free, 1)
                    dve.tensor_tensor(state[:], state[:],
                                      const[:, C_SD:C_SD + 4].unsqueeze(2).to_broadcast([P, 4, RV]),
                                      ALU.mult).then_inc(dve_made, 1)
                elif kind == "GA":
                    dve.wait_ge(act_made, act_count(g, stage, "sig"))
                    dve.wait_ge(act_made, act_count(g, ("WA", t, n), "m"))
                    m = qk_m[:, t, n * CW:(n + 1) * CW]
                    dve.tensor_tensor(m, m, qa[:, t], ALU.mult).then_inc(dve_made, 1)
                elif kind == "WR":
                    dve.wait_ge(act_made, act_count(g, ("GR", t, n), "sig"))
                    dve.wait_ge(filled, fill_count(g, stage))
                    bank, free = bank_of(stage)
                    dve.tensor_tensor(qa[:, t], bank[:, :], qa[:, t], ALU.mult).then_inc(step_sem(), 1)
                    dve.wait_ge(step_sem(), next_step(g))
                    dve.sem_inc(free, 1)
                    m = qk_m[:, t, n * CW:(n + 1) * CW]
                    dve.wait_ge(dve_made, g * NDVE + DVE_AT[(("GA", t, n), "m")] + 1)
                    dve.tensor_tensor(m, m, qa[:, t], ALU.add).then_inc(dve_made, 1)
                elif kind == "WO":
                    dve.wait_ge(filled, fill_count(g, stage))
                    bank, free = bank_of(stage)
                    hcol = xh[:, t, n * CW:(n + 1) * CW]
                    dve.tensor_tensor(hcol, bank[:, :], hcol, ALU.add).then_inc(step_sem(), 1)
                    dve.wait_ge(step_sem(), next_step(g))
                    dve.sem_inc(free, 1)
                    dve.sem_inc(dve_made, 1)
                elif kind == "norm2":
                    dve.wait_ge(act_made, act_count(g, stage, "rms"))
                    dve.reciprocal(col(RSTD + t), col(RMS + t)).then_inc(step_sem(), 1)
                    dve.wait_ge(step_sem(), next_step(g))
                    dve.sem_inc(dve_made, 1)
                    if t == 0:
                        dve.wait_ge(filled, fill_count(g, ("WR", GT - 1, 1)))
                    dve.scalar_tensor_tensor(out=hn[:, t], in0=xh[:, t], scalar=col(RSTD + t), in1=gain_ffn[:],
                                             op0=ALU.mult, op1=ALU.mult).then_inc(dve_made, 1)
                elif kind == "top":
                    dve.wait_ge(act_made, g * NACT + ACT_AT[(("keys", None, n), "scores")] + 1)
                    dve.sem_inc(passed, 1)
                    sixteen_largest(g, [(scores[:, tt, 2 * n + half], top_v[:, tt, half], top_i[:, tt, half])
                                        for tt in range(GT) for half in range(2)])
                    dve.sem_inc(dve_made, 1)
                elif kind == "pick":
                    for tt in range(GT):
                        ins = dve.tensor_tensor(cands[:, tt, n].rearrange("p (a b) -> p a b", a=TOPK),
                                                top_v[:, tt, 0].unsqueeze(2).to_broadcast([P, TOPK, TOPK]),
                                                top_v[:, tt, 1].unsqueeze(1).to_broadcast([P, TOPK, TOPK]), ALU.add)
                    ins.then_inc(step_sem(), 1)
                    dve.wait_ge(step_sem(), next_step(g))
                    dve.sem_inc(passed, 1)
                    sixteen_largest(g, [(cands[:, tt, n], pick_v[:, tt], pick_i[:, tt]) for tt in range(GT)])
                    dve.tensor_tensor(expg[:], pick_v[:], pick_v[:, :, 0:1].to_broadcast([P, GT, TOPK]),
                                             ALU.subtract).then_inc(step_sem(), 1)
                    dve.wait_ge(step_sem(), next_step(g))
                    dve.sem_inc(dve_made, 1)
                elif kind == "index":
                    both = GT * TOPK
                    slots = slice(n * TOPK, (n + 1) * TOPK)
                    if n < EARLY_HEADS:
                        index, gate = index_next, gate_next
                    else:
                        index, gate = index_cur, gate_cur
                        if n == EARLY_HEADS:
                            m = GATHER[("v", PH + n, TOPK - 1)]
                            dve.wait_ge(used_pe, g * NUSED_PE + USED[m][1])
                            dve.wait_ge(used_dve, g * NUSED_DVE + USED[m][0])
                        else:
                            dve.wait_ge(used_pe, (g + 1) * NUSED_PE)
                    dve.tensor_scalar(part[:, 0], pick_i[:], 4, None, ALU.logical_shift_right)
                    dve.tensor_scalar(part[:, 1], pick_i[:], 15, None, ALU.bitwise_and)
                    dve.tensor_copy(top_if[:, :, :, :].rearrange("p w t j -> p t w j"), top_i[:]).then_inc(step_sem(), 1)
                    dve.wait_ge(step_sem(), next_step(g))
                    hot = probs[:, 0:4].rearrange("p a b -> p (a b)")
                    hot_s = hot.rearrange("p (s j) -> p s j", j=TOPK)
                    hot_wt = hot.rearrange("p (w s j) -> p w s j", w=2 * GT, j=TOPK)
                    dve.tensor_tensor(
                        hot_s, part[:, :, :, :].rearrange("p w t s -> p (w t s)").unsqueeze(2).to_broadcast(
                            [P, 2 * both, TOPK]),
                        const[:, C_IOTA:C_IOTA + 16].unsqueeze(1).to_broadcast([P, 2 * both, TOPK]), ALU.is_equal).then_inc(step_sem(), 1)
                    dve.wait_ge(step_sem(), next_step(g))
                    dve.tensor_tensor(
                        hot_wt, hot_wt, top_if[:, :, :, :].rearrange("p w t j -> p (w t) j").unsqueeze(2).to_broadcast(
                            [P, 2 * GT, TOPK, TOPK]), ALU.mult).then_inc(step_sem(), 1)
                    dve.wait_ge(step_sem(), next_step(g))
                    dve.tensor_reduce(sel[:, :, :, :].rearrange("p w t s -> p (w t s)"), hot_s, AX.X, ALU.add).then_inc(step_sem(), 1)
                    dve.wait_ge(step_sem(), next_step(g))
                    dve.scalar_tensor_tensor(out=index[:, :, slots], in0=sel[:, 0], scalar=float(NKEY), in1=sel[:, 1],
                                             op0=ALU.mult, op1=ALU.add)
                    dve.wait_ge(act_made, act_count(g, ("pick", None, n), "exp"))
                    dve.tensor_reduce(col(GSUM, GT), expg[:], AX.X, ALU.add).then_inc(step_sem(), 1)
                    dve.wait_ge(step_sem(), next_step(g))
                    dve.reciprocal(col(GINV, GT), col(GSUM, GT)).then_inc(step_sem(), 1)
                    dve.wait_ge(step_sem(), next_step(g))
                    dve.tensor_tensor(gate[:, :, slots], expg[:],
                                             col(GINV, GT).unsqueeze(2).to_broadcast([P, GT, TOPK]), ALU.mult).then_inc(step_sem(), 1)
                    dve.wait_ge(step_sem(), next_step(g))
                    dve.sem_inc(dve_made, 1)

            def retrieve(g, h, q):
                for k in range(QN * q, QN * q + QN):
                    if h < NH2:
                        n = GATHER[("u", h, k)]
                        t = h // PH
                        dve.wait_ge(row_landed[n % RING], landed_in(g, n))
                        dve.tensor_tensor_reduce(out=rows[:, n % RING], in0=rows[:, n % RING], in1=hn_cur[:, t],
                                                 scale=1.0, scalar=0.0, op0=ALU.mult, op1=ALU.add,
                                                 accum_out=dots[:, h % 2, k:k + 1]).then_inc(used_dve, 1)
                    if not h:
                        continue
                    hp = h - 1
                    t, s0 = hp // PH, (hp % PH) * TOPK
                    if k == 0:
                        dve.wait_ge(gelu_made, g * NH2 + hp + 1)
                        dve.tensor_tensor(coef[:, hp % 2], dots[:, hp % 2],
                                          gate_cur[:, t, s0:s0 + TOPK], ALU.mult).then_inc(coef_made, 1)
                    if on_pe(hp, k):
                        continue
                    n = GATHER[("v", hp, k)]
                    number = DVE_ROWS[t].index((hp, k))
                    dve.wait_ge(row_landed[n % RING], landed_in(g, n))
                    c = coef[:, hp % 2, k:k + 1]
                    if number == 0:
                        dve.wait_ge(coef_made, g * NH2 + hp + 1)
                        ins = dve.tensor_scalar(vacc[:], rows[:, n % RING], c, None, ALU.mult)
                    else:
                        prev = GATHER[("v", *DVE_ROWS[t][number - 1])]
                        dve.wait_ge(used_dve, (g + 1) * NUSED_DVE + USED[prev][0])
                        if DVE_ROWS[t][number - 1][0] != hp:
                            dve.wait_ge(coef_made, g * NH2 + hp + 1)
                        ins = dve.scalar_tensor_tensor(out=vacc[:], in0=rows[:, n % RING], scalar=c, in1=vacc[:],
                                                       op0=ALU.mult, op1=ALU.add)
                    ins.then_inc(used_dve, 1)
                if h and (h - 1) % PH == PH - 1 and q == TOPK // QN - 1:
                    t = (h - 1) // PH
                    base = (g + 1) * NACC + t * PER_TILE
                    dve.wait_ge(used_dve, (g + 1) * NUSED_DVE + USED[GATHER[("v", *DVE_ROWS[t][-1])]][0])
                    pes = USED[GATHER[("v", *PE_ROWS[t][-1])]][1]
                    dve.wait_ge(used_pe, (g + 1) * NUSED_PE + pes)
                    dve.tensor_tensor(vacc[:, 0:CW], vacc[:, 0:CW], vsum[0][:, :], ALU.add).then_inc(acc_made, 1)
                    dve.tensor_tensor(vacc[:, CW:D], vacc[:, CW:D], vsum[1][:, :], ALU.add).then_inc(acc_made, 1)
                    dve.wait_ge(acc_made, base + 2)
                    dve.wait_ge(handed_act, g * GT + GT)
                    dve.tensor_tensor(h_cur[:, t], h_cur[:, t], vacc[:], ALU.add).then_inc(acc_made, 1)
                    dve.wait_ge(fin_rms, g * (2 * GT) + 2 * t + 2)
                    dve.reciprocal(col(FRSTD), col(FRMS)).then_inc(acc_made, 1)
                    dve.wait_ge(acc_made, base + 4)
                    dve.scalar_tensor_tensor(out=h_cur[:, t], in0=h_cur[:, t], scalar=col(FRSTD), in1=gain_fin[:],
                                             op0=ALU.mult, op1=ALU.mult).then_inc(out_made, 1)

            def hand_over(g, t):
                early = slice(0, EARLY_HEADS * TOPK)
                last_dve, last_pe = GATHER[("v", *DVE_ROWS[t][-1])], GATHER[("v", *PE_ROWS[t][-1])]
                if not is_first(g):
                    dve.wait_ge(used_pe, g * NUSED_PE + USED[last_pe][1])
                if not is_first(g):
                    dve.wait_ge(used_dve, g * NUSED_DVE + USED[last_dve][0])
                dve.wait_ge(dve_made, g * NDVE + DVE_AT[(("index", None, EARLY_HEADS - 1), "index")] + 1)
                dve.tensor_copy(index_cur[:, t, early], index_next[:, t])
                dve.tensor_copy(gate_cur[:, t, early], gate_next[:, t])
                dve.tensor_copy(hn_cur[:, t], hn[:, t]).then_inc(handed_dve, 1)
                dve.wait_ge(handed_dve, g * GT + t + 1)

            dve.sem_inc(used_dve, NUSED_DVE)
            dve.sem_inc(acc_made, NACC)
            dve.wait_ge(consts_landed, 16)
            dve.wait_ge(gains_landed, 16)
            dve.wait_ge(set_up, 4)
            start_steps(0)
            for stage in EARLY:
                front(0, stage)
            hand_over(0, 0)
            for stage in HEAD_1:
                front(0, stage)
            per_group[0] = steps[0]
            with dve.Fori(0, GROUPS - 1) as r:
                start_steps(1)
                for n, (h, q) in enumerate(EIGHTHS):
                    if n == HAND_0:
                        hand_over(r + 1, 0)
                    retrieve(r, h, q)
                    if n == HAND_1:
                        hand_over(r, 1)
                    for stage in LATE_SHARE.get(n, ()):
                        front(r, stage)
                    if n == LATE_TO - 1:
                        end_late()
                        start_steps(0)
                    for stage in EARLY_SHARE.get(n, ()):
                        front(r + 1, stage)
                assert steps[0] == per_group[0]
            start_steps(1)
            for n, (h, q) in enumerate(EIGHTHS):
                retrieve(GROUPS - 1, h, q)
                if n == HAND_1:
                    hand_over(GROUPS - 1, 1)
                for stage in LATE_SHARE.get(n, ()):
                    front(GROUPS - 1, stage)


_INS = ["x", "norm_mix", "w_in", "att_sinks", "w_att_branch", "w_ret_branch", "w_out", "norm_ffn", "peer_w_query",
        "peer_sub_keys_1", "peer_sub_keys_2", "peer_u", "peer_v", "norm_final"]


def kernel(**inputs):
    import numpy as _np
    import concourse.bacc as _bacc
    from concourse import mybir as _mybir
    from concourse.bass_utils import run_bass_kernel_spmd as _run

    nc = _bacc.Bacc("TRN2", target_bir_lowering=False, num_devices=1)
    arrays, aps = {}, {}
    for name in _INS:
        a = _np.ascontiguousarray(inputs[name])
        if a.ndim == 3:
            a = a[0]
        arrays[f"in_{name}"] = a
        aps[name] = nc.dram_tensor(f"in_{name}", a.shape, _mybir.dt.from_np(a.dtype), kind="ExternalInput").ap()
    const_table, rot_table, mask_table = shape_constants()
    for name, a in (("const_table", const_table), ("rot_table", rot_table), ("mask_table", mask_table)):
        arrays[f"in_{name}"] = a
        aps[name] = nc.dram_tensor(f"in_{name}", a.shape, _mybir.dt.from_np(a.dtype), kind="ExternalInput").ap()
    out = nc.dram_tensor("out_0", (SEQ, D), _mybir.dt.float32, kind="ExternalOutput").ap()
    build_block(nc, *[aps[n] for n in _INS], aps["const_table"], aps["rot_table"], aps["mask_table"], out)
    r = _run(nc, [arrays], core_ids=[0])
    return r.results[0]["out_0"].reshape(1, SEQ, D)
```
